# Optimizing a Trainium2 kernel written in Bass

```python
import math
import jax, jax.numpy as jnp
from jax import lax
import numpy as np

D_MODEL = 1024
BATCH = 1
SEQ = 1024
DEPTH = 2
DEC_BATCH = 8
DEC_SEQ = 8
PAST_LEN = 2048
PAGE_SIZE = 128

F32 = jnp.float32
N_EVEN = (DEPTH + 1) // 2
N_ODD = DEPTH // 2
GLA_HEADS = 4
GLA_DK = 64
GLA_DV = 128
GLA_GATE_RANK = 16
GLA_TAU = 16.0
GLA_CHUNK = 16
DSA_HEADS = 8
DSA_KV_HEADS = 2
DSA_GROUP = DSA_HEADS // DSA_KV_HEADS
HEAD_DIM = 64
IDX_HEADS = 8
IDX_DIM = 64
DSA_TOPK = 256
DSA_QBLOCK = 128
SWA_HEADS = 16
SWA_KV_HEADS = 4
SWA_GROUP = SWA_HEADS // SWA_KV_HEADS
WINDOW = 128
ROPE_THETA = 150000.0
D_FF = -(-8 * D_MODEL // (3 * 256)) * 256
ALPHA = (2.0 * DEPTH) ** 0.25
BETA = (8.0 * DEPTH) ** -0.25
LN_EPS = 1e-5
RMS_EPS = 1e-6

EVEN_COLS = (GLA_HEADS * GLA_DK, GLA_HEADS * GLA_DK, GLA_HEADS * GLA_DV, GLA_HEADS * GLA_DV, GLA_GATE_RANK,
             DSA_HEADS * HEAD_DIM, DSA_KV_HEADS * HEAD_DIM, DSA_KV_HEADS * HEAD_DIM,
             IDX_HEADS * IDX_DIM, IDX_DIM, IDX_HEADS)
EVEN_MIX = GLA_HEADS * GLA_DV + DSA_HEADS * HEAD_DIM
ODD_COLS = (SWA_HEADS * HEAD_DIM, SWA_KV_HEADS * HEAD_DIM, SWA_KV_HEADS * HEAD_DIM)
ODD_MIX = SWA_HEADS * HEAD_DIM

kernel_name = "hybrid_gla_dsa_swa_deepnorm_step"

def split_cols(h, sizes):
    return jnp.split(h, np.cumsum(sizes)[:-1].tolist(), axis=-1)

def layer_norm(x, g, b):
    xf = x.astype(F32)
    mu = xf.mean(-1, keepdims=True)
    var = jnp.square(xf - mu).mean(-1, keepdims=True)
    return ((xf - mu) * lax.rsqrt(var + LN_EPS) * g + b).astype(x.dtype)

def swiglu(x, w_gu, w_down):
    gate, up = jnp.split(x @ w_gu, 2, axis=-1)
    return (jax.nn.silu(gate) * up) @ w_down

def rope(x, pos):
    half = HEAD_DIM // 2
    inv = ROPE_THETA ** (-jnp.arange(half, dtype=F32) / half)
    ang = pos.astype(F32)[:, None] * inv[None, :]
    cos = jnp.cos(ang)[None, :, None, :]
    sin = jnp.sin(ang)[None, :, None, :]
    x1 = x[..., :half].astype(F32)
    x2 = x[..., half:].astype(F32)
    return jnp.concatenate([x1 * cos - x2 * sin, x2 * cos + x1 * sin], axis=-1).astype(x.dtype)

def gla_chunked(q, k, v, glog, s0):
    B, L, H, DK = q.shape
    DV = v.shape[-1]
    C = math.gcd(L, GLA_CHUNK)
    n = L // C
    q, k, v, glog = [t.reshape(B, n, C, H, t.shape[-1]) for t in (q, k, v, glog)]
    b = jnp.cumsum(glog.astype(F32), axis=2)
    causal = jnp.tril(jnp.ones((C, C), bool))[None, None, :, :, None, None]
    diff = b[:, :, :, None] - b[:, :, None, :]
    decay = jnp.exp(jnp.where(causal, diff, -jnp.inf))
    a = jnp.einsum('bnthd,bnshd,bntshd->bnhts', q, k, decay)
    o_intra = jnp.einsum('bnhts,bnshv->bnthv', a, v)
    q_in = q * jnp.exp(b)
    b_last = b[:, :, -1]
    k_in = k * jnp.exp(b_last[:, :, None] - b)
    kv = jnp.einsum('bnshd,bnshv->bnhdv', k_in, v)

    def step(S, inp):
        qi, dec, kvi = inp
        o = jnp.einsum('bthd,bhdv->bthv', qi, S)
        S = jnp.exp(dec)[..., None] * S + kvi
        return S, o

    S, o_inter = lax.scan(step, s0.astype(F32),
                          (jnp.moveaxis(q_in, 1, 0), jnp.moveaxis(b_last, 1, 0), jnp.moveaxis(kv, 1, 0)))
    o = o_intra + jnp.moveaxis(o_inter, 0, 1)
    return o.reshape(B, L, H, DV), S

def gla_out(o, r, norm_g):
    B, L = o.shape[:2]
    of = o.astype(F32)
    of = of * lax.rsqrt(jnp.mean(of * of, -1, keepdims=True) + RMS_EPS) * norm_g
    return (of.reshape(B, L, -1) * jax.nn.silu(r.astype(F32))).astype(r.dtype)

def indexer_scores(iq, iw, ik):
    dots = jax.nn.relu(jnp.einsum('bqhd,bsd->bqhs', iq, ik).astype(F32))
    return jnp.einsum('bqhs,bqh->bqs', dots, iw.astype(F32))

def dsa_attend(q, k_sel, v_sel, valid):
    B, Q = q.shape[:2]
    qg = q.reshape(B, Q, DSA_KV_HEADS, DSA_GROUP, HEAD_DIM)
    s = jnp.einsum('bqkgd,bqnkd->bqkgn', qg, k_sel).astype(F32) * HEAD_DIM ** -0.5
    s = jnp.where(valid[:, :, None, None, :], s, -jnp.inf)
    p = jax.nn.softmax(s, axis=-1)
    o = jnp.einsum('bqkgn,bqnkd->bqkgd', p.astype(v_sel.dtype), v_sel)
    return o.reshape(B, Q, DSA_HEADS * HEAD_DIM)

def dsa_prompt(q, k, v, iq, ik, iw):
    B, L = q.shape[:2]
    kk = min(DSA_TOPK, L // 4)
    nb = L // DSA_QBLOCK
    blk = lambda t: jnp.moveaxis(t.reshape(B, nb, DSA_QBLOCK, *t.shape[2:]), 1, 0)
    key_pos = jnp.arange(L)

    def one_block(args):
        i, qb, iqb, iwb = args
        t = i * DSA_QBLOCK + jnp.arange(DSA_QBLOCK)
        sc = indexer_scores(iqb, iwb, ik)
        sc = jnp.where((key_pos[None, :] <= t[:, None])[None], sc, -jnp.inf)
        _, idx = lax.top_k(sc, kk)
        ks = jax.vmap(lambda a, j: a[j])(k, idx)
        vs = jax.vmap(lambda a, j: a[j])(v, idx)
        return dsa_attend(qb, ks, vs, idx <= t[None, :, None])

    o = lax.map(one_block, (jnp.arange(nb), blk(q), blk(iq), blk(iw)))
    return jnp.moveaxis(o, 0, 1).reshape(B, L, -1)

def dsa_sample(layer, q, k_new, v_new, iq, ik_new, iw, cache_k, cache_v, cache_idx, page_table):
    Bd, Q = q.shape[:2]
    L = PAST_LEN + Q
    kk = min(DSA_TOPK, L // 4)
    ik_past = cache_idx[layer, page_table].reshape(Bd, PAST_LEN, IDX_DIM)
    ik_all = jnp.concatenate([ik_past, ik_new], axis=1)
    t = PAST_LEN + jnp.arange(Q)
    sc = indexer_scores(iq, iw, ik_all)
    sc = jnp.where((jnp.arange(L)[None, :] <= t[:, None])[None], sc, -jnp.inf)
    _, idx = lax.top_k(sc, kk)
    bidx = jnp.arange(Bd)[:, None, None]
    in_past = (idx < PAST_LEN)[..., None, None]
    ip = jnp.minimum(idx, PAST_LEN - 1)
    phys = page_table[bidx, ip // PAGE_SIZE]
    off = ip % PAGE_SIZE
    inew = jnp.clip(idx - PAST_LEN, 0, Q - 1)
    ks = jnp.where(in_past, cache_k[layer, phys, off], k_new[bidx, inew])
    vs = jnp.where(in_past, cache_v[layer, phys, off], v_new[bidx, inew])
    return dsa_attend(q, ks, vs, idx <= t[None, :, None])

def even_project(x, w_in, gate_w2, gate_b):
    B, L, _ = x.shape
    gq, gk, gv, gr, gg, dq, dk, dv, iq, ik, iw = split_cols(x @ w_in, EVEN_COLS)
    glog = jax.nn.log_sigmoid((gg @ gate_w2 + gate_b).astype(F32)) / GLA_TAU
    gla = (gq.reshape(B, L, GLA_HEADS, GLA_DK) * GLA_DK ** -0.5,
           gk.reshape(B, L, GLA_HEADS, GLA_DK),
           gv.reshape(B, L, GLA_HEADS, GLA_DV),
           gr,
           glog.reshape(B, L, GLA_HEADS, GLA_DK))
    dsa = (dq.reshape(B, L, DSA_HEADS, HEAD_DIM),
           dk.reshape(B, L, DSA_KV_HEADS, HEAD_DIM),
           dv.reshape(B, L, DSA_KV_HEADS, HEAD_DIM),
           iq.reshape(B, L, IDX_HEADS, IDX_DIM),
           ik,
           iw * (IDX_HEADS ** -0.5 * IDX_DIM ** -0.5))
    return gla, dsa

def even_prompt(x, w_in, gate_w2, gate_b, norm_g, w_out):
    (gq, gk, gv, gr, glog), (dq, dk, dv, iq, ik, iw) = even_project(x, w_in, gate_w2, gate_b)
    s0 = jnp.zeros((x.shape[0], GLA_HEADS, GLA_DK, GLA_DV), F32)
    o_gla, S = gla_chunked(gq, gk, gv, glog, s0)
    y_gla = gla_out(o_gla, gr, norm_g)
    y_dsa = dsa_prompt(dq, dk, dv, iq, ik, iw)
    out = jnp.concatenate([y_gla, y_dsa.astype(y_gla.dtype)], axis=-1) @ w_out
    return out, (dk, dv, ik, S)

def even_sample(layer, x, cache_k, cache_v, cache_idx, state_gla, page_table, w_in, gate_w2, gate_b, norm_g, w_out):
    (gq, gk, gv, gr, glog), (dq, dk, dv, iq, ik, iw) = even_project(x, w_in, gate_w2, gate_b)
    o_gla, S = gla_chunked(gq, gk, gv, glog, state_gla[layer])
    y_gla = gla_out(o_gla, gr, norm_g)
    y_dsa = dsa_sample(layer, dq, dk, dv, iq, ik, iw, cache_k, cache_v, cache_idx, page_table)
    out = jnp.concatenate([y_gla, y_dsa.astype(y_gla.dtype)], axis=-1) @ w_out
    return out, (dk, dv, ik, S)

def sink_attend(q, k, v, mask, sinks):
    s = jnp.einsum('bnqkgd,bnckd->bnkgqc', q, k).astype(F32) * HEAD_DIM ** -0.5
    s = jnp.where(mask[None, :, None, None], s, -jnp.inf)
    sink = sinks.astype(F32).reshape(1, 1, SWA_KV_HEADS, SWA_GROUP, 1, 1)
    m = jnp.maximum(s.max(-1, keepdims=True), sink)
    p = jnp.exp(s - m)
    p = p / (p.sum(-1, keepdims=True) + jnp.exp(sink - m))
    return jnp.einsum('bnkgqc,bnckd->bnqkgd', p.astype(v.dtype), v)

def swa_qkv(x, w_in, pos):
    B, L, _ = x.shape
    qh, kh, vh = split_cols(x @ w_in, ODD_COLS)
    q = rope(qh.reshape(B, L, SWA_HEADS, HEAD_DIM), pos)
    k = rope(kh.reshape(B, L, SWA_KV_HEADS, HEAD_DIM), pos)
    v = vh.reshape(B, L, SWA_KV_HEADS, HEAD_DIM)
    return q, k, v

def odd_prompt(x, w_in, sinks, w_out):
    B, L, _ = x.shape
    q, k, v = swa_qkv(x, w_in, jnp.arange(L))
    nb = L // WINDOW
    qb = q.reshape(B, nb, WINDOW, SWA_KV_HEADS, SWA_GROUP, HEAD_DIM)
    kb = k.reshape(B, nb, WINDOW, SWA_KV_HEADS, HEAD_DIM)
    vb = v.reshape(B, nb, WINDOW, SWA_KV_HEADS, HEAD_DIM)
    band = lambda t: jnp.concatenate([jnp.concatenate([jnp.zeros_like(t[:, :1]), t[:, :-1]], axis=1), t], axis=2)
    a = jnp.arange(WINDOW)[None, :, None]
    c = jnp.arange(2 * WINDOW)[None, None, :]
    blk = jnp.arange(nb)[:, None, None]
    mask = (c > a) & (c <= a + WINDOW) & ((blk > 0) | (c >= WINDOW))
    o = sink_attend(qb, band(kb), band(vb), mask, sinks).reshape(B, L, ODD_MIX)
    return o @ w_out, (k[:, -WINDOW:], v[:, -WINDOW:])

def odd_sample(x, buf_k, buf_v, w_in, sinks, w_out):
    Bd, Q, _ = x.shape
    pos = PAST_LEN + jnp.arange(Q)
    q, k, v = swa_qkv(x, w_in, pos)
    kc = jnp.concatenate([buf_k, k], axis=1)
    vc = jnp.concatenate([buf_v, v], axis=1)
    kpos = PAST_LEN - WINDOW + jnp.arange(WINDOW + Q)
    d = pos[:, None] - kpos[None, :]
    mask = ((d >= 0) & (d < WINDOW))[None]
    o = sink_attend(q.reshape(Bd, 1, Q, SWA_KV_HEADS, SWA_GROUP, HEAD_DIM), kc[:, None], vc[:, None], mask, sinks)
    return o.reshape(Bd, Q, ODD_MIX) @ w_out, (kc[:, -WINDOW:], vc[:, -WINDOW:])

def trunk(x, even_fn, odd_fn, ffn_w_gu, ffn_w_down, ln_g, ln_b):
    even_states, odd_states = [], []
    for l in range(DEPTH):
        if l % 2 == 0:
            mix, st = even_fn(l // 2, x)
            even_states.append(st)
        else:
            mix, st = odd_fn(l // 2, x)
            odd_states.append(st)
        h = layer_norm(ALPHA * x + mix, ln_g[l, 0], ln_b[l, 0])
        x = layer_norm(ALPHA * h + swiglu(h, ffn_w_gu[l], ffn_w_down[l]), ln_g[l, 1], ln_b[l, 1])
    ev = [jnp.stack(z) for z in zip(*even_states)]
    od = [jnp.stack(z) for z in zip(*odd_states)]
    return x, ev, od

def setup_inputs(seed: int = 0) -> dict:
    key = jax.random.key(seed)
    ks = iter(jax.random.split(key, 32))
    nrm = lambda shape, scale: jax.random.normal(next(ks), shape, F32) * scale
    n_pages = PAST_LEN // PAGE_SIZE
    n_used = DEC_BATCH * n_pages
    n_pool = n_used + (n_used + 3) // 4
    perm = jax.random.permutation(next(ks), n_pool)
    page_table = perm[:n_used].reshape(DEC_BATCH, n_pages).astype(jnp.int32)
    return {
        "x_prompt": nrm((BATCH, SEQ, D_MODEL), 1.0),
        "x_sample": nrm((DEC_BATCH, DEC_SEQ, D_MODEL), 1.0),
        "cache_k": nrm((N_EVEN, n_pool, PAGE_SIZE, DSA_KV_HEADS, HEAD_DIM), 1.0),
        "cache_v": nrm((N_EVEN, n_pool, PAGE_SIZE, DSA_KV_HEADS, HEAD_DIM), 1.0),
        "cache_idx": nrm((N_EVEN, n_pool, PAGE_SIZE, IDX_DIM), 1.0),
        "state_gla": nrm((N_EVEN, DEC_BATCH, GLA_HEADS, GLA_DK, GLA_DV), 1.0),
        "state_swa_k": nrm((N_ODD, DEC_BATCH, WINDOW, SWA_KV_HEADS, HEAD_DIM), 1.0),
        "state_swa_v": nrm((N_ODD, DEC_BATCH, WINDOW, SWA_KV_HEADS, HEAD_DIM), 1.0),
        "page_table": page_table,
        "w_in_even": nrm((N_EVEN, D_MODEL, sum(EVEN_COLS)), D_MODEL ** -0.5),
        "gla_gate_w2": nrm((N_EVEN, GLA_GATE_RANK, GLA_HEADS * GLA_DK), GLA_GATE_RANK ** -0.5),
        "gla_gate_b": nrm((N_EVEN, GLA_HEADS * GLA_DK), 0.1),
        "gla_norm_g": 1.0 + nrm((N_EVEN, GLA_DV), 0.02),
        "w_out_even": nrm((N_EVEN, EVEN_MIX, D_MODEL), EVEN_MIX ** -0.5 * BETA),
        "w_in_odd": nrm((N_ODD, D_MODEL, sum(ODD_COLS)), D_MODEL ** -0.5),
        "swa_sinks": nrm((N_ODD, SWA_HEADS), 1.0),
        "w_out_odd": nrm((N_ODD, ODD_MIX, D_MODEL), ODD_MIX ** -0.5 * BETA),
        "ffn_w_gu": nrm((DEPTH, D_MODEL, 2 * D_FF), D_MODEL ** -0.5),
        "ffn_w_down": nrm((DEPTH, D_FF, D_MODEL), D_FF ** -0.5 * BETA),
        "ln_g": 1.0 + nrm((DEPTH, 2, D_MODEL), 0.02),
        "ln_b": nrm((DEPTH, 2, D_MODEL), 0.02),
    }

def reference(x_prompt, x_sample, cache_k, cache_v, cache_idx, state_gla, state_swa_k, state_swa_v, page_table,
              w_in_even, gla_gate_w2, gla_gate_b, gla_norm_g, w_out_even, w_in_odd, swa_sinks, w_out_odd,
              ffn_w_gu, ffn_w_down, ln_g, ln_b):
    even_p = lambda i, h: even_prompt(h, w_in_even[i], gla_gate_w2[i], gla_gate_b[i], gla_norm_g[i], w_out_even[i])
    odd_p = lambda i, h: odd_prompt(h, w_in_odd[i], swa_sinks[i], w_out_odd[i])
    even_s = lambda i, h: even_sample(i, h, cache_k, cache_v, cache_idx, state_gla, page_table, w_in_even[i],
                                      gla_gate_w2[i], gla_gate_b[i], gla_norm_g[i], w_out_even[i])
    odd_s = lambda i, h: odd_sample(h, state_swa_k[i], state_swa_v[i], w_in_odd[i], swa_sinks[i], w_out_odd[i])

    y_prompt, (k_p, v_p, idx_p, gla_p), (swk_p, swv_p) = trunk(x_prompt, even_p, odd_p, ffn_w_gu, ffn_w_down, ln_g, ln_b)
    y_sample, (k_s, v_s, idx_s, gla_s), (swk_s, swv_s) = trunk(x_sample, even_s, odd_s, ffn_w_gu, ffn_w_down, ln_g, ln_b)
    return (y_prompt, y_sample, k_p, v_p, idx_p, gla_p, swk_p, swv_p, k_s, v_s, idx_s, gla_s, swk_s, swv_s)


_drawn_inputs = setup_inputs


def setup_inputs(seed=0):
    import zlib

    import numpy as np

    out = dict(_drawn_inputs(seed))
    spreads = {}
    factors = {'gla_norm_g': 31.054,
     'swa_sinks': 8.0,
     'cache_k': 4.07,
     'cache_v': 3.288,
     'cache_idx': 3.466}
    for name, (base, spread) in spreads.items():
        noise = np.random.default_rng([zlib.crc32(name.encode()), seed]).standard_normal(out[name].shape)
        drawn = base * np.exp(spread * noise) if base else spread * noise
        out[name] = __import__('jax').numpy.asarray(drawn.astype(out[name].dtype))
    for name, factor in factors.items():
        out[name] = (out[name] * factor).astype(out[name].dtype)
    return out
```

```python
from contextlib import ExitStack
import math

import concourse.bass as bass
from concourse import mybir

ALU = mybir.AluOpType
ACT = mybir.ActivationFunctionType
AX_X = mybir.AxisListType.X
F32 = mybir.dt.float32
BF16 = mybir.dt.bfloat16
I32 = mybir.dt.int32
U8 = mybir.dt.uint8

P = 128
D = 1024
KD = D // P
SEQ, DEC_BATCH, DEC_SEQ = 1024, 8, 8
NS = DEC_BATCH * DEC_SEQ
NT = SEQ // P
NTOK = SEQ + NS
TILES = NT + 1
ALPHA = 4.0 ** 0.25
LN_EPS, RMS_EPS = 1e-5, 1e-6
GLA_H, DK, DV, TAU = 4, 64, 128, 16.0
HD = 64
W_GQ, W_GK, W_GV, W_GR, W_GG, W_DQ, W_DK, W_DV, W_IQ, W_IK, W_IW, W_END = (
    0, 256, 512, 1024, 1536, 1552, 2064, 2192, 2320, 2832, 2896, 2904)
C_GQ, C_GK, C_GV, C_GR, C_DQ, C_IQ, C_GG, C_DK, C_DV, C_IK, C_IW, C_END = (
    0, 256, 512, 1024, 1536, 2048, 2560, 2576, 2704, 2832, 2960, 2968)
D_FF = 2816
KF = D_FF // P

def rows(i):
    return P if i < NT else NS

def bcast_rows(ap1d, n, parts=P):
    return bass.AP(ap1d.tensor, ap1d.offset, [[0, parts], [1, n]])

def by_group(start):
    return [((g * 2 + kv) * HD, start + (kv * 4 + g) * HD, HD) for g in range(4) for kv in range(2)]

EVEN_CHUNKS = [[(0, W_GQ, 512)], [(0, W_GV, 512)], [(0, W_GR, 512)], by_group(W_DQ), [(0, W_IQ, 512)],
               [(0, W_GG, 16), (C_DK - C_GG, W_DK, 256), (C_IK - C_GG, W_IK, 64), (C_IK + 64 - C_GG, W_IK, 72)]]
ODD_CHUNKS = [by_group(0), by_group(512), [(0, 1024, 512)]]

def in_projection(nc, st, x_tile, w, chunks, XT, dest, stores, tag, load_x):
    SLOTS = 2
    NCH = len(chunks)
    ncols = 512 * (NCH - 1) + max(a + n for a, _, n in chunks[-1])
    landed = [16 * sum(len(chunks[d]) for d in range(c % SLOTS, c + 1, SLOTS)) for c in range(NCH)]
    w_v = w.rearrange("(k p) n -> p k n", p=P)
    with ExitStack() as ctx:
        sb = lambda n, s, d=F32: ctx.enter_context(nc.sbuf_tensor(f"{tag}_{n}", s, d))
        sem = lambda n: st.sem(f"{tag}_{n}")
        wbuf = sb("w", [P, SLOTS, KD, 512])
        ps = ctx.enter_context(nc.psum_tensor(f"{tag}_ps", [P, 8, 512], F32))
        w_in = [sem(f"w_in{k}") for k in range(SLOTS)]
        mm_done, act_evac, dve_evac = sem("mm_done"), sem("act_evac"), sem("dve_evac")
        stored = sem("stored")
        if load_x:
            xbuf = sb("x", [P, 2, D])
            x_in = [sem(f"x_in{k}") for k in range(2)]
            t_done, t_evac = sem("t_done"), sem("t_evac")

        with nc.Block() as block:
            @block.sync
            def _(sp):
                def load_w(c):
                    if c >= SLOTS:
                        sp.wait_ge(mm_done, (c - SLOTS + 1) * TILES)
                    for a, b, n in chunks[c]:
                        sp.dma_start(wbuf[:, c % SLOTS, :, a:a + n], w_v[:, :, b:b + n]).then_inc(w_in[c % SLOTS], 16)
                if load_x:
                    for i in range(TILES):
                        if i >= 2:
                            sp.wait_ge(t_done, 2 * (i - 1))
                        sp.dma_start(xbuf[0:rows(i), i % 2, :], x_tile(i)).then_inc(x_in[i % 2], 16)
                        if i == 0:
                            load_w(0)
                    load_w(1)
                else:
                    load_w(0)
                    load_w(1)
                for c in range(SLOTS, NCH):
                    load_w(c)

            @block.tensor
            def _(pe):
                if load_x:
                    for i in range(TILES):
                        r = rows(i)
                        pe.wait_ge(x_in[i % 2], 16 * (i // 2 + 1))
                        for h in range(2):
                            j = 2 * i + h
                            if j >= 8:
                                pe.wait_ge(t_evac, j - 7)
                            for k in range(4):
                                kk = 4 * h + k
                                last = nc.tensor.transpose(ps[:, j % 8, k * P:k * P + r],
                                                           xbuf[0:r, i % 2, kk * P:(kk + 1) * P], st.ident[0:r, 0:r])
                            last.then_inc(t_done, 1)
                    pe.wait_ge(t_evac, 2 * TILES)
                for c in range(NCH):
                    n = min(512, ncols - 512 * c)
                    pe.wait_ge(w_in[c % SLOTS], landed[c])
                    for i in range(TILES):
                        s, r = c * TILES + i, rows(i)
                        if s >= 8:
                            pe.wait_ge(act_evac if s % 2 == 0 else dve_evac, (s - 8) // 2 + 1)
                        for k in range(KD):
                            last = nc.tensor.matmul(ps[0:r, s % 8, 0:n], XT[:, k, i * P:i * P + r],
                                                    wbuf[:, c % SLOTS, k, 0:n], start=(k == 0), stop=(k == KD - 1))
                        last.then_inc(mm_done, 1)

            def copy_out(eng, op, parity, done):
                for c in range(NCH):
                    n = min(512, ncols - 512 * c)
                    for i in range(TILES):
                        s, r = c * TILES + i, rows(i)
                        if s % 2 == parity:
                            eng.wait_ge(mm_done, s + 1)
                            op(dest(i)[0:r, 512 * c:512 * c + n], ps[0:r, s % 8, 0:n]).then_inc(done, 1)

            @block.scalar
            def _(act):
                if load_x:
                    for i in range(TILES):
                        for h in range(2):
                            j = 2 * i + h
                            act.wait_ge(t_done, j + 1)
                            nc.scalar.copy(XT[:, 4 * h:4 * h + 4, i * P:i * P + rows(i)],
                                           ps[:, j % 8, :].rearrange("p (k t) -> p k t", k=4)[:, :, 0:rows(i)]).then_inc(t_evac, 1)
                copy_out(act, nc.scalar.copy, 0, act_evac)

            @block.vector
            def _(dve):
                copy_out(dve, nc.vector.tensor_copy, 1, dve_evac)

            @block.gpsimd
            def _(pool):
                total = NCH * TILES
                pool.wait_ge(act_evac, (total + 1) // 2)
                pool.wait_ge(dve_evac, total // 2)
                n = 0
                for out_ap, src in stores:
                    pool.dma_start(out_ap, src).then_inc(stored, 16)
                    n += 1
                if n:
                    pool.wait_ge(stored, 16 * n)



def chained(eng, sem):
    count = [0]

    def link(ins):
        count[0] += 1
        ins.then_inc(sem, 1)
        eng.wait_ge(sem, count[0])
    return link


def gla(nc, st, A, C, O, H, Hs):
    NL = 8
    with ExitStack() as ctx:
        sb = lambda n, s, d=F32: ctx.enter_context(nc.sbuf_tensor(f"gla_{n}", s, d))
        sem = lambda n: st.sem(f"gla_{n}")
        w2, gb, ng = sb("w2", [16, 256]), sb("gb", [P, 2]), sb("ng", [P, DV])
        lev_f, lev = sb("levf", [P, NL, P]), sb("lev", [P, NL, P], U8)
        reset, bsel = sb("reset", [P, 192]), sb("bsel", [NS, 8])
        S = sb("S", [P, 2, DV])
        SS = sb("SS", [P, DEC_BATCH, 2, DV])
        qT, kT = sb("qT", [P, 2, P]), sb("kT", [P, 2, P])
        ggT = sb("ggT", [16, P])
        z, az, cs = sb("z", [P, 2, P]), sb("az", [P, 2, P]), sb("cs", [P, 2, P])
        E = sb("E", [P, NL + 1, 2, P])
        QM = sb("QM", [P, NL, 2, P])
        dec = sb("dec", [P, 2, 8])
        A_sb = sb("A", [P, 2, 2, P])
        qin, kin, kinT = sb("qin", [P, 2, P]), sb("kin", [P, 2, P]), sb("kinT", [P, 2, P])
        oT = sb("oT", [P, 2, 2, NS])
        ssq, rs = sb("ssq", [P, 4]), sb("rs", [P, 4])
        junk, er = sb("junk", [P, DV]), sb("er", [P, 512])
        ps = ctx.enter_context(nc.psum_tensor("gla_ps", [P, 8, 512], F32))
        tr, zp, misc = ps[:, 0, :], ps[:, 1, :], ps[:, 2, :]
        o_ps = [ps[:, 7, :], ps[:, 1, :]]
        ot_ps = [ps[:, 0, :], ps[:, 2, :]]

        def o_of(h, r):
            return o_ps[h % 2][0:r, (h // 2) * DV:(h // 2 + 1) * DV]

        cin, cst = sem("const_in"), sem("const_ready")
        t_done, t_act, g_dve = sem("qk_transposed"), sem("qk_copied"), sem("gg_copied")
        z_biased = sem("z_biased")
        z_done, az_done, ln_done = sem("z_done"), sem("az_done"), sem("ln_done")
        d_done, e_done, qk_done = sem("diff_done"), sem("exp_done"), sem("scaled_done")
        lev_done, lev_used = sem("level_done"), sem("level_used")
        kt_done, kt_act = sem("kin_transposed"), sem("kin_copied")
        o_done, ot_done, ot_act = sem("o_done"), sem("oT_done"), sem("oT_copied")
        kv_done, kv_used = sem("kv_done"), sem("kv_used")
        sq_done, ms_done, rs_done, er_done, y_done = (sem("sq_done"), sem("ms_done"), sem("rs_done"),
                                                      sem("silu_exp_done"), sem("y_done"))
        dch, ach, pch, kb_done = sem("dve_step"), sem("act_step"), sem("pool_step"), sem("kin_masked")
        s_out = sem("state_out")
        kinTb = QM

        def tile_of(i):
            return H[:, i, :] if i < NT else Hs[:, :]

        def lv(i):
            return NL if i < NT else 4

        lev0 = [0]
        for i in range(TILES):
            lev0.append(lev0[-1] + lv(i))
        half = lambda h: slice(64 * (h % 2), 64 * (h % 2) + 64)

        with nc.Block() as block:
            @block.sync
            def _(sp):
                for dst, src in ((w2[:, :], A["gla_gate_w2"][0]),
                                 (ng[:, :], bcast_rows(A["gla_norm_g"], DV)), (lev_f[:, :, :], C["levels"]),
                                 (reset[:, :], C["reset"]), (bsel[:, :], C["batchsel"])):
                    sp.dma_start(dst, src).then_inc(cin, 16)
                sp.dma_start(gb[:, :], A["gla_gate_b"].rearrange("o (c p) -> p (o c)", p=P),
                             allow_slow_non_contiguous=True).then_inc(cin, 16)
                for hf in range(2):
                    sp.dma_start(SS[64 * hf:64 * hf + 64, :, :, :],
                                 A["state_gla"][0].rearrange("b (r f) d v -> f d b r v", f=2)[hf]).then_inc(cin, 16)
                sp.wait_ge(kv_used, NT)
                for hf in range(2):
                    sp.dma_start(O[5][0, 0].rearrange("(r f) d v -> f d r v", f=2)[hf],
                                 S[64 * hf:64 * hf + 64, :, :]).then_inc(s_out, 16)
                sp.wait_ge(kv_used, NT + DEC_BATCH)
                for hf in range(2):
                    sp.dma_start(O[11][0].rearrange("b (r f) d v -> f d b r v", f=2)[hf],
                                 SS[64 * hf:64 * hf + 64, :, :, :]).then_inc(s_out, 16)
                sp.wait_ge(s_out, 64)

            @block.tensor
            def _(pe):
                for i in range(TILES):
                    r, T = rows(i), tile_of(i)
                    if i >= 1:
                        pe.wait_ge(y_done, i)
                        pe.wait_ge(t_act, i)
                        pe.wait_ge(g_dve, i)
                    for p in range(2):
                        nc.tensor.transpose(tr[:, p * P:p * P + r], T[0:r, C_GQ + p * P:C_GQ + (p + 1) * P], st.ident[0:r, 0:r])
                        nc.tensor.transpose(tr[:, (2 + p) * P:(2 + p) * P + r], T[0:r, C_GK + p * P:C_GK + (p + 1) * P], st.ident[0:r, 0:r])
                    nc.tensor.transpose(zp[0:16, 0:r], T[0:r, C_GG:C_GG + 16], st.ident[0:r, 0:r]).then_inc(t_done, 1)
                    pe.wait_ge(g_dve, i + 1)
                    if i == 0:
                        pe.wait_ge(cin, 16 * 8)
                    for p in range(2):
                        last = nc.tensor.matmul(zp[:, P + p * P:P + p * P + r], w2[:, p * P:(p + 1) * P], ggT[:, 0:r],
                                                start=True, stop=True)
                    last.then_inc(z_done, 1)
                    pe.wait_ge(qk_done, i + 1)
                    for p in range(2):
                        last = nc.tensor.transpose(misc[0:r, p * P:(p + 1) * P], kin[:, p, 0:r], st.ident[:, :])
                    last.then_inc(kt_done, 1)
                    for l in range(lv(i)):
                        g = lev0[i] + l
                        if g >= 2:
                            pe.wait_ge(lev_used, g - 1)
                        for h in range(GLA_H):
                            kk = kT[half(h), h // 2, 0:r] if l == 0 else E[half(h), l, h // 2, 0:r]
                            qq = qT[half(h), h // 2, 0:r] if l == 0 else QM[half(h), l, h // 2, 0:r]
                            last = nc.tensor.matmul(ps[0:r, 3 + 2 * (g % 2) + h % 2, (h // 2) * P:(h // 2) * P + r], kk, qq, start=True, stop=True)
                        last.then_inc(lev_done, 1)
                    if i == NT:
                        pe.wait_ge(kt_act, i + 1)
                        for h in range(GLA_H):
                            for b in range(DEC_BATCH):
                                last = nc.tensor.matmul(ot_ps[h % 2][:, (h // 2) * NS + 8 * b:(h // 2) * NS + 8 * b + 8], SS[half(h), b, h // 2, :],
                                                        qin[half(h), h // 2, 8 * b:8 * b + 8], start=True, stop=True)
                        last.then_inc(ot_done, 1)
                        pe.wait_ge(ot_act, 2)
                    pe.wait_ge(lev_used, lev0[i + 1])
                    if 1 <= i < NT:
                        pe.wait_ge(kv_used, i)
                    for h in range(GLA_H):
                        nc.tensor.matmul(o_of(h, r), A_sb[0:r, h % 2, h // 2, 0:r],
                                         T[0:r, C_GV + h * DV:C_GV + (h + 1) * DV], start=True, stop=False)
                        if i < NT:
                            last = nc.tensor.matmul(o_of(h, r), qin[half(h), h // 2, 0:r],
                                                    S[half(h), h // 2, :], start=False, stop=True)
                        else:
                            last = nc.tensor.matmul(o_of(h, r), oT[:, h % 2, h // 2, :], st.ident[:, :],
                                                    start=False, stop=True)
                    last.then_inc(o_done, 1)
                    pe.wait_ge(kt_act, i + 1)
                    if i < NT:
                        for p in range(2):
                            last = nc.tensor.matmul(misc[:, p * 256:(p + 1) * 256], kinT[0:r, p, :],
                                                    T[0:r, C_GV + 256 * p:C_GV + 256 * p + 256], start=True, stop=True)
                        last.then_inc(kv_done, 1)
                        pe.wait_ge(kv_used, i + 1)
                    else:
                        for b in range(DEC_BATCH):
                            pe.wait_ge(kb_done, b + 1)
                            pe.wait_ge(kv_used, NT + b)
                            for p in range(2):
                                last = nc.tensor.matmul(misc[:, p * 256:(p + 1) * 256], kinTb[0:r, b, p, :],
                                                        T[0:r, C_GV + 256 * p:C_GV + 256 * p + 256], start=True, stop=True)
                            last.then_inc(kv_done, 1)

            @block.scalar
            def _(act):
                link = chained(act, ach)
                for i in range(TILES):
                    r, T = rows(i), tile_of(i)
                    act.wait_ge(t_done, i + 1)
                    if i >= 1:
                        act.wait_ge(o_done, i)
                        act.wait_ge(qk_done, i)
                    trv = tr.rearrange("p (a t) -> p a t", a=4)
                    nc.scalar.mul(qT[:, :, 0:r], trv[:, 0:2, 0:r], DK ** -0.5)
                    nc.scalar.copy(kT[:, :, 0:r], trv[:, 2:4, 0:r]).then_inc(t_act, 1)
                    act.wait_ge(z_biased, i + 1)
                    nc.scalar.activation(az[:, :, 0:r], z[:, :, 0:r], ACT.Abs).then_inc(az_done, 1)
                    act.wait_ge(az_done, i + 1)
                    link(nc.scalar.activation(az[:, :, 0:r], az[:, :, 0:r], ACT.Exp, scale=-1.0))
                    nc.scalar.activation(az[:, :, 0:r], az[:, :, 0:r], ACT.Ln, bias=1.0).then_inc(ln_done, 1)
                    act.wait_ge(d_done, i + 1)
                    nc.scalar.activation(dec[:, :, :], dec[:, :, :], ACT.Exp, scale=1 / TAU)
                    if i < NT:
                        nc.scalar.activation(E[:, :, :, :], E[:, :, :, :], ACT.Exp, scale=1 / TAU).then_inc(e_done, 1)
                    else:
                        nc.scalar.activation(E[:, 0:4, :, 0:r], E[:, 0:4, :, 0:r], ACT.Exp, scale=1 / TAU)
                        nc.scalar.activation(E[:, NL, :, 0:r], E[:, NL, :, 0:r], ACT.Exp, scale=1 / TAU).then_inc(e_done, 1)
                    act.wait_ge(kt_done, i + 1)
                    nc.scalar.copy(kinT[0:r, :, :], misc.rearrange("p (a t) -> p a t", a=4)[0:r, 0:2, :]).then_inc(kt_act, 1)
                    nc.scalar.activation(er[0:r, :], T[0:r, C_GR:C_GR + 512], ACT.Exp, scale=-1.0).then_inc(er_done, 1)
                    if i == NT:
                        act.wait_ge(ot_done, 1)
                        for hf in range(2):
                            nc.scalar.copy(oT[:, hf, :, :], ot_ps[hf][:, 0:2 * NS].rearrange("p (h t) -> p h t", h=2)
                                           ).then_inc(ot_act, 1)
                    act.wait_ge(o_done, i + 1)
                    for h in range(GLA_H):
                        ins = nc.scalar.activation(junk[0:r, :], o_of(h, r), ACT.Square,
                                                   accum_out=ssq[0:r, h:h + 1])
                        if h < GLA_H - 1:
                            link(ins)
                        else:
                            ins.then_inc(sq_done, 1)
                    act.wait_ge(ms_done, i + 1)
                    link(nc.scalar.activation(rs[0:r, :], ssq[0:r, :], ACT.Ln))
                    nc.scalar.activation(rs[0:r, :], rs[0:r, :], ACT.Exp, scale=-0.5).then_inc(rs_done, 1)

            @block.gpsimd
            def _(pool):
                link = chained(pool, pch)
                pool.wait_ge(cst, 1)
                for i in range(TILES):
                    r, T = rows(i), tile_of(i)
                    if i == NT:
                        pool.wait_ge(kt_act, i + 1)
                        pool.wait_ge(lev_used, lev0[i + 1])
                        for b in range(DEC_BATCH):
                            nc.gpsimd.tensor_scalar(kinTb[0:r, b, :, :], kinT[0:r, :, :], bsel[0:r, b:b + 1], None,
                                                    ALU.mult).then_inc(kb_done, 1)

            @block.vector
            def _(dve):
                link = chained(dve, dch)
                dve.wait_ge(cin, 16 * 8)
                link(nc.vector.tensor_copy(lev[:, :, :], lev_f[:, :, :]))
                link(nc.vector.memset(A_sb[:, :, :], 0.0))
                nc.vector.memset(S[:, :, :], 0.0).then_inc(cst, 1)
                dve.wait_ge(cst, 1)
                for i in range(TILES):
                    r, T = rows(i), tile_of(i)
                    dve.wait_ge(t_done, i + 1)
                    nc.vector.tensor_copy(ggT[:, 0:r], zp[0:16, 0:r]).then_inc(g_dve, 1)
                    dve.wait_ge(z_done, i + 1)
                    for p in range(2):
                        ins = nc.vector.tensor_scalar(z[:, p, 0:r], zp[:, P + p * P:P + p * P + r], gb[:, p:p + 1], None, ALU.add)
                        if p == 0:
                            link(ins)
                    ins.then_inc(z_biased, 1)
                    dve.wait_ge(az_done, i + 1)
                    link(nc.vector.tensor_scalar(z[:, :, 0:r], z[:, :, 0:r], 0.0, None, ALU.min))
                    dve.wait_ge(ln_done, i + 1)
                    link(nc.vector.tensor_tensor(z[:, :, 0:r], z[:, :, 0:r], az[:, :, 0:r], ALU.subtract))
                    o0 = 0 if i < NT else P
                    for p in range(2):
                        link(nc.vector.tensor_tensor_scan(cs[:, p, 0:r], reset[:, o0:o0 + r], z[:, p, 0:r], 0.0,
                                                          ALU.mult, ALU.add))
                    nb0 = 1 if i < NT else DEC_BATCH
                    T0 = r // nb0
                    link(nc.vector.tensor_copy(dec[:, :, :], cs[:, :, T0 - 1:r:T0] if i == NT else
                                               cs[:, :, r - 1:r].to_broadcast([P, 2, 8])))
                    for p in range(2):
                        link(nc.vector.tensor_tensor(
                            E[:, 0, p, 0:r].rearrange("p (b t) -> p b t", b=nb0),
                            dec[:, p, 0:nb0].unsqueeze(2).to_broadcast([P, nb0, T0]),
                            cs[:, p, 0:r].rearrange("p (b t) -> p b t", b=nb0), ALU.subtract))
                    link(nc.vector.tensor_copy(E[:, NL, :, 0:r], cs[:, :, 0:r]))
                    for l in range(1, lv(i)):
                        L = 2 ** (l - 1)
                        for p in range(2):
                            c3 = cs[:, p, 0:r].rearrange("p (b f t) -> p b f t", f=2, t=L)
                            e3 = E[:, l, p, 0:r].rearrange("p (b f t) -> p b f t", f=2, t=L)
                            nb = r // (2 * L)
                            anchor = c3[:, :, 0, L - 1:L].to_broadcast([P, nb, L])
                            nc.vector.tensor_tensor(e3[:, :, 0, :], anchor, c3[:, :, 0, :], ALU.subtract)
                            ins = nc.vector.tensor_tensor(e3[:, :, 1, :], c3[:, :, 1, :], anchor, ALU.subtract)
                            if l == lv(i) - 1 and p == 1:
                                ins.then_inc(d_done, 1)
                    dve.wait_ge(e_done, i + 1)
                    dve.wait_ge(t_act, i + 1)
                    n = lv(i)
                    nc.vector.tensor_tensor(qin[:, :, 0:r], E[:, NL, :, 0:r], qT[:, :, 0:r], ALU.mult)
                    nc.vector.tensor_tensor(kin[:, :, 0:r], E[:, 0, :, 0:r], kT[:, :, 0:r], ALU.mult)
                    for p in range(2):
                        qb = qT[:, p:p + 1, 0:r].to_broadcast([P, n - 1, r])
                        kb = kT[:, p:p + 1, 0:r].to_broadcast([P, n - 1, r])
                        link(nc.vector.tensor_tensor(QM[:, 1:n, p, 0:r], E[:, 1:n, p, 0:r], qb, ALU.mult))
                        ins = nc.vector.tensor_tensor(E[:, 1:n, p, 0:r], E[:, 1:n, p, 0:r], kb, ALU.mult)
                    ins.then_inc(qk_done, 1)
                    if i == NT:
                        dve.wait_ge(o_done, NT)
                        dve.wait_ge(lev_used, lev0[NT])
                        link(nc.vector.memset(A_sb[0:r, :, :, 0:r], 0.0))
                    for l in range(n):
                        g = lev0[i] + l
                        dve.wait_ge(lev_done, g + 1)
                        if g >= 1:
                            dve.wait_ge(lev_used, g)
                        for hf in range(2):
                            ins = nc.vector.copy_predicated(
                                A_sb[0:r, hf, :, 0:r], lev[0:r, l:l + 1, 0:r].to_broadcast([r, 2, r]),
                                ps[0:r, 3 + 2 * (g % 2) + hf, 0:2 * P].rearrange("s (h t) -> s h t", h=2)[:, :, 0:r])
                        ins.then_inc(lev_used, 1)
                    dve.wait_ge(er_done, i + 1)
                    link(nc.vector.tensor_scalar(er[0:r, :], er[0:r, :], 1.0, None, ALU.add))
                    link(nc.vector.reciprocal(er[0:r, :], er[0:r, :]))
                    link(nc.vector.tensor_tensor(er[0:r, :], er[0:r, :], T[0:r, C_GR:C_GR + 512], ALU.mult))
                    e4 = er[0:r, :].rearrange("p (h v) -> p h v", h=4)
                    link(nc.vector.tensor_tensor(e4, e4, ng[0:r, :].unsqueeze(1).to_broadcast([r, 4, DV]), ALU.mult))
                    if i < NT:
                        dve.wait_ge(kv_done, i + 1)
                        for h in range(GLA_H):
                            ins = nc.vector.scalar_tensor_tensor(
                                out=S[half(h), h // 2, :], in0=S[half(h), h // 2, :], scalar=dec[half(h), h // 2, 0:1],
                                in1=misc[half(h), (h // 2) * 256 + (h % 2) * DV:(h // 2) * 256 + (h % 2) * DV + DV],
                                op0=ALU.mult, op1=ALU.add)
                        ins.then_inc(kv_used, 1)
                    else:
                        for b in range(DEC_BATCH):
                            dve.wait_ge(kv_done, i + 1 + b)
                            for h in range(GLA_H):
                                ins = nc.vector.scalar_tensor_tensor(
                                    out=SS[half(h), b, h // 2, :], in0=SS[half(h), b, h // 2, :],
                                    scalar=dec[half(h), h // 2, b:b + 1],
                                    in1=misc[half(h), (h // 2) * 256 + (h % 2) * DV:(h // 2) * 256 + (h % 2) * DV + DV],
                                    op0=ALU.mult, op1=ALU.add)
                            ins.then_inc(kv_used, 1)
                    dve.wait_ge(sq_done, i + 1)
                    nc.vector.tensor_scalar(ssq[0:r, :], ssq[0:r, :], 1.0 / DV, RMS_EPS, ALU.mult, ALU.add).then_inc(ms_done, 1)
                    dve.wait_ge(rs_done, i + 1)
                    for h in range(GLA_H):
                        ins = nc.vector.scalar_tensor_tensor(
                            out=T[0:r, C_GR + h * DV:C_GR + (h + 1) * DV], in0=o_of(h, r),
                            scalar=rs[0:r, h:h + 1], in1=er[0:r, h * DV:(h + 1) * DV], op0=ALU.mult, op1=ALU.mult)
                    ins.then_inc(y_done, 1)
                dve.wait_ge(y_done, TILES)


TOPK = 256
NEG = -1e30
TAKEN = -3e38
AS = HD ** -0.5
IWS = 512.0 ** -0.5


def dsa_prompt(nc, st, A, C, O, H, Hs, XT):
    HEADS = [(kv, g) for g in range(4) for kv in range(2)]
    NH = len(HEADS)
    idx_steps = [(i, h, c) for i in range(2, NT) for h in range(8) for c in range(-(-(i + 1) * P // 512))]
    idx_no = {s: n for n, s in enumerate(idx_steps)}
    groups = [(i, n, c) for i in range(NT) for n in range(NH) for c in range(-(-(i + 1) // 4))]
    grp_no = {s: n for n, s in enumerate(groups)}
    with ExitStack() as ctx:
        sb = lambda n, s, d=F32: ctx.enter_context(nc.sbuf_tensor(f"dsa_{n}", s, d))
        sem = lambda n: st.sem(f"dsa_{n}")
        KT, IKT = sb("KT", [P, SEQ]), sb("IKT", [P, SEQ])
        qT, iqT = sb("qT", [P, 4, P]), sb("iqT", [P, 4, P])
        rel = sb("rel", [P, 4, 512])
        iws = sb("iws", [P, 8])
        sc, wk = sb("sc", [P, SEQ]), sb("wk", [P, SEQ])
        m8 = sb("m8", [P, 8])
        bias = sb("bias", [P, SEQ], BF16)
        identb = sb("identb", [P, P], BF16)
        causal = sb("causal", [P, P])
        Pb, PT = sb("P", [P, 2, SEQ]), sb("PT", [P, 2, NT, P])
        mx, nm, sm, rs = sb("mx", [P, 2]), sb("nm", [P, 2]), sb("sm", [P, NH]), sb("rs", [P, NH])
        ps = ctx.enter_context(nc.psum_tensor("dsa_ps", [P, 8, 512], F32))
        cin = sem("const_in")
        t_done, t_act = sem("transposed"), sem("transposed_copied")
        ix_done, ix_act, ix_dve = sem("index_dots"), sem("index_relu"), sem("index_added")
        b_done = sem("bias_ready")
        s_done, m_done, e_done = sem("scores"), sem("max_done"), sem("probs")
        pt_done, pt_copied = sem("probs_transposed"), sem("probsT_copied")
        o_done, y_done, yt_done, yt_act = sem("o_done"), sem("y_done"), sem("y_transposed"), sem("yT_copied")
        dch = sem("dve_step")
        half = lambda kv: slice(64 * kv, 64 * kv + 64)

        IB, used = {}, [0, 0]
        for s in idx_steps:
            hf = s[1] % 2
            IB[s] = 4 * hf + used[hf] % 4
            used[hf] += 1

        with nc.Block() as block:
            @block.sync
            def _(sp):
                sp.dma_start(causal[:, :], C["causal"]).then_inc(cin, 16)
                sp.wait_ge(cin, 16)

            @block.tensor
            def _(pe):
                for i in range(NT):
                    T = H[:, i, :]
                    if i >= 1:
                        pe.wait_ge(yt_act, 2 * i)
                        pe.wait_ge(pt_copied, grp_no[(i, 0, 0)])
                    for g in range(4):
                        nc.tensor.transpose(ps[:, 0, g * P:(g + 1) * P],
                                            T[:, C_DQ + g * P:C_DQ + (g + 1) * P], st.ident[:, :])
                        nc.tensor.transpose(ps[:, 1, g * P:(g + 1) * P], T[:, C_IQ + g * P:C_IQ + (g + 1) * P], st.ident[:, :])
                    nc.tensor.transpose(ps[:, 2, 0:P], T[:, C_DK:C_DK + P], st.ident[:, :])
                    nc.tensor.transpose(ps[:, 2, P:2 * P], T[:, C_IK:C_IK + P], st.ident[:, :]).then_inc(t_done, 1)
                    pe.wait_ge(t_act, 3 * (i + 1))
                    if i >= 2:
                        for h in range(8):
                            hf = half(h % 2)
                            for c in range(-(-(i + 1) * P // 512)):
                                g = idx_no[(i, h, c)]
                                n = min(512, (i + 1) * P - 512 * c)
                                if g >= 2 * 2:
                                    pe.wait_ge(ix_act, g - 3)
                                nc.tensor.matmul(ps[:, IB[(i, h, c)], 0:n], iqT[hf, h // 2, :],
                                                 IKT[hf, 512 * c:512 * c + n], start=True, stop=True).then_inc(ix_done, 1)
                        pe.wait_ge(ix_act, idx_no[(i, 7, -(-(i + 1) * P // 512) - 1)] + 1)
                    pe.wait_ge(b_done, i + 1)

                    def scores(n):
                        kv, g = HEADS[n]
                        a = i * NH + n
                        if a >= 2:
                            pe.wait_ge(e_done, a - 1)
                        for c in range(-(-(i + 1) * P // 512)):
                            w = min(512, (i + 1) * P - 512 * c)
                            nc.tensor.matmul(ps[:, 2 * kv + c, 0:w], identb[:, :], bias[:, 512 * c:512 * c + w],
                                             start=True, stop=False)
                            last = nc.tensor.matmul(ps[:, 2 * kv + c, 0:w], qT[half(kv), g, :], KT[half(kv), 512 * c:512 * c + w],
                                                    start=False, stop=True)
                        last.then_inc(s_done, 1)

                    def attend(n):
                        kv, g = HEADS[n]
                        a = i * NH + n
                        pe.wait_ge(e_done, a + 1)
                        for c in range(-(-(i + 1) // 4)):
                            gn = grp_no[(i, n, c)]
                            if gn >= 2:
                                pe.wait_ge(pt_copied, gn - 1)
                            for j in range(4 * c, min(4 * c + 4, i + 1)):
                                last = nc.tensor.transpose(ps[:, 4 + gn % 2, (j % 4) * P:(j % 4 + 1) * P],
                                                           Pb[:, a % 2, j * P:(j + 1) * P], st.ident[:, :])
                            last.then_inc(pt_done, 1)
                        pe.wait_ge(pt_copied, grp_no[(i, n, -(-(i + 1) // 4) - 1)] + 1)
                        h = kv * 4 + g
                        for j in range(i + 1):
                            last = nc.tensor.matmul(ps[:, 6, h * HD:(h + 1) * HD], PT[:, a % 2, j, :],
                                                    H[:, j, C_DV + kv * HD:C_DV + (kv + 1) * HD],
                                                    start=(j == 0), stop=(j == i))
                        last.then_inc(o_done, 1)

                    scores(0)
                    for n in range(NH):
                        if n + 1 < NH:
                            scores(n + 1)
                        attend(n)
                    pe.wait_ge(y_done, i + 1)
                    for k in range(KD):
                        c0 = C_GR + k * P if k < 4 else C_DQ + (k - 4) * P
                        last = nc.tensor.transpose(ps[:, 7 if k < 4 else 2, (k % 4) * P:(k % 4 + 1) * P],
                                                   T[:, c0:c0 + P], st.ident[:, :])
                        if k % 4 == 3:
                            last.then_inc(yt_done, 1)

            @block.scalar
            def _(act):
                for i in range(NT):
                    act.wait_ge(t_done, i + 1)
                    nc.scalar.copy(qT[:, :, :], ps[:, 0, :].rearrange("p (a t) -> p a t", a=4)).then_inc(t_act, 1)
                    nc.scalar.copy(iqT[:, :, :], ps[:, 1, :].rearrange("p (a t) -> p a t", a=4)).then_inc(t_act, 1)
                    nc.scalar.copy(KT[:, i * P:(i + 1) * P], ps[:, 2, 0:P])
                    nc.scalar.copy(IKT[:, i * P:(i + 1) * P], ps[:, 2, P:2 * P]).then_inc(t_act, 1)
                    if i >= 2:
                        for h in range(8):
                            for c in range(-(-(i + 1) * P // 512)):
                                g = idx_no[(i, h, c)]
                                n = min(512, (i + 1) * P - 512 * c)
                                act.wait_ge(ix_done, g + 1)
                                if g >= 4:
                                    act.wait_ge(ix_dve, g - 3)
                                nc.scalar.activation(rel[:, g % 4, 0:n], ps[:, IB[(i, h, c)], 0:n], ACT.Relu).then_inc(ix_act, 1)
                    L = (i + 1) * P
                    for n in range(NH):
                        kv, g = HEADS[n]
                        a = i * NH + n
                        act.wait_ge(m_done, a + 1)
                        if a >= 2:
                            act.wait_ge(o_done, a - 1)
                        nc.scalar.activation(Pb[:, a % 2, 0:L], ps[:, 2 * kv:2 * kv + 2, :].rearrange("p b n -> p (b n)")[:, 0:L],
                                             ACT.Exp, bias=nm[:, a % 2:a % 2 + 1], scale=AS,
                                             accum_out=sm[:, n:n + 1]).then_inc(e_done, 1)
                    for k in range(2):
                        act.wait_ge(yt_done, 2 * i + k + 1)
                        nc.scalar.copy(XT[:, 4 * k:4 * k + 4, i * P:(i + 1) * P],
                                       ps[:, 7 if k == 0 else 2, :].rearrange("p (a t) -> p a t", a=4)).then_inc(yt_act, 1)

            @block.vector
            def _(dve):
                link = chained(dve, dch)
                dve.wait_ge(cin, 16)
                link(nc.vector.tensor_copy(identb[:, :], st.ident[:, :]))
                link(nc.vector.memset(bias[:, :], 0.0))
                for i in range(NT):
                    T, L = H[:, i, :], (i + 1) * P
                    if i >= 1:
                        dve.wait_ge(s_done, i * NH)
                    if i < 2:
                        if i == 1:
                            link(nc.vector.memset(bias[:, 0:P], 0.0))
                        nc.vector.tensor_copy(bias[:, L - P:L], causal[:, :]).then_inc(b_done, 1)
                    else:
                        link(nc.vector.tensor_scalar(iws[:, :], T[:, C_IW:C_IW + 8], IWS, None, ALU.mult))
                        for h in range(8):
                            for c in range(-(-L // 512)):
                                g = idx_no[(i, h, c)]
                                n = min(512, L - 512 * c)
                                dve.wait_ge(ix_act, g + 1)
                                if h == 0:
                                    nc.vector.tensor_scalar(sc[:, 512 * c:512 * c + n], rel[:, g % 4, 0:n], iws[:, h:h + 1],
                                                            None, ALU.mult).then_inc(ix_dve, 1)
                                else:
                                    dve.wait_ge(ix_dve, g)
                                    nc.vector.scalar_tensor_tensor(
                                        out=sc[:, 512 * c:512 * c + n], in0=rel[:, g % 4, 0:n], scalar=iws[:, h:h + 1],
                                        in1=sc[:, 512 * c:512 * c + n], op0=ALU.mult, op1=ALU.add).then_inc(ix_dve, 1)
                        dve.wait_ge(ix_dve, idx_no[(i, 7, -(-L // 512) - 1)] + 1)
                        link(nc.vector.tensor_tensor(sc[:, L - P:L], sc[:, L - P:L], causal[:, :], ALU.add))
                        for k in range(TOPK // 8):
                            src = sc if k == 0 else wk
                            link(nc.vector.max(m8[:, :], src[:, 0:L]))
                            link(nc.vector.match_replace(wk[:, 0:L], m8[:, :], src[:, 0:L], TAKEN))
                        nc.vector.tensor_scalar(bias[:, 0:L], wk[:, 0:L], -2e38, NEG, ALU.is_ge, ALU.mult).then_inc(b_done, 1)

                    def row_max(n):
                        kv, g = HEADS[n]
                        a = i * NH + n
                        dve.wait_ge(s_done, a + 1)
                        link(nc.vector.reduce_max(mx[:, a % 2:a % 2 + 1],
                                                  ps[:, 2 * kv:2 * kv + 2, :].rearrange("p b n -> p (b n)")[:, 0:L], AX_X))
                        if a >= 2:
                            dve.wait_ge(e_done, a - 1)
                        nc.vector.tensor_scalar(nm[:, a % 2:a % 2 + 1], mx[:, a % 2:a % 2 + 1], -AS, None,
                                                ALU.mult).then_inc(m_done, 1)

                    def copy_pt(n):
                        a = i * NH + n
                        if a >= 2:
                            dve.wait_ge(o_done, a - 1)
                        for c in range(-(-(i + 1) // 4)):
                            gn = grp_no[(i, n, c)]
                            w = min(4, i + 1 - 4 * c)
                            dve.wait_ge(pt_done, gn + 1)
                            nc.vector.tensor_copy(PT[:, a % 2, 4 * c:4 * c + w, :],
                                                  ps[:, 4 + gn % 2, 0:w * P].rearrange("p (a t) -> p a t", t=P)).then_inc(pt_copied, 1)

                    row_max(0)
                    for n in range(NH):
                        if n + 1 < NH:
                            row_max(n + 1)
                        copy_pt(n)
                    dve.wait_ge(e_done, (i + 1) * NH)
                    link(nc.vector.reciprocal(rs[:, :], sm[:, :]))
                    dve.wait_ge(o_done, (i + 1) * NH)
                    for kv in range(2):
                        ins = nc.vector.tensor_tensor(
                            T[:, C_DQ + kv * 256:C_DQ + (kv + 1) * 256].rearrange("p (g d) -> p g d", g=4),
                            ps[:, 6, kv * 256:(kv + 1) * 256].rearrange("p (g d) -> p g d", g=4),
                            rs[:, kv::2].unsqueeze(2).to_broadcast([P, 4, HD]), ALU.mult)
                    ins.then_inc(y_done, 1)
                dve.wait_ge(y_done, NT)


PAGES = 16
PAST = PAGES * P
LK = PAST + DEC_SEQ
CHUNKS = [(0, 512), (512, 512), (1024, 512), (1536, 512), (2048, 8)]


def dsa_sample(nc, st, A, C, O, Hs, XT):
    NB, NP_ = DEC_BATCH, DEC_BATCH // 2
    scr_w = nc.dram_tensor("scratch_iw", (NS, 8), F32, kind="Internal").ap()
    scr_y = nc.dram_tensor("scratch_y", (NS, 512), F32, kind="Internal").ap()
    n_pool = A["cache_k"].shape[1]
    with ExitStack() as ctx:
        sb = lambda n, s, d=F32: ctx.enter_context(nc.sbuf_tensor(f"smp_{n}", s, d))
        sem = lambda n: st.sem(f"smp_{n}")
        pages = sb("pages", [1, NB * PAGES], I32)
        idxp, ikT = sb("idxp", [P, 2, PAGES, HD]), sb("ikT", [HD, 2, LK])
        iqT, ikn = sb("iqT", [HD, NB, 8, DEC_SEQ]), sb("ikn", [HD, NS])
        rel = sb("rel", [NS, 2, 512])
        iwd = sb("iwd", [NS, NB])
        gat, gw = sb("gat", [NS, NB, NS]), sb("gw", [NS, NB, NS])
        sc, wk, m8 = sb("sc", [NS, LK]), sb("wk", [NS, LK]), sb("m8", [NS, 8])
        bias = sb("bias", [NS, LK], BF16)
        c8 = sb("c8", [NS, 8])
        spf, spb = sb("spf", [NS, NP_, P]), sb("spb", [NS, NP_, P], BF16)
        qz, KnT = sb("qz", [P, NB, 2, 4, DEC_SEQ]), sb("KnT", [P, NS])
        Kp, KT = sb("Kp", [P, 2, PAGES, P]), sb("KT", [P, 2, LK])
        Vp, Vn = sb("Vp", [P, 2, PAGES, P]), sb("Vn", [DEC_SEQ, NB, P])
        Pb, PT = sb("P", [P, LK]), sb("PT", [P, PAGES + 1, P])
        mx, nm, sm, rs = sb("mx", [P, 1]), sb("nm", [P, 1]), sb("sm", [P, 1]), sb("rs", [P, 1])
        yq = sb("yq", [P, NP_, HD])
        ps = ctx.enter_context(nc.psum_tensor("smp_ps", [P, 8, 512], F32))
        flat = ps[:, 0:5, :].rearrange("p b n -> p (b n)")
        cin, pin = sem("const_in"), sem("page_table_in")
        ix_in = [sem("index_pages0"), sem("index_pages1")]
        k_in, v_in = [sem("k_pages0"), sem("k_pages1")], [sem("v_pages0"), sem("v_pages1")]
        w_out, w_in, vn_in = sem("iw_out"), sem("iw_in"), sem("v_new_in")
        h_t, h_c = sem("heads_transposed"), sem("heads_copied")
        it_done, it_copied = sem("index_transposed"), sem("index_copied")
        dt_done, dt_relu, sum_done = sem("dots"), sem("relu"), sem("summed")
        gw_done, b_done = sem("weights_ready"), sem("bias_ready")
        kt_done, kt_copied = sem("k_transposed"), sem("k_copied")
        s_done, m_done, e_done, pt_done, pt_copied = (sem("scores"), sem("max"), sem("probs"), sem("p_transposed"),
                                                      sem("p_copied"))
        o_done, y_done, y_out, y_in, yt_done, yt_copied = (sem("o"), sem("y"), sem("y_out"), sem("y_in"),
                                                           sem("yT"), sem("yT_copied"))
        dch, ach = sem("dve_step"), sem("act_step")
        zeroed = sem("qz_zeroed")

        with nc.Block() as block:
            @block.sync
            def _(sp):
                sp.dma_start(pages[:, :], A["page_table"].rearrange("(o a) b -> o (a b)", o=1)).then_inc(pin, 16)
                sp.dma_start(scr_w, Hs[0:NS, C_IW:C_IW + 8]).then_inc(w_out, 16)
                for dst, src in ((gat[:, :, :], C["gather"]), (c8[:, :], C["causal8"]), (spf[:, :, :], C["spread"])):
                    sp.dma_start(dst, src).then_inc(cin, 16)
                sp.wait_ge(pin, 16)
                sp.wait_ge(w_out, 16)
                for h in range(8):
                    sp.dma_start(iwd[8 * h:8 * h + 8, :], bass.AP(scr_w.tensor, h, [[8, 8], [64, 8]]),
                                 allow_slow_non_contiguous=True).then_inc(w_in, 16)
                for b in range(NB):
                    sp.dma_start(Vn[:, b, :], Hs[8 * b:8 * b + 8, C_DV:C_DV + P]).then_inc(vn_in, 16)

                def load_pages(b, cache, dst, landed):
                    with sp.Fori(0, PAGES) as j:
                        page = sp.value_load(pages[0:1, bass.ds(j + b * PAGES, 1)], min_val=0, max_val=n_pool - 1)
                        src = cache[bass.ds(page, 1)]
                        src = src.rearrange("o p k d -> (o p) (k d)") if len(src.shape) == 4 else src.rearrange("o p d -> (o p) d")
                        sp.dma_start(dst(j), src).then_inc(landed, 16)

                def load_kv(b):
                    s = b % 2
                    if b >= 2:
                        sp.wait_ge(kt_done, 4 * (b - 1))
                        sp.wait_ge(o_done, b // 2)
                    load_pages(b, A["cache_k"][0], lambda j: Kp[:, s, bass.ds(j, 1), :].rearrange("p o c -> p (o c)"), k_in[s])
                    load_pages(b, A["cache_v"][0], lambda j: Vp[:, s, bass.ds(j, 1), :].rearrange("p o c -> p (o c)"), v_in[s])

                for b in range(NB):
                    s = b % 2
                    if b >= 2:
                        sp.wait_ge(it_done, 4 * (b - 1))
                    load_pages(b, A["cache_idx"][0], lambda j: idxp[:, s, bass.ds(j, 1), :].rearrange("p o c -> p (o c)"), ix_in[s])
                    if b == 1:
                        load_kv(0)
                        load_kv(1)
                for b in range(2, NB):
                    load_kv(b)

            @block.gpsimd
            def _(pool):
                for p in range(NP_):
                    pool.wait_ge(y_done, p + 1)
                    for b2 in range(2):
                        pool.dma_start(bass.AP(scr_y.tensor, (2 * p + b2) * DEC_SEQ * 512, [[HD, 8], [512, DEC_SEQ], [1, HD]]),
                                       yq[64 * b2:64 * b2 + 64, p, :]).then_inc(y_out, 16)
                pool.wait_ge(y_out, 32 * NP_)
                pool.dma_start(Hs[0:NS, C_DQ:C_DQ + 512], scr_y).then_inc(y_in, 16)
                pool.wait_ge(y_in, 16)

            @block.tensor
            def _(pe):
                I64 = st.ident[0:NS, 0:NS]
                for h in range(8):
                    nc.tensor.transpose(ps[0:HD, 0, h * NS:(h + 1) * NS], Hs[0:NS, C_IQ + h * HD:C_IQ + (h + 1) * HD], I64)
                nc.tensor.transpose(ps[0:HD, 1, 0:NS], Hs[0:NS, C_IK:C_IK + HD], I64)
                nc.tensor.transpose(ps[:, 1, NS:2 * NS], Hs[0:NS, C_DK:C_DK + P], I64)
                for g in range(4):
                    last = nc.tensor.transpose(ps[:, 2, g * NS:(g + 1) * NS], Hs[0:NS, C_DQ + g * P:C_DQ + (g + 1) * P], I64)
                last.then_inc(h_t, 1)
                pe.wait_ge(h_c, 5)
                for b in range(NB):
                    s = b % 2
                    pe.wait_ge(ix_in[s], 16 * PAGES * (b // 2 + 1))
                    for q in range(4):
                        g = 4 * b + q
                        if g >= 1:
                            pe.wait_ge(it_copied, g + (g - 1) // 4)
                        for j in range(4):
                            last = nc.tensor.transpose(ps[0:HD, 5, j * P:(j + 1) * P], idxp[:, s, 4 * q + j, :], st.ident[:, :])
                        last.then_inc(it_done, 1)
                    pe.wait_ge(it_copied, 5 * (b + 1))

                    def add_heads(c):
                        g, (c0, n) = 5 * b + c, CHUNKS[c]
                        pe.wait_ge(dt_relu, g + 1)
                        if g == 0:
                            pe.wait_ge(gw_done, 1)
                        nc.tensor.matmul(ps[0:NS, c, 0:n], gw[:, b, :], rel[:, g % 2, 0:n],
                                         start=(b == 0), stop=(b == NB - 1)).then_inc(sum_done, 1)

                    for c, (c0, n) in enumerate(CHUNKS):
                        g = 5 * b + c
                        if g >= 2:
                            pe.wait_ge(dt_relu, g - 1)
                        nc.tensor.matmul(ps[0:NS, 6 + g % 2, 0:n], iqT[:, b, :, :].rearrange("d h q -> d (h q)"),
                                         ikT[:, s, c0:c0 + n], start=True, stop=True).then_inc(dt_done, 1)
                        if c >= 1:
                            add_heads(c - 1)
                    add_heads(4)

                def keys_T(b):
                    s = b % 2
                    pe.wait_ge(k_in[s], 16 * PAGES * (b // 2 + 1))
                    for q in range(4):
                        g = 4 * b + q
                        if g >= 2:
                            pe.wait_ge(kt_copied, g - 1)
                        for j in range(4):
                            last = nc.tensor.transpose(ps[:, 5 + g % 2, j * P:(j + 1) * P], Kp[:, s, 4 * q + j, :], st.ident[:, :])
                        last.then_inc(kt_done, 1)

                pe.wait_ge(dt_relu, 5 * NB)
                for p in range(NP_):
                    if p >= 1:
                        pe.wait_ge(pt_copied, 5 * p)
                    keys_T(2 * p)
                    keys_T(2 * p + 1)
                    pe.wait_ge(kt_copied, 8 * (p + 1))
                    if p == 0:
                        pe.wait_ge(b_done, 1)
                    else:
                        pe.wait_ge(e_done, p)
                    for c, (c0, n) in enumerate(CHUNKS):
                        nc.tensor.matmul(ps[:, c, 0:n], spb[:, p, :], bias[:, c0:c0 + n], start=True, stop=False)
                        for b2 in range(2):
                            last = nc.tensor.matmul(ps[64 * b2:64 * b2 + 64, c, 0:n],
                                                    qz[:, 2 * p + b2, :, :, :].rearrange("d v g q -> d (v g q)"),
                                                    KT[:, b2, c0:c0 + n], start=False, stop=True)
                    last.then_inc(s_done, 1)
                    pe.wait_ge(e_done, p + 1)
                    for c in range(5):
                        g = 5 * p + c
                        if g >= 2:
                            pe.wait_ge(pt_copied, g - 1)
                        for j in range(4 * c, min(4 * c + 4, PAGES + 1)):
                            n = P if j < PAGES else DEC_SEQ
                            last = nc.tensor.transpose(ps[0:n, 5 + g % 2, (j % 4) * P:(j % 4 + 1) * P],
                                                       Pb[:, j * P:j * P + n], st.ident[:, :])
                        last.then_inc(pt_done, 1)
                    pe.wait_ge(pt_copied, 5 * (p + 1))
                    pe.wait_ge(vn_in, 16 * NB)
                    if p >= 1:
                        pe.wait_ge(y_done, p)
                    for b2 in range(2):
                        pe.wait_ge(v_in[b2], 16 * PAGES * (p + 1))
                        r = slice(64 * b2, 64 * b2 + 64)
                        for j in range(PAGES):
                            nc.tensor.matmul(ps[r, 7, 0:P], PT[:, j, r], Vp[:, b2, j, :], start=(j == 0), stop=False)
                        last = nc.tensor.matmul(ps[r, 7, 0:P], PT[0:DEC_SEQ, PAGES, r], Vn[:, 2 * p + b2, :], start=False, stop=True)
                    last.then_inc(o_done, 1)
                pe.wait_ge(y_in, 16)
                for k in range(KD):
                    c0 = C_GR + k * P if k < 4 else C_DQ + (k - 4) * P
                    last = nc.tensor.transpose(ps[:, 0, k * NS:(k + 1) * NS], Hs[0:NS, c0:c0 + P], I64)
                last.then_inc(yt_done, 1)

            @block.scalar
            def _(act):
                act.wait_ge(h_t, 1)
                nc.scalar.copy(iqT[:, :, :, :].rearrange("d b h q -> d h b q"),
                               ps[0:HD, 0, :].rearrange("d (h b q) -> d h b q", h=8, b=NB)).then_inc(h_c, 1)
                nc.scalar.copy(ikn[:, :], ps[0:HD, 1, 0:NS]).then_inc(h_c, 1)
                nc.scalar.copy(KnT[:, :], ps[:, 1, NS:2 * NS]).then_inc(h_c, 1)
                act.wait_ge(zeroed, 1)
                for kv in range(2):
                    hf = slice(64 * kv, 64 * kv + 64)
                    nc.scalar.copy(qz[hf, :, kv, :, :].rearrange("d b g q -> d g b q"),
                                   ps[hf, 2, 0:4 * NS].rearrange("d (g b q) -> d g b q", g=4, b=NB)).then_inc(h_c, 1)
                act.wait_ge(h_c, 5)

                for b in range(NB):
                    s = b % 2
                    if b >= 2:
                        act.wait_ge(dt_done, 5 * (b - 1))
                    for q in range(4):
                        act.wait_ge(it_done, 4 * b + q + 1)
                        nc.scalar.copy(ikT[:, s, 512 * q:512 * (q + 1)], ps[0:HD, 5, :]).then_inc(it_copied, 1)
                    nc.scalar.copy(ikT[:, s, PAST:LK], ikn[:, 8 * b:8 * b + 8]).then_inc(it_copied, 1)
                    for c, (c0, n) in enumerate(CHUNKS):
                        g = 5 * b + c
                        act.wait_ge(dt_done, g + 1)
                        if g >= 2:
                            act.wait_ge(sum_done, g - 1)
                        nc.scalar.activation(rel[:, g % 2, 0:n], ps[0:NS, 6 + g % 2, 0:n], ACT.Relu).then_inc(dt_relu, 1)
                for p in range(NP_):
                    for b2 in range(2):
                        b = 2 * p + b2
                        if p >= 1 and b2 == 0:
                            act.wait_ge(s_done, p)
                        for q in range(4):
                            act.wait_ge(kt_done, 4 * b + q + 1)
                            ins = nc.scalar.copy(KT[:, b2, 512 * q:512 * (q + 1)], ps[:, 5 + (4 * b + q) % 2, :])
                            if q == 3:
                                link_kn = nc.scalar.copy(KT[:, b2, PAST:LK], KnT[:, 8 * b:8 * b + 8])
                                link_kn.then_inc(kt_copied, 1)
                            else:
                                ins.then_inc(kt_copied, 1)
                    act.wait_ge(m_done, p + 1)
                    if p >= 1:
                        act.wait_ge(pt_done, 5 * p)
                    nc.scalar.activation(Pb[:, :], flat[:, 0:LK], ACT.Exp, bias=nm[:, 0:1], scale=AS,
                                         accum_out=sm[:, 0:1]).then_inc(e_done, 1)
                act.wait_ge(yt_done, 1)
                nc.scalar.copy(XT[:, :, SEQ:NTOK], ps[:, 0, :].rearrange("p (k t) -> p k t", k=KD)).then_inc(yt_copied, 1)
                act.wait_ge(yt_copied, 1)

            @block.vector
            def _(dve):
                link = chained(dve, dch)
                nc.vector.memset(qz[:, :, :, :, :], 0.0).then_inc(zeroed, 1)
                dve.wait_ge(cin, 48)
                link(nc.vector.tensor_copy(spb[:, :, :], spf[:, :, :]))
                dve.wait_ge(w_in, 128)
                for b in range(NB):
                    link(nc.vector.tensor_scalar(gw[:, b, :], gat[:, b, :], iwd[:, b:b + 1], IWS, ALU.mult, ALU.mult))
                dve.sem_inc(gw_done, 1)
                dve.wait_ge(sum_done, 5 * NB)
                link(nc.vector.tensor_copy(sc[:, 0:PAST], ps[0:NS, 0:4, :].rearrange("p b n -> p (b n)")))
                link(nc.vector.tensor_tensor(sc[:, PAST:LK], ps[0:NS, 4, 0:8], c8[:, :], ALU.add))
                for k in range(TOPK // 8):
                    src = sc if k == 0 else wk
                    link(nc.vector.max(m8[:, :], src[:, :]))
                    link(nc.vector.match_replace(wk[:, :], m8[:, :], src[:, :], TAKEN))
                nc.vector.tensor_scalar(bias[:, :], wk[:, :], -2e38, NEG, ALU.is_ge, ALU.mult).then_inc(b_done, 1)
                for p in range(NP_):
                    dve.wait_ge(s_done, p + 1)
                    link(nc.vector.reduce_max(mx[:, :], flat[:, 0:LK], AX_X))
                    if p >= 1:
                        dve.wait_ge(e_done, p)
                    nc.vector.tensor_scalar(nm[:, :], mx[:, :], -AS, None, ALU.mult).then_inc(m_done, 1)
                    if p >= 1:
                        dve.wait_ge(o_done, p)
                    for c in range(5):
                        g = 5 * p + c
                        dve.wait_ge(pt_done, g + 1)
                        if c < 4:
                            nc.vector.tensor_copy(PT[:, 4 * c:4 * c + 4, :],
                                                  ps[:, 5 + g % 2, :].rearrange("p (a t) -> p a t", a=4)).then_inc(pt_copied, 1)
                        else:
                            nc.vector.tensor_copy(PT[0:DEC_SEQ, PAGES, :], ps[0:DEC_SEQ, 5 + g % 2, 0:P]).then_inc(pt_copied, 1)
                    dve.wait_ge(e_done, p + 1)
                    link(nc.vector.reciprocal(rs[:, :], sm[:, :]))
                    dve.wait_ge(o_done, p + 1)
                    for b2 in range(2):
                        for kv in range(2):
                            r = slice(64 * b2 + 32 * kv, 64 * b2 + 32 * kv + 32)
                            ins = nc.vector.tensor_scalar(yq[r, p, :], ps[r, 7, kv * HD:(kv + 1) * HD], rs[r, 0:1],
                                                          None, ALU.mult)
                    ins.then_inc(y_done, 1)


class LayerNorm:

    def __init__(self, st, ctx, tag, l, which, X, A):
        nc = st.nc
        self.nc, self.X = nc, X
        self.src = [bcast_rows(A["ln_g"][l, which], D), bcast_rows(A["ln_b"][l, which], D)]
        sb = lambda n, s: ctx.enter_context(nc.sbuf_tensor(f"{tag}_{n}", s, F32))
        self.gb, self.stats, self.mv, self.rstd = (sb("gb", [P, 2, D]), sb("stats", [P, 2, 12]), sb("mv", [P, 2, 2]),
                                                   sb("rstd", [P, 2, 1]))
        self.gb_in, self.var_ready, self.rstd_ready, self.scaled, self.gained, self.norm_done = (
            st.sem(f"{tag}_{n}") for n in ("gb_in", "var_ready", "rstd_ready", "scaled", "gained", "norm_done"))

    def load(self, eng):
        for k in range(2):
            eng.dma_start(self.gb[:, k, :], self.src[k]).then_inc(self.gb_in, 16)

    def dve_stats(self, i, link):
        r, v, s = rows(i), self.nc.vector, i % 2
        for h in range(2):
            link(v.bn_stats(self.stats[0:r, s, 6 * h:6 * h + 6], self.X[0:r, i, 512 * h:512 * h + 512]))
        link(v.bn_aggr(self.mv[0:r, s, :], self.stats[0:r, s, :]))
        v.tensor_scalar(self.mv[0:r, s, 1:2], self.mv[0:r, s, 1:2], LN_EPS, None, ALU.add).then_inc(self.var_ready, 1)

    def act(self, act, i):
        r, s = rows(i), i % 2
        act.wait_ge(self.var_ready, i + 1)
        if i >= 2:
            act.wait_ge(self.scaled, i - 1)
        self.nc.scalar.activation(self.rstd[0:r, s, :], self.mv[0:r, s, 1:2], ACT.Ln).then_inc(self.rstd_ready, 1)
        act.wait_ge(self.rstd_ready, 2 * i + 1)
        self.nc.scalar.activation(self.rstd[0:r, s, :], self.rstd[0:r, s, :], ACT.Exp, scale=-0.5).then_inc(self.rstd_ready, 1)

    def dve_scale(self, dve, i):
        r, s = rows(i), i % 2
        dve.wait_ge(self.rstd_ready, 2 * i + 2)
        self.nc.vector.tensor_scalar(self.X[0:r, i, :], self.X[0:r, i, :], self.mv[0:r, s, 0:1], self.rstd[0:r, s, :],
                                     ALU.subtract, ALU.mult).then_inc(self.scaled, 1)

    def pool(self, pool, i):
        r = rows(i)
        if i == 0:
            pool.wait_ge(self.gb_in, 32)
        pool.wait_ge(self.scaled, i + 1)
        self.nc.gpsimd.tensor_tensor(self.X[0:r, i, :], self.X[0:r, i, :], self.gb[0:r, 0, :], ALU.mult).then_inc(self.gained, 1)
        pool.wait_ge(self.gained, i + 1)
        self.nc.gpsimd.tensor_tensor(self.X[0:r, i, :], self.X[0:r, i, :], self.gb[0:r, 1, :], ALU.add).then_inc(self.norm_done, 1)


def out_projection(nc, st, A, w, l, XT, X, x_rows):
    tag = f"out{l}"
    with ExitStack() as ctx:
        sem = lambda n: st.sem(f"{tag}_{n}")
        wbuf = ctx.enter_context(nc.sbuf_tensor(f"{tag}_w", [P, 2, KD, 512], F32))
        ps = ctx.enter_context(nc.psum_tensor(f"{tag}_ps", [P, 8, 512], F32))
        ln = LayerNorm(st, ctx, f"{tag}_ln", l, 0, X, A)
        w_in, x_in = [sem("w_in0"), sem("w_in1")], sem("x_in")
        mm_done, added, t_done, t_copied, dch = sem("mm_done"), sem("added"), sem("transposed"), sem("copied"), sem("dve_step")
        w_v = w.rearrange("(k p) n -> p k n", p=P)
        with nc.Block() as block:
            @block.sync
            def _(sp):
                for c in range(2):
                    sp.dma_start(wbuf[:, c, :, :], w_v[:, :, 512 * c:512 * c + 512]).then_inc(w_in[c], 16)
                ln.load(sp)

            @block.tensor
            def _(pe):
                def transposes(i):
                    pe.wait_ge(ln.norm_done, i + 1)
                    for h in range(2):
                        j, r = 2 * i + h, rows(i)
                        if j >= 4:
                            pe.wait_ge(t_copied, j - 3)
                        for k in range(4):
                            kk = 4 * h + k
                            last = nc.tensor.transpose(ps[:, 4 + j % 4, k * P:k * P + r], X[0:r, i, kk * P:(kk + 1) * P],
                                                       st.ident[0:r, 0:r])
                        last.then_inc(t_done, 1)

                LAG = 2
                for i in range(TILES):
                    r = rows(i)
                    for c in range(2):
                        s = 2 * i + c
                        if i == 0:
                            pe.wait_ge(w_in[c], 16)
                        if s >= 4:
                            pe.wait_ge(added, s - 3)
                        for k in range(KD):
                            last = nc.tensor.matmul(ps[0:r, s % 4, :], XT[:, k, i * P:i * P + r], wbuf[:, c, k, :],
                                                    start=(k == 0), stop=(k == KD - 1))
                        last.then_inc(mm_done, 1)
                    if i >= LAG:
                        transposes(i - LAG)
                for i in range(TILES - LAG, TILES):
                    transposes(i)

            @block.scalar
            def _(act):
                def copy_t(i):
                    for h in range(2):
                        j, r = 2 * i + h, rows(i)
                        act.wait_ge(t_done, j + 1)
                        nc.scalar.copy(XT[:, 4 * h:4 * h + 4, i * P:i * P + r],
                                       ps[:, 4 + j % 4, :].rearrange("p (k t) -> p k t", k=4)[:, :, 0:r]).then_inc(t_copied, 1)

                for i in range(TILES):
                    ln.act(act, i)
                    if i >= 1:
                        copy_t(i - 1)
                copy_t(TILES - 1)

            @block.gpsimd
            def _(pool):
                if x_rows is not None:
                    pool.dma_start(X[:, 0:NT, :], A["x_prompt"][0].rearrange("(i p) c -> p i c", p=P)).then_inc(x_in, 16)
                    pool.dma_start(X[0:NS, NT, :], x_rows(NT)).then_inc(x_in, 16)
                for i in range(TILES):
                    ln.pool(pool, i)

            @block.vector
            def _(dve):
                link = chained(dve, dch)
                if x_rows is not None:
                    dve.wait_ge(x_in, 32)
                for i in range(TILES):
                    r = rows(i)
                    for c in range(2):
                        s = 2 * i + c
                        dve.wait_ge(mm_done, s + 1)
                        xs = X[0:r, i, 512 * c:512 * c + 512]
                        nc.vector.scalar_tensor_tensor(out=xs, in0=xs, scalar=ALPHA, in1=ps[0:r, s % 4, :],
                                                       op0=ALU.mult, op1=ALU.add).then_inc(added, 1)
                    dve.wait_ge(added, 2 * i + 2)
                    ln.dve_stats(i, link)
                    if i >= 1:
                        ln.dve_scale(dve, i - 1)
                ln.dve_scale(dve, TILES - 1)
                dve.wait_ge(ln.scaled, TILES)


TOKC = [(0, 384), (384, 384), (768, 320)]
NF = 256


def ffn(nc, st, A, l, XT, X, y_out):
    tag = f"ffn{l}"
    with ExitStack() as ctx:
        aT = ctx.enter_context(nc.sbuf_tensor(f"{tag}_aT", [P, KF, NTOK], F32))
        ffn_up(nc, st, A["ffn_w_gu"][l], f"{tag}u", XT, aT)
        ffn_down(nc, st, A, l, f"{tag}d", aT, XT, X, y_out)


def ffn_up(nc, st, w, tag, XT, aT):
    w_v = w.rearrange("(k p) n -> p k n", p=P)
    with ExitStack() as ctx:
        sem = lambda n: st.sem(f"{tag}_{n}")
        wbuf = ctx.enter_context(nc.sbuf_tensor(f"{tag}_w", [P, 2, 2, KD, P], F32))
        sg = ctx.enter_context(nc.sbuf_tensor(f"{tag}_sg", [P, 3, 384], F32))
        ps = ctx.enter_context(nc.psum_tensor(f"{tag}_ps", [P, 3, 2, 512], F32))
        w_in = [sem("w_in0"), sem("w_in1")]
        mm_done, silu_done, prod_done = sem("mm_done"), sem("silu_done"), sem("prod_done")
        with nc.Block() as block:
            @block.sync
            def _(sp):
                def load(ff, s):
                    for k in range(2):
                        sp.dma_start(wbuf[:, s, k, :, :], w_v[:, :, bass.ds(ff * P + k * D_FF, P)]).then_inc(w_in[s], 16)
                load(0, 0)
                load(1, 1)
                with sp.Fori(0, KF // 2 - 1) as it:
                    for s in range(2):
                        sp.wait_ge(mm_done, it * 6 + (3 * s + 3))
                        load(it * 2 + (2 + s), s)

            @block.tensor
            def _(pe):
                def body(it, first):
                    for s in range(2):
                        pe.wait_ge(w_in[s], it * 32 + 32)
                        for t, (t0, n) in enumerate(TOKC):
                            if not (first and s == 0):
                                pe.wait_ge(prod_done, it * 6 + (3 * s + t - 2))
                            for k2 in range(2):
                                for k in range(KD):
                                    last = nc.tensor.matmul(ps[:, t, k2, 0:n], wbuf[:, s, k2, k, :], XT[:, k, t0:t0 + n],
                                                            start=(k == 0), stop=(k == KD - 1))
                            last.then_inc(mm_done, 1)
                body(0, True)
                with pe.Fori(1, KF // 2) as it:
                    body(it, False)

            @block.scalar
            def _(act):
                def body(it, first):
                    for s in range(2):
                        for t, (t0, n) in enumerate(TOKC):
                            act.wait_ge(mm_done, it * 6 + (3 * s + t + 1))
                            if not (first and s == 0):
                                act.wait_ge(prod_done, it * 6 + (3 * s + t - 2))
                            nc.scalar.activation(sg[:, t, 0:n], ps[:, t, 0, 0:n], ACT.Silu).then_inc(silu_done, 1)
                body(0, True)
                with act.Fori(1, KF // 2) as it:
                    body(it, False)

            @block.vector
            def _(dve):
                with dve.Fori(0, KF // 2) as it:
                    for s in range(2):
                        for t, (t0, n) in enumerate(TOKC):
                            dve.wait_ge(silu_done, it * 6 + (3 * s + t + 1))
                            nc.vector.tensor_tensor(aT[:, bass.ds(it * 2 + s, 1), t0:t0 + n].rearrange("p o n -> p (o n)"),
                                                    sg[:, t, 0:n], ps[:, t, 1, 0:n], ALU.mult).then_inc(prod_done, 1)
                dve.wait_ge(prod_done, 3 * KF)


def ffn_down(nc, st, A, l, tag, aT, XT, X, y_out):
    NCH, KH = D // NF, KF // 2
    w_v = A["ffn_w_down"][l].rearrange("(k p) n -> p k n", p=P)
    with ExitStack() as ctx:
        sem = lambda n: st.sem(f"{tag}_{n}")
        wbuf = ctx.enter_context(nc.sbuf_tensor(f"{tag}_w", [P, KF, NF], F32))
        ps = ctx.enter_context(nc.psum_tensor(f"{tag}_ps", [P, 8, 512], F32))
        ln = LayerNorm(st, ctx, f"{tag}_ln", l, 1, X, A)
        w_in, w_used = [sem("w_in0"), sem("w_in1")], [sem("w_used0"), sem("w_used1")]
        mm_done, added, t_done, t_copied, dch = sem("mm_done"), sem("added"), sem("transposed"), sem("copied"), sem("dve_step")
        stored = sem("stored")

        def acc(i):
            return ps[0:rows(i), i // 2, (i % 2) * NF:(i % 2 + 1) * NF]

        def acc_last(i):
            return ps[0:rows(i), i % 5, 0:NF]

        with nc.Block() as block:
            @block.sync
            def _(sp):
                def load(c, h):
                    sp.dma_start(wbuf[:, h * KH:(h + 1) * KH, :], w_v[:, h * KH:(h + 1) * KH, bass.ds(c * NF, NF)]).then_inc(w_in[h], 16)
                load(0, 0)
                load(0, 1)
                ln.load(sp)
                with sp.Fori(1, NCH) as c:
                    for h in range(2):
                        sp.wait_ge(w_used[h], c)
                        load(c, h)
                if y_out is not None:
                    for i in range(TILES):
                        sp.wait_ge(ln.norm_done, i + 1)
                        sp.dma_start(y_out(i), X[0:rows(i), i, :]).then_inc(stored, 16)
                    sp.wait_ge(stored, 16 * TILES)

            @block.tensor
            def _(pe):
                def product(i, k):
                    return nc.tensor.matmul(acc(i), aT[:, k, i * P:i * P + rows(i)], wbuf[:, k, :],
                                            start=(k == 0 and i % 2 == 0), stop=(k == KF - 1), skip_group_check=True)

                def side_by_side(c, first):
                    for h in range(2):
                        pe.wait_ge(w_in[h], c * 16 + 16)
                        for k in range(h * KH, (h + 1) * KH):
                            for i in range(TILES):
                                if k == 0 and i % 2 == 0 and not first:
                                    pe.wait_ge(added, c * TILES + (min(i + 2, TILES) - TILES))
                                last = product(i, k)
                                if k == KF - 1:
                                    last.then_inc(mm_done, 1)
                        if h == 0:
                            last.then_inc(w_used[0], 1)
                    pe.wait_ge(mm_done, c * TILES + TILES)
                    pe.sem_inc(w_used[1], 1)

                side_by_side(0, True)
                with pe.Fori(1, NCH - 1) as c:
                    side_by_side(c, False)

                def transposes(i):
                    pe.wait_ge(ln.norm_done, i + 1)
                    for h in range(2):
                        j, r = 2 * i + h, rows(i)
                        if j >= 2:
                            pe.wait_ge(t_copied, j - 1)
                        for k in range(4):
                            kk = 4 * h + k
                            last = nc.tensor.transpose(ps[:, 6 + j % 2, k * P:k * P + r], X[0:r, i, kk * P:(kk + 1) * P],
                                                       st.ident[0:r, 0:r])
                        last.then_inc(t_done, 1)

                LAG = 2
                c = NCH - 1
                for h in range(2):
                    pe.wait_ge(w_in[h], c * 16 + 16)
                for i in range(TILES):
                    if i < 5:
                        pe.wait_ge(added, (c - 1) * TILES + min(2 * i + 2, TILES))
                    else:
                        pe.wait_ge(added, c * TILES + i - 4)
                    for k in range(KF):
                        last = nc.tensor.matmul(acc_last(i), aT[:, k, i * P:i * P + rows(i)], wbuf[:, k, :],
                                                start=(k == 0), stop=(k == KF - 1))
                    last.then_inc(mm_done, 1)
                    if y_out is None and i >= LAG:
                        transposes(i - LAG)
                if y_out is None:
                    for i in range(TILES - LAG, TILES):
                        transposes(i)

            @block.scalar
            def _(act):
                def copy_t(i):
                    for h in range(2):
                        j, r = 2 * i + h, rows(i)
                        act.wait_ge(t_done, j + 1)
                        nc.scalar.copy(XT[:, 4 * h:4 * h + 4, i * P:i * P + r],
                                       ps[:, 6 + j % 2, :].rearrange("p (k t) -> p k t", k=4)[:, :, 0:r]).then_inc(t_copied, 1)
                for i in range(TILES):
                    ln.act(act, i)
                    if y_out is None and i >= 1:
                        copy_t(i - 1)
                if y_out is None:
                    copy_t(TILES - 1)

            @block.gpsimd
            def _(pool):
                for i in range(TILES):
                    ln.pool(pool, i)

            @block.vector
            def _(dve):
                link = chained(dve, dch)

                def add(c, i, acc):
                    xs = X[0:rows(i), i, bass.ds(c * NF, NF)]
                    nc.vector.scalar_tensor_tensor(out=xs, in0=xs, scalar=ALPHA, in1=acc(i), op0=ALU.mult,
                                                   op1=ALU.add).then_inc(added, 1)
                with dve.Fori(0, NCH - 1) as c:
                    for i in range(TILES):
                        dve.wait_ge(mm_done, c * TILES + min(i // 2 * 2 + 2, TILES))
                        add(c, i, acc)
                for i in range(TILES):
                    dve.wait_ge(mm_done, (NCH - 1) * TILES + i + 1)
                    add(NCH - 1, i, acc_last)
                    dve.wait_ge(added, (NCH - 1) * TILES + i + 1)
                    ln.dve_stats(i, link)
                    if i >= 1:
                        ln.dve_scale(dve, i - 1)
                ln.dve_scale(dve, TILES - 1)
                dve.wait_ge(ln.scaled, TILES)


SQ, SK, SV = 0, 1024, 1280
SCOLS = 1536


def swa_prompt(nc, st, A, C, O, H, XT):
    units = [(m, v) for m in range(2) for v in range(2)]
    NU = len(units)
    with ExitStack() as ctx:
        sb = lambda n, s, d=F32: ctx.enter_context(nc.sbuf_tensor(f"swa_{n}", s, d))
        sem = lambda n: st.sem(f"swa_{n}")
        cs = sb("cos", [P, TILES, 32])
        sn = sb("sin", [P, TILES, 32])
        xc, xs = sb("xc", [P, 20, 2, 32]), sb("xs", [P, 2, 20, 2, 32])
        KT, qT = sb("KT", [P, 2, SEQ]), sb("qT", [P, 8, P])
        band_f, band, identb = sb("bandf", [P, 2 * P]), sb("band", [P, 2 * P], BF16), sb("identb", [P, P], BF16)
        sinks = sb("sinks", [P, 16])
        mx, nm, es, sm, rs = sb("mx", [P, 16]), sb("nm", [P, 16]), sb("es", [P, 16]), sb("sm", [P, 16]), sb("rs", [P, 16])
        Pb, PT = sb("P", [P, 2, 4, 2 * P]), sb("PT", [P, 2, 8, P])
        ps = ctx.enter_context(nc.psum_tensor("swa_ps", [P, 8, 512], F32))
        cin, rot_s, rot_done, dch = sem("const_in"), sem("sin_done"), sem("rotated"), sem("dve_step")
        t_done, t_copied = sem("transposed"), sem("transposed_copied")
        s_done, m_done, e_done, ds_done, es_done = sem("scores"), sem("max"), sem("probs"), sem("sink_diff"), sem("sink_exp")
        pt_done, pt_dve, pt_act, o_done = sem("p_transposed"), sem("p_copied_dve"), sem("p_copied_act"), sem("o")
        y_done, yt_done, yt_copied, stored = sem("y"), sem("yT"), sem("yT_copied"), sem("stored")
        const_ready = sem("const_ready")

        with nc.Block() as block:
            @block.sync
            def _(sp):
                for dst, src in ((cs[:, :, :], C["cos"]), (sn[:, :, :], C["sin"]), (band_f[:, :], C["band"]),
                                 (sinks[:, :], bcast_rows(A["swa_sinks"], 16))):
                    sp.dma_start(dst, src).then_inc(cin, 16)
                sp.wait_ge(rot_done, NT)
                sp.dma_start(O[6][0, 0].rearrange("w k d -> w (k d)"), H[:, NT - 1, SK:SK + 256]).then_inc(stored, 16)
                sp.dma_start(O[7][0, 0].rearrange("w k d -> w (k d)"), H[:, NT - 1, SV:SV + 256]).then_inc(stored, 16)
                sp.wait_ge(stored, 32)

            @block.gpsimd
            def _(pool):
                pool.wait_ge(cin, 64)
                for i in range(TILES):
                    r = rows(i)
                    if i >= 2:
                        pool.wait_ge(rot_done, i - 1)
                    x4 = H[0:r, i, SQ:SV].rearrange("p (h f d) -> p (h f) d", f=2, d=32)
                    nc.gpsimd.tensor_tensor(xs[0:r, i % 2, :, :, :].rearrange("p h f d -> p (h f) d"), x4,
                                            sn[0:r, i:i + 1, :].to_broadcast([r, 40, 32]), ALU.mult).then_inc(rot_s, 1)

            @block.tensor
            def _(pe):
                pe.wait_ge(const_ready, 1)
                for i in range(NT):
                    T = H[:, i, :]
                    w, k0 = (P, P) if i == 0 else (2 * P, 0)
                    c0 = max(i - 1, 0) * P
                    pe.wait_ge(rot_done, i + 1)
                    if i >= 1:
                        pe.wait_ge(yt_copied, 2 * i)
                    for j in range(8):
                        nc.tensor.transpose(ps[:, 4 + j // 4, (j % 4) * P:(j % 4 + 1) * P], T[:, SQ + j * P:SQ + (j + 1) * P],
                                            st.ident[:, :])
                    if i >= 1:
                        pe.wait_ge(y_done, i)
                    for m in range(2):
                        last = nc.tensor.transpose(ps[:, 6, m * P:(m + 1) * P], T[:, SK + m * P:SK + (m + 1) * P], st.ident[:, :])
                    last.then_inc(t_done, 1)
                    pe.wait_ge(t_copied, 3 * (i + 1))

                    def scores(u):
                        m, v = units[u]
                        a, hf = i * NU + u, slice(64 * v, 64 * v + 64)
                        if a >= 2:
                            pe.wait_ge(e_done, a - 1)
                        for b in range(2):
                            o2 = ps[:, 2 * v + b, 0:2 * w]
                            nc.tensor.matmul(o2.rearrange("p (a n) -> p a n", a=2), identb[:, :],
                                             band[:, k0:k0 + w].unsqueeze(1).to_broadcast([P, 2, w]), start=True, stop=False,
                                             skip_group_check=True)
                            for g2 in range(2):
                                last = nc.tensor.matmul(o2[:, g2 * w:(g2 + 1) * w], qT[hf, 4 * m + 2 * b + g2, :],
                                                        KT[hf, m, c0:c0 + w], start=False, stop=True, skip_group_check=True)
                        last.then_inc(s_done, 1)

                    def attend(u):
                        m, v = units[u]
                        a = i * NU + u
                        pe.wait_ge(e_done, a + 1)
                        if a >= 1:
                            pe.wait_ge(pt_dve, a)
                            pe.wait_ge(pt_act, a)
                        nb = w // P
                        for g in range(4):
                            for b in range(nb):
                                last = nc.tensor.transpose(ps[:, 4 + g // 2, ((g % 2) * nb + b) * P:((g % 2) * nb + b + 1) * P],
                                                           Pb[:, a % 2, g, b * P:(b + 1) * P], st.ident[:, :])
                        last.then_inc(pt_done, 1)
                        pe.wait_ge(pt_dve, a + 1)
                        pe.wait_ge(pt_act, a + 1)
                        for g in range(4):
                            h = (2 * m + v) * 4 + g
                            for b in range(nb):
                                last = nc.tensor.matmul(ps[:, 6 + m, (h % 8) * HD:(h % 8 + 1) * HD], PT[:, a % 2, g * nb + b, :],
                                                        H[:, c0 // P + b, SV + (2 * m + v) * HD:SV + (2 * m + v + 1) * HD],
                                                        start=(b == 0), stop=(b == nb - 1))
                        last.then_inc(o_done, 1)

                    scores(0)
                    for u in range(NU):
                        if u + 1 < NU:
                            scores(u + 1)
                        attend(u)
                    pe.wait_ge(y_done, i + 1)
                    for k in range(KD):
                        last = nc.tensor.transpose(ps[:, 4 + k // 4, (k % 4) * P:(k % 4 + 1) * P], T[:, k * P:(k + 1) * P],
                                                   st.ident[:, :])
                        if k % 4 == 3:
                            last.then_inc(yt_done, 1)

            @block.scalar
            def _(act):
                for i in range(NT):
                    nb = 1 if i == 0 else 2
                    act.wait_ge(t_done, i + 1)
                    for j in range(2):
                        nc.scalar.copy(qT[:, 4 * j:4 * j + 4, :], ps[:, 4 + j, :].rearrange("p (a t) -> p a t", a=4)).then_inc(t_copied, 1)
                    nc.scalar.copy(KT[:, :, i * P:(i + 1) * P], ps[:, 6, 0:2 * P].rearrange("p (a t) -> p a t", a=2)).then_inc(t_copied, 1)

                    def exps(u):
                        m, v = units[u]
                        a = i * NU + u
                        act.wait_ge(m_done, a + 1)
                        if a >= 2:
                            act.wait_ge(pt_done, a - 1)
                        for g in range(4):
                            h = 4 * (2 * m + v) + g
                            w = nb * P
                            ins = nc.scalar.activation(Pb[:, a % 2, g, 0:w], ps[:, 2 * v + g // 2, (g % 2) * w:(g % 2 + 1) * w],
                                                       ACT.Exp, bias=nm[:, h:h + 1], scale=AS, accum_out=sm[:, h:h + 1])
                        ins.then_inc(e_done, 1)

                    def copy_pt(u):
                        a = i * NU + u
                        if a >= 2:
                            act.wait_ge(o_done, a - 1)
                        act.wait_ge(pt_done, a + 1)
                        nc.scalar.copy(PT[:, a % 2, 2 * nb:4 * nb, :],
                                       ps[:, 5, 0:2 * nb * P].rearrange("p (a t) -> p a t", t=P)).then_inc(pt_act, 1)

                    exps(0)
                    for u in range(NU):
                        if u + 1 < NU:
                            exps(u + 1)
                        copy_pt(u)
                    act.wait_ge(ds_done, i + 1)
                    nc.scalar.activation(es[:, :], es[:, :], ACT.Exp).then_inc(es_done, 1)
                    for k in range(2):
                        act.wait_ge(yt_done, 2 * i + k + 1)
                        nc.scalar.copy(XT[:, 4 * k:4 * k + 4, i * P:(i + 1) * P],
                                       ps[:, 4 + k, :].rearrange("p (a t) -> p a t", a=4)).then_inc(yt_copied, 1)

            @block.vector
            def _(dve):
                link = chained(dve, dch)
                dve.wait_ge(cin, 64)
                link(nc.vector.tensor_copy(identb[:, :], st.ident[:, :]))
                link(nc.vector.tensor_copy(band[:, :], band_f[:, :]))
                dve.sem_inc(const_ready, 1)

                def rotate(i):
                    r = rows(i)
                    x3 = H[0:r, i, SQ:SV].rearrange("p (h f d) -> p h f d", f=2, d=32)
                    link(nc.vector.tensor_tensor(xc[0:r, :, :, :].rearrange("p h f d -> p (h f) d"),
                                                 H[0:r, i, SQ:SV].rearrange("p (h d) -> p h d", d=32),
                                                 cs[0:r, i:i + 1, :].to_broadcast([r, 40, 32]), ALU.mult))
                    dve.wait_ge(rot_s, i + 1)
                    s5 = xs[0:r, i % 2, :, :, :]
                    link(nc.vector.tensor_tensor(x3[:, :, 0, :], xc[0:r, :, 0, :], s5[:, :, 1, :], ALU.subtract))
                    nc.vector.tensor_tensor(x3[:, :, 1, :], xc[0:r, :, 1, :], s5[:, :, 0, :], ALU.add).then_inc(rot_done, 1)
                    dve.wait_ge(rot_done, i + 1)

                rotate(0)
                for i in range(NT):
                    nb = 1 if i == 0 else 2
                    w = nb * P
                    rotate(i + 1)

                    def row_max(u):
                        m, v = units[u]
                        a, h0 = i * NU + u, 4 * (2 * m + v)
                        h4 = slice(h0, h0 + 4)
                        dve.wait_ge(s_done, a + 1)
                        if nb == 2:
                            link(nc.vector.reduce_max(mx[:, h4], ps[:, 2 * v:2 * v + 2, :].rearrange("p b (g n) -> p (b g) n", g=2), AX_X))
                        else:
                            for b in range(2):
                                link(nc.vector.reduce_max(mx[:, h0 + 2 * b:h0 + 2 * b + 2],
                                                          ps[:, 2 * v + b, 0:2 * w].rearrange("p (g n) -> p g n", g=2), AX_X))
                        link(nc.vector.scalar_tensor_tensor(out=mx[:, h4], in0=mx[:, h4], scalar=AS, in1=sinks[:, h4],
                                                            op0=ALU.mult, op1=ALU.max))
                        nc.vector.tensor_scalar(nm[:, h4], mx[:, h4], -1.0, None, ALU.mult).then_inc(m_done, 1)

                    def copy_pt(u):
                        a = i * NU + u
                        if a >= 2:
                            dve.wait_ge(o_done, a - 1)
                        dve.wait_ge(pt_done, a + 1)
                        nc.vector.tensor_copy(PT[:, a % 2, 0:2 * nb, :],
                                              ps[:, 4, 0:2 * nb * P].rearrange("p (a t) -> p a t", t=P)).then_inc(pt_dve, 1)

                    if i >= 1:
                        dve.wait_ge(e_done, i * NU)
                        dve.wait_ge(y_done, i)
                    row_max(0)
                    for u in range(NU):
                        if u + 1 < NU:
                            row_max(u + 1)
                        copy_pt(u)
                    nc.vector.tensor_tensor(es[:, :], sinks[:, :], mx[:, :], ALU.subtract).then_inc(ds_done, 1)
                    dve.wait_ge(es_done, i + 1)
                    dve.wait_ge(e_done, (i + 1) * NU)
                    link(nc.vector.tensor_tensor(rs[:, :], sm[:, :], es[:, :], ALU.add))
                    link(nc.vector.reciprocal(rs[:, :], rs[:, :]))
                    dve.wait_ge(o_done, (i + 1) * NU)
                    for m in range(2):
                        ins = nc.vector.tensor_tensor(
                            H[:, i, SQ + 512 * m:SQ + 512 * m + 512].rearrange("p (h d) -> p h d", d=HD),
                            ps[:, 6 + m, :].rearrange("p (h d) -> p h d", d=HD),
                            rs[:, 8 * m:8 * m + 8].unsqueeze(2).to_broadcast([P, 8, HD]), ALU.mult)
                    ins.then_inc(y_done, 1)
                dve.wait_ge(y_done, NT)


def swa_sample(nc, st, A, C, O, H, XT):
    NB, NK = DEC_BATCH, P + DEC_SEQ
    scr = nc.dram_tensor("scratch_ys", (NS, D), F32, kind="Internal").ap()
    T = H[:, NT, :]
    with ExitStack() as ctx:
        sb = lambda n, s, d=F32: ctx.enter_context(nc.sbuf_tensor(f"sws_{n}", s, d))
        sem = lambda n: st.sem(f"sws_{n}")
        Kb, Vb, Vn = sb("Kb", [P, NB, 256]), sb("Vb", [P, NB, 256]), sb("Vn", [DEC_SEQ, NB, 256])
        KT, kn = sb("KT", [P, NB, 2, NK]), sb("kn", [P, 2, NS])
        qz = sb("qz", [P, NB, 2, 2, 4, DEC_SEQ])
        band_f, band, identb = sb("bandf", [P, NK]), sb("band", [P, NK], BF16), sb("identb", [P, P], BF16)
        sink = sb("sink", [P, 1])
        mx, nm, es, sm, rs = (sb(n, [P, NB]) for n in ("mx", "nm", "es", "sm", "rs"))
        Pb, PT = sb("P", [P, NB, NK]), sb("PT", [P, NB, P])
        PTn = sb("PTn", [DEC_SEQ, NB, P])
        yq, Y = sb("yq", [P, NB, HD]), sb("Y", [NS, D])
        ps = ctx.enter_context(nc.psum_tensor("sws_ps", [P, 8, 512], F32))
        buf_in, cin, vn_in, ready, dch = sem("buffers_in"), sem("const_in"), sem("v_new_in"), sem("ready"), sem("dve_step")
        q_done, q_copied, k_done, k_copied = sem("qT"), sem("qT_copied"), sem("kT"), sem("kT_copied")
        s_done, m_done, e_done, pt_done, pt_copied = sem("scores"), sem("max"), sem("probs"), sem("pT"), sem("pT_copied")
        o_done, y_done, y_out, y_in, yt_done, yt_copied, stored = (sem("o"), sem("y"), sem("y_out"), sem("y_in"), sem("yT"),
                                                                   sem("yT_copied"), sem("stored"))

        def score(b, n=NK):
            return ps[:, b // 3, (b % 3) * NK:(b % 3) * NK + n]

        with nc.Block() as block:
            @block.sync
            def _(sp):
                sp.dma_start(Kb[:, :, :], A["state_swa_k"][0].rearrange("b w k d -> w b (k d)")).then_inc(buf_in, 16)
                sp.dma_start(Vb[:, :, :], A["state_swa_v"][0].rearrange("b w k d -> w b (k d)")).then_inc(buf_in, 16)
                sp.dma_start(band_f[:, :], C["bands"]).then_inc(cin, 16)
                sp.dma_start(sink[:, :], bass.AP(A["swa_sinks"].tensor, 0, [[1, 16], [0, DEC_SEQ], [1, 1]]),
                             allow_slow_non_contiguous=True).then_inc(cin, 16)
                for b in range(NB):
                    sp.dma_start(Vn[:, b, :], T[8 * b:8 * b + 8, SV:SV + 256]).then_inc(vn_in, 16)
                for o, src, c in ((O[12], A["state_swa_k"], SK), (O[13], A["state_swa_v"], SV)):
                    sp.dma_start(o[0, :, 0:P - DEC_SEQ].rearrange("b w k d -> b (w k d)"),
                                 src[0, :, DEC_SEQ:P].rearrange("b w k d -> b (w k d)")).then_inc(stored, 16)
                    for b in range(NB):
                        sp.dma_start(o[0, b, P - DEC_SEQ:P].rearrange("w k d -> w (k d)"), T[8 * b:8 * b + 8, c:c + 256]).then_inc(stored, 16)
                sp.wait_ge(y_done, 1)
                for b in range(NB):
                    sp.dma_start(bass.AP(scr.tensor, b * DEC_SEQ * D, [[HD, 16], [D, DEC_SEQ], [1, HD]]), yq[:, b, :]).then_inc(y_out, 16)
                sp.wait_ge(y_out, 16 * NB)
                sp.dma_start(Y[:, :], scr).then_inc(y_in, 16)
                sp.wait_ge(stored, 32 + 32 * NB)

            @block.tensor
            def _(pe):
                I64 = st.ident[0:NS, 0:NS]
                for j in range(8):
                    nc.tensor.transpose(ps[:, 3, j * NS:(j + 1) * NS], T[0:NS, SQ + j * P:SQ + (j + 1) * P], I64)
                for m in range(2):
                    last = nc.tensor.transpose(ps[:, 4, m * NS:(m + 1) * NS], T[0:NS, SK + m * P:SK + (m + 1) * P], I64)
                last.then_inc(q_done, 1)
                pe.wait_ge(buf_in, 32)
                for b in range(0, NB, 2):
                    g = b // 2
                    if g >= 2:
                        pe.wait_ge(k_copied, g - 1)
                    for j in range(4):
                        last = nc.tensor.transpose(ps[:, 6 + g % 2, j * P:(j + 1) * P],
                                                   Kb[:, b + j // 2, (j % 2) * P:(j % 2 + 1) * P], st.ident[:, :])
                    last.then_inc(k_done, 1)
                pe.wait_ge(k_copied, NB // 2 + 1)
                pe.wait_ge(q_copied, 3)
                pe.wait_ge(ready, 1)
                for b in range(NB):
                    nc.tensor.matmul(score(b), identb[:, :], band[:, :], start=True, stop=False, skip_group_check=True)
                    for m in range(2):
                        last = nc.tensor.matmul(score(b)[64 * m:64 * m + 64, :],
                                                qz[:, b, m, :, :, :].rearrange("d v g q -> d (v g q)"), KT[:, b, m, :],
                                                start=False, stop=True, skip_group_check=True)
                last.then_inc(s_done, 1)
                pe.wait_ge(e_done, 1)
                for b in range(NB):
                    nc.tensor.transpose(ps[:, 3 + b // 4, (b % 4) * P:(b % 4 + 1) * P], Pb[:, b, 0:P], st.ident[:, :])
                for b in range(NB):
                    last = nc.tensor.transpose(ps[0:DEC_SEQ, 6 + b // 4, (b % 4) * P:(b % 4 + 1) * P], Pb[:, b, P:NK], st.ident[:, :])
                last.then_inc(pt_done, 1)
                pe.wait_ge(pt_copied, 2)
                pe.wait_ge(vn_in, 16 * NB)
                for b in range(NB):
                    for m in range(2):
                        r = slice(64 * m, 64 * m + 64)
                        o = ps[r, b // 4, (b % 4) * P:(b % 4 + 1) * P]
                        nc.tensor.matmul(o, PT[:, b, r], Vb[:, b, m * P:(m + 1) * P], start=True, stop=False)
                        last = nc.tensor.matmul(o, PTn[:, b, r], Vn[:, b, m * P:(m + 1) * P], start=False, stop=True)
                last.then_inc(o_done, 1)
                pe.wait_ge(y_in, 16)
                for k in range(KD):
                    last = nc.tensor.transpose(ps[:, 5, k * NS:(k + 1) * NS], Y[:, k * P:(k + 1) * P], I64)
                last.then_inc(yt_done, 1)

            @block.scalar
            def _(act):
                act.wait_ge(q_done, 1)
                act.wait_ge(ready, 1)
                for v in range(2):
                    hf = slice(64 * v, 64 * v + 64)
                    for m in range(2):
                        ins = nc.scalar.copy(qz[hf, :, m, v, :, :].rearrange("d b g q -> d g b q"),
                                             ps[hf, 3, 4 * m * NS:4 * (m + 1) * NS].rearrange("d (g b q) -> d g b q", g=4, b=NB))
                    ins.then_inc(q_copied, 1)
                nc.scalar.copy(kn[:, :, :], ps[:, 4, 0:2 * NS].rearrange("p (m t) -> p m t", m=2)).then_inc(q_copied, 1)
                act.wait_ge(q_copied, 3)
                for m in range(2):
                    ins = nc.scalar.copy(KT[:, :, m, P:NK], kn[:, m, :].rearrange("p (b q) -> p b q", b=NB))
                for g in range(NB // 2):
                    act.wait_ge(k_done, g + 1)
                    ins = nc.scalar.copy(KT[:, 2 * g:2 * g + 2, :, 0:P],
                                         ps[:, 6 + g % 2, :].rearrange("p (b m t) -> p b m t", b=2, m=2))
                    ins.then_inc(k_copied, 1)
                act.wait_ge(k_copied, NB // 2)
                act.sem_inc(k_copied, 1)
                act.wait_ge(m_done, 1)
                nc.scalar.activation(es[:, :], es[:, :], ACT.Exp)
                for b in range(NB):
                    ins = nc.scalar.activation(Pb[:, b, :], score(b), ACT.Exp, bias=nm[:, b:b + 1], scale=AS,
                                               accum_out=sm[:, b:b + 1])
                ins.then_inc(e_done, 1)
                act.wait_ge(pt_done, 1)
                nc.scalar.copy(PTn[:, :, :], ps[0:DEC_SEQ, 6:8, :].rearrange("p c (b t) -> p (c b) t", b=4)).then_inc(pt_copied, 1)
                act.wait_ge(yt_done, 1)
                nc.scalar.copy(XT[:, :, SEQ:NTOK], ps[:, 5, :].rearrange("p (k t) -> p k t", k=KD)).then_inc(yt_copied, 1)
                act.wait_ge(yt_copied, 1)

            @block.vector
            def _(dve):
                link = chained(dve, dch)
                link(nc.vector.memset(qz[:, :, :, :, :, :], 0.0))
                link(nc.vector.tensor_copy(identb[:, :], st.ident[:, :]))
                dve.wait_ge(cin, 32)
                nc.vector.tensor_copy(band[:, :], band_f[:, :]).then_inc(ready, 1)
                dve.wait_ge(s_done, 1)
                for c in range(3):
                    n = 3 if c < 2 else 2
                    link(nc.vector.reduce_max(mx[:, 3 * c:3 * c + n],
                                              ps[:, c, 0:n * NK].rearrange("p (b n) -> p b n", n=NK), AX_X))
                link(nc.vector.tensor_scalar(mx[:, :], mx[:, :], AS, sink[:, 0:1], ALU.mult, ALU.max))
                link(nc.vector.tensor_scalar(nm[:, :], mx[:, :], -1.0, None, ALU.mult))
                nc.vector.tensor_scalar(es[:, :], nm[:, :], sink[:, 0:1], None, ALU.add).then_inc(m_done, 1)
                dve.wait_ge(pt_done, 1)
                nc.vector.tensor_copy(PT[:, :, :], ps[:, 3:5, :].rearrange("p c (b t) -> p (c b) t", b=4)).then_inc(pt_copied, 1)
                dve.wait_ge(e_done, 1)
                link(nc.vector.tensor_tensor(rs[:, :], sm[:, :], es[:, :], ALU.add))
                link(nc.vector.reciprocal(rs[:, :], rs[:, :]))
                dve.wait_ge(o_done, 1)
                for kv in range(4):
                    r, v = slice(32 * kv, 32 * kv + 32), kv % 2
                    ins = nc.vector.tensor_tensor(
                        yq[r, :, :], ps[r, 0:2, :].rearrange("p c (b d) -> p (c b) d", b=4)[:, :, v * HD:(v + 1) * HD],
                        rs[r, :].unsqueeze(2).to_broadcast([32, NB, HD]), ALU.mult)
                ins.then_inc(y_done, 1)


def rest(nc, st, A, C, O, XT, x_rows):
    def y_rows(i):
        if i < NT:
            return O[0][0, i * P:(i + 1) * P, :]
        return O[1].rearrange("b s d -> (b s) d")

    with ExitStack() as ctx:
        X = ctx.enter_context(nc.sbuf_tensor("X", [P, TILES, D], F32))
        out_projection(nc, st, A, A["w_out_even"][0], 0, XT, X, x_rows)
        ffn(nc, st, A, 0, XT, X, None)
        st.end_phase()
        with ExitStack() as mix:
            H = mix.enter_context(nc.sbuf_tensor("H1", [P, TILES, SCOLS], F32))
            in_projection(nc, st, None, A["w_in_odd"][0], ODD_CHUNKS, XT, lambda i: H[:, i, :], [], "ino", False)
            swa_prompt(nc, st, A, C, O, H, XT)
            swa_sample(nc, st, A, C, O, H, XT)
            st.end_phase()
        out_projection(nc, st, A, A["w_out_odd"][0], 1, XT, X, None)
        ffn(nc, st, A, 1, XT, X, y_rows)
        st.end_phase()
class State:

    def __init__(self, nc, ctx):
        self.nc, self.ctx = nc, ctx

        self.phase_sems = []

    def sem(self, name):
        s = self.nc.alloc_semaphore(name=name)
        self.phase_sems.append(s)
        return s

    def end_phase(self):
        self.nc.clear_and_free_semaphores(self.phase_sems)
        self.nc.all_engine_barrier()
        self.phase_sems = []

    def sbuf(self, name, shape, dt=F32):
        return self.ctx.enter_context(self.nc.sbuf_tensor(name, shape, dt))



def build(nc, A, C, O):
    with ExitStack() as ctx:
        st = State(nc, ctx)
        st.ident = st.sbuf("ident", [P, P])
        s_c = st.sem("const_in")
        with nc.Block() as block:
            @block.sync
            def _(sp):
                sp.dma_start(st.ident[:, :], C["ident"]).then_inc(s_c, 16)
                sp.wait_ge(s_c, 16)
        XT = st.sbuf("XT", [P, KD, NTOK])

        def x_rows(i):
            if i < NT:
                return A["x_prompt"][0, i * P:(i + 1) * P, :]
            return A["x_sample"].rearrange("b s d -> (b s) d")

        with ExitStack() as mix:
            Hs = mix.enter_context(nc.sbuf_tensor("Hs", [P, C_END], F32))
            with ExitStack() as mixp:
                H = mixp.enter_context(nc.sbuf_tensor("H", [P, NT, C_END], F32))
                stores = []
                for out_p, out_s, a, b in ((O[2], O[8], C_DK, C_DV), (O[3], O[9], C_DV, C_IK), (O[4], O[10], C_IK, C_IK + HD)):
                    fl = "o b t k d -> (o b t) (k d)" if len(out_p.shape) == 5 else "o b t d -> (o b t) d"
                    stores.append((out_p.rearrange(fl).rearrange("(i p) c -> p i c", p=P), H[:, :, a:b]))
                    stores.append((out_s.rearrange(fl), Hs[0:NS, a:b]))
                in_projection(nc, st, x_rows, A["w_in_even"][0], EVEN_CHUNKS, XT,
                              lambda i: H[:, i, :] if i < NT else Hs[:, :], stores, "ine", True)
                st.end_phase()
                gla(nc, st, A, C, O, H, Hs)
                st.end_phase()
                dsa_prompt(nc, st, A, C, O, H, Hs, XT)
            st.end_phase()
            dsa_sample(nc, st, A, C, O, Hs, XT)
            st.end_phase()
        rest(nc, st, A, C, O, XT, x_rows)


_INS = ["x_prompt", "x_sample", "cache_k", "cache_v", "cache_idx", "state_gla", "state_swa_k", "state_swa_v",
        "page_table", "w_in_even", "gla_gate_w2", "gla_gate_b", "gla_norm_g", "w_out_even", "w_in_odd", "swa_sinks",
        "w_out_odd", "ffn_w_gu", "ffn_w_down", "ln_g", "ln_b"]
_OUTS = [(1, 1024, 1024), (8, 8, 1024), (1, 1, 1024, 2, 64), (1, 1, 1024, 2, 64), (1, 1, 1024, 64), (1, 1, 4, 64, 128),
         (1, 1, 128, 4, 64), (1, 1, 128, 4, 64), (1, 8, 8, 2, 64), (1, 8, 8, 2, 64), (1, 8, 8, 64), (1, 8, 4, 64, 128),
         (1, 8, 128, 4, 64), (1, 8, 128, 4, 64)]


def shape_constants():
    import numpy as np
    c = {"ident": np.eye(128, dtype=np.float32)}
    s, t = np.arange(128)[:, None], np.arange(128)[None, :]
    lev = [(s == t)]
    for n in range(7):
        L = 2 ** n
        lev.append((s // (2 * L) == t // (2 * L)) & (s // L % 2 == 0) & (t // L % 2 == 1))
    c["levels"] = np.stack(lev, 1).astype(np.float32)
    reset = np.ones((128, 192), np.float32)
    reset[:, 128:192:8] = 0.0
    c["reset"] = reset
    c["batchsel"] = (np.arange(64)[:, None] // 8 == np.arange(8)[None, :]).astype(np.float32)
    c["causal"] = np.where(t <= s, 0.0, -1e30).astype(np.float32)
    qi, ki = np.arange(64)[:, None], np.arange(8)[None, :]
    c["causal8"] = np.where(ki <= qi % 8, 0.0, -1e30).astype(np.float32)
    sp = np.zeros((64, 4, 128), np.float32)
    for pair in range(4):
        for r in range(128):
            sp[(2 * pair + r // 64) * 8 + r % 8, pair, r] = 1.0
    c["spread"] = sp
    gat = np.zeros((64, 8, 64), np.float32)
    for b in range(8):
        for r in range(64):
            gat[r, b, b * 8 + r % 8] = 1.0
    c["gather"] = gat
    a, k2 = np.arange(128)[:, None], np.arange(256)[None, :]
    c["band"] = np.where((k2 > a) & (k2 <= a + 128), 0.0, -1e30).astype(np.float32)
    q8, k136 = (np.arange(128) % 8)[:, None], np.arange(136)[None, :]
    c["bands"] = np.where((k136 > q8) & (k136 <= q8 + 128), 0.0, -1e30).astype(np.float32)
    pos = np.concatenate([np.arange(1024), 2048 + np.arange(64) % 8, np.zeros(64)]).astype(np.float32)
    inv = (np.float32(150000.0) ** (-np.arange(32, dtype=np.float32) / np.float32(32))).astype(np.float32)
    ang = pos[:, None] * inv[None, :]
    c["cos"] = np.cos(ang).astype(np.float32).reshape(9, 128, 32).transpose(1, 0, 2)
    c["sin"] = np.sin(ang).astype(np.float32).reshape(9, 128, 32).transpose(1, 0, 2)
    return c


def kernel(**inputs):
    import numpy as _np
    import concourse.bacc as _bacc
    from concourse import mybir as _mybir
    from concourse.bass_utils import run_bass_kernel_spmd as _run

    nc = _bacc.Bacc("TRN2", target_bir_lowering=False, num_devices=1)
    arrays, A, C, O = {}, {}, {}, []
    for name in _INS:
        a = _np.ascontiguousarray(inputs[name])
        arrays[f"in_{name}_dram"] = a
        A[name] = nc.dram_tensor(f"in_{name}_dram", a.shape, _mybir.dt.from_np(a.dtype), kind="ExternalInput").ap()
    for name, a in shape_constants().items():
        a = _np.ascontiguousarray(a)
        arrays[f"const_{name}"] = a
        C[name] = nc.dram_tensor(f"const_{name}", a.shape, _mybir.dt.from_np(a.dtype), kind="ExternalInput").ap()
    for i, shape in enumerate(_OUTS):
        O.append(nc.dram_tensor(f"out_{i}_dram", shape, F32, kind="ExternalOutput").ap())
    build(nc, A, C, O)
    r = _run(nc, [arrays], core_ids=[0])
    return tuple(r.results[0][f"out_{i}_dram"] for i in range(len(_OUTS)))
```

```python
from contextlib import ExitStack
import math

import concourse.bass as bass
from concourse import mybir

ALU = mybir.AluOpType
ACT = mybir.ActivationFunctionType
AX_X = mybir.AxisListType.X
F32 = mybir.dt.float32
F32R = mybir.dt.float32r
BF16 = mybir.dt.bfloat16
I32 = mybir.dt.int32
U8 = mybir.dt.uint8

P = 128
D = 1024
KD = D // P
SEQ, DEC_BATCH, DEC_SEQ = 1024, 8, 8
NS = DEC_BATCH * DEC_SEQ
NT = SEQ // P
NTOK = SEQ + NS
TILES = NT + 1
ALPHA = 4.0 ** 0.25
LN_EPS, RMS_EPS = 1e-5, 1e-6
GLA_H, DK, DV, TAU = 4, 64, 128, 16.0
HD = 64
W_GQ, W_GK, W_GV, W_GR, W_GG, W_DQ, W_DK, W_DV, W_IQ, W_IK, W_IW, W_END = (
    0, 256, 512, 1024, 1536, 1552, 2064, 2192, 2320, 2832, 2896, 2904)
C_GQ, C_GK, C_GV, C_GR, C_DQ, C_IQ, C_GG, C_DK, C_DV, C_IK, C_IW, C_END = (
    0, 256, 512, 1024, 1536, 2048, 2560, 2576, 2704, 2832, 2960, 2968)
D_FF = 2816
KF = D_FF // P

def rows(i):
    return P if i < NT else NS

def bcast_rows(ap1d, n, parts=P):
    return bass.AP(ap1d.tensor, ap1d.offset, [[0, parts], [1, n]])

def by_group(start):
    return [((g * 2 + kv) * HD, start + (kv * 4 + g) * HD, HD) for g in range(4) for kv in range(2)]

EVEN_CHUNKS = [[(0, W_GQ, 512)], [(0, W_GV, 512)], [(0, W_GR, 512)], by_group(W_DQ), [(0, W_IQ, 512)],
               [(0, W_GG, 16), (C_DK - C_GG, W_DK, 256), (C_IK - C_GG, W_IK, 64), (C_IK + 64 - C_GG, W_IK, 72)]]
ODD_CHUNKS = [by_group(0), by_group(512), [(0, 1024, 512)]]

def in_projection(nc, st, x_tile, w, chunks, XT, dest, stores, tag, load_x):
    SLOTS = 2
    NCH = len(chunks)
    ncols = 512 * (NCH - 1) + max(a + n for a, _, n in chunks[-1])
    landed = [16 * sum(len(chunks[d]) for d in range(c % SLOTS, c + 1, SLOTS)) for c in range(NCH)]
    w_v = w.rearrange("(k p) n -> p k n", p=P)
    with ExitStack() as ctx:
        sb = lambda n, s, d=F32: ctx.enter_context(nc.sbuf_tensor(f"{tag}_{n}", s, d))
        sem = lambda n: st.sem(f"{tag}_{n}")
        wbuf = sb("w", [P, SLOTS, KD, 512])
        ps = ctx.enter_context(nc.psum_tensor(f"{tag}_ps", [P, 8, 512], F32))
        w_in = [sem(f"w_in{k}") for k in range(SLOTS)]
        mm_done, act_evac, dve_evac = sem("mm_done"), sem("act_evac"), sem("dve_evac")
        stored = sem("stored")
        if load_x:
            xbuf = sb("x", [P, 2, D])
            x_in = [sem(f"x_in{k}") for k in range(2)]
            t_done, t_evac = sem("t_done"), sem("t_evac")

        with nc.Block() as block:
            @block.sync
            def _(sp):
                def load_w(c):
                    if c >= SLOTS:
                        sp.wait_ge(mm_done, (c - SLOTS + 1) * TILES)
                    for a, b, n in chunks[c]:
                        sp.dma_start(wbuf[:, c % SLOTS, :, a:a + n], w_v[:, :, b:b + n]).then_inc(w_in[c % SLOTS], 16)
                if load_x:
                    for i in range(TILES):
                        if i >= 2:
                            sp.wait_ge(t_done, 2 * (i - 1))
                        sp.dma_start(xbuf[0:rows(i), i % 2, :], x_tile(i)).then_inc(x_in[i % 2], 16)
                        if i == 0:
                            load_w(0)
                    load_w(1)
                else:
                    load_w(0)
                    load_w(1)
                for c in range(SLOTS, NCH):
                    load_w(c)

            @block.tensor
            def _(pe):
                if load_x:
                    for i in range(TILES):
                        r = rows(i)
                        pe.wait_ge(x_in[i % 2], 16 * (i // 2 + 1))
                        for h in range(2):
                            j = 2 * i + h
                            if j >= 8:
                                pe.wait_ge(t_evac, j - 7)
                            for k in range(4):
                                kk = 4 * h + k
                                last = nc.tensor.transpose(ps[:, j % 8, k * P:k * P + r],
                                                           xbuf[0:r, i % 2, kk * P:(kk + 1) * P], st.ident[0:r, 0:r])
                            last.then_inc(t_done, 1)
                    pe.wait_ge(t_evac, 2 * TILES)
                for c in range(NCH):
                    n = min(512, ncols - 512 * c)
                    pe.wait_ge(w_in[c % SLOTS], landed[c])
                    for i in range(TILES):
                        s, r = c * TILES + i, rows(i)
                        if s >= 8:
                            pe.wait_ge(act_evac if s % 2 == 0 else dve_evac, (s - 8) // 2 + 1)
                        for k in range(KD):
                            last = nc.tensor.matmul(ps[0:r, s % 8, 0:n], XT[:, k, i * P:i * P + r],
                                                    wbuf[:, c % SLOTS, k, 0:n], start=(k == 0), stop=(k == KD - 1))
                        last.then_inc(mm_done, 1)

            def copy_out(eng, op, parity, done):
                for c in range(NCH):
                    n = min(512, ncols - 512 * c)
                    for i in range(TILES):
                        s, r = c * TILES + i, rows(i)
                        if s % 2 == parity:
                            eng.wait_ge(mm_done, s + 1)
                            op(dest(i)[0:r, 512 * c:512 * c + n], ps[0:r, s % 8, 0:n]).then_inc(done, 1)

            @block.scalar
            def _(act):
                if load_x:
                    for i in range(TILES):
                        for h in range(2):
                            j = 2 * i + h
                            act.wait_ge(t_done, j + 1)
                            nc.scalar.copy(XT[:, 4 * h:4 * h + 4, i * P:i * P + rows(i)],
                                           ps[:, j % 8, :].rearrange("p (k t) -> p k t", k=4)[:, :, 0:rows(i)]).then_inc(t_evac, 1)
                copy_out(act, nc.scalar.copy, 0, act_evac)

            @block.vector
            def _(dve):
                copy_out(dve, nc.vector.tensor_copy, 1, dve_evac)

            @block.gpsimd
            def _(pool):
                total = NCH * TILES
                pool.wait_ge(act_evac, (total + 1) // 2)
                pool.wait_ge(dve_evac, total // 2)
                n = 0
                for out_ap, src in stores:
                    pool.dma_start(out_ap, src).then_inc(stored, 16)
                    n += 1
                if n:
                    pool.wait_ge(stored, 16 * n)



def chained(eng, sem):
    count = [0]

    def link(ins):
        count[0] += 1
        ins.then_inc(sem, 1)
        eng.wait_ge(sem, count[0])
    return link


def gla(nc, st, A, C, O, H, Hs):
    NL = 8
    with ExitStack() as ctx:
        sb = lambda n, s, d=F32: ctx.enter_context(nc.sbuf_tensor(f"gla_{n}", s, d))
        sem = lambda n: st.sem(f"gla_{n}")
        w2, gb, ng = sb("w2", [16, 256]), sb("gb", [P, 2]), sb("ng", [P, DV])
        lev_f, lev = sb("levf", [P, NL, P]), sb("lev", [P, NL, P], U8)
        reset, bsel = sb("reset", [P, 192]), sb("bsel", [NS, 8])
        S = sb("S", [P, 2, DV])
        SS = sb("SS", [P, DEC_BATCH, 2, DV])
        qT, kT = sb("qT", [P, 2, 2, P]), sb("kT", [P, 2, 2, P])
        ggT = sb("ggT", [16, P])
        z, az, cs = sb("z", [P, 2, P]), sb("az", [P, 2, P]), sb("cs", [P, 2, P])
        EE = sb("E", [P, 2, NL + 1, 2, P])
        QM = sb("QM", [P, NL, 2, P])
        decs = sb("dec", [P, 2, 2, 8])
        A_sb = sb("A", [P, 2, 2, P])
        qin, kin, kinT = sb("qin", [P, 2, P]), sb("kin", [P, 2, P]), sb("kinT", [P, 2, P])
        oT = sb("oT", [P, 2, 2, NS])
        ssq, rs = sb("ssq", [P, 4]), sb("rs", [P, 4])
        junk = sb("junk", [P, DV])
        ps = ctx.enter_context(nc.psum_tensor("gla_ps", [P, 8, 512], F32))
        tr, misc, gg_ps = ps[:, 0, :], ps[:, 1, :], ps[:, 7, :]
        o_ps = [ps[:, 7, :], ps[:, 2, :]]
        ot_ps = [ps[:, 0, :], ps[:, 1, :]]

        def o_of(h, r):
            return o_ps[h % 2][0:r, (h // 2) * DV:(h // 2 + 1) * DV]

        cin, cst = sem("const_in"), sem("const_ready")
        t_done, t_act, g_dve = sem("qk_transposed"), sem("qk_copied"), sem("gg_copied")
        z_biased = sem("z_biased")
        z_done, az_done, ln_done = sem("z_done"), sem("az_done"), sem("ln_done")
        d_done, e_done, qk_done = sem("diff_done"), sem("exp_done"), sem("scaled_done")
        lev_done, lev_used = sem("level_done"), sem("level_used")
        kt_done, kt_act = sem("kin_transposed"), sem("kin_copied")
        o_done, ot_done, ot_act = sem("o_done"), sem("oT_done"), sem("oT_copied")
        kv_done, kv_used = sem("kv_done"), sem("kv_used")
        sq_done, ms_done, rs_done, y_done = sem("sq_done"), sem("ms_done"), sem("rs_done"), sem("y_done")
        silu_done, gate_done = sem("silu_done"), sem("gate_done")
        dch, ach, pch, kb_done = sem("dve_step"), sem("act_step"), sem("pool_step"), sem("kin_masked")
        s_out = sem("state_out")
        kinTb = QM

        def tile_of(i):
            return H[:, i, :] if i < NT else Hs[:, :]

        def lv(i):
            return NL if i < NT else 4

        lev0 = [0]
        for i in range(TILES):
            lev0.append(lev0[-1] + lv(i))
        half = lambda h: slice(64 * (h % 2), 64 * (h % 2) + 64)

        with nc.Block() as block:
            @block.sync
            def _(sp):
                for dst, src in ((w2[:, :], A["gla_gate_w2"][0]),
                                 (ng[:, :], bcast_rows(A["gla_norm_g"], DV)), (lev_f[:, :, :], C["levels"]),
                                 (reset[:, :], C["reset"]), (bsel[:, :], C["batchsel"])):
                    sp.dma_start(dst, src).then_inc(cin, 16)
                sp.dma_start(gb[:, :], A["gla_gate_b"].rearrange("o (c p) -> p (o c)", p=P),
                             allow_slow_non_contiguous=True).then_inc(cin, 16)
                for hf in range(2):
                    sp.dma_start(SS[64 * hf:64 * hf + 64, :, :, :],
                                 A["state_gla"][0].rearrange("b (r f) d v -> f d b r v", f=2)[hf]).then_inc(cin, 16)
                sp.wait_ge(kv_used, NT)
                for hf in range(2):
                    sp.dma_start(O[5][0, 0].rearrange("(r f) d v -> f d r v", f=2)[hf],
                                 S[64 * hf:64 * hf + 64, :, :]).then_inc(s_out, 16)
                sp.wait_ge(kv_used, NT + DEC_BATCH)
                for hf in range(2):
                    sp.dma_start(O[11][0].rearrange("b (r f) d v -> f d b r v", f=2)[hf],
                                 SS[64 * hf:64 * hf + 64, :, :, :]).then_inc(s_out, 16)
                sp.wait_ge(s_out, 64)

            @block.tensor
            def _(pe):
                def front_transposes(i):
                    r, T = rows(i), tile_of(i)
                    if i >= 1:
                        pe.wait_ge(t_act, i)
                    if i >= 2:
                        pe.wait_ge(y_done, i - 1)
                    for p in range(2):
                        nc.tensor.transpose(tr[:, p * P:p * P + r], T[0:r, C_GQ + p * P:C_GQ + (p + 1) * P], st.ident[0:r, 0:r])
                        nc.tensor.transpose(tr[:, (2 + p) * P:(2 + p) * P + r], T[0:r, C_GK + p * P:C_GK + (p + 1) * P], st.ident[0:r, 0:r])
                    nc.tensor.transpose(gg_ps[0:16, 0:r], T[0:r, C_GG:C_GG + 16], st.ident[0:r, 0:r]).then_inc(t_done, 1)

                def front_gates(i):
                    r = rows(i)
                    pe.wait_ge(g_dve, i + 1)
                    if i == 0:
                        pe.wait_ge(cin, 16 * 8)
                    else:
                        pe.wait_ge(kt_act, i)
                    for p in range(2):
                        last = nc.tensor.matmul(misc[:, p * P:p * P + r], w2[:, p * P:(p + 1) * P], ggT[:, 0:r],
                                                start=True, stop=True)
                    last.then_inc(z_done, 1)

                def level(i, l):
                    r, s, g = rows(i), i % 2, lev0[i] + l
                    if g >= 2:
                        pe.wait_ge(lev_used, g - 1)
                    for h in range(GLA_H):
                        kk = kT[half(h), s, h // 2, 0:r] if l == 0 else EE[half(h), s, l, h // 2, 0:r]
                        qq = qT[half(h), s, h // 2, 0:r] if l == 0 else QM[half(h), l, h // 2, 0:r]
                        last = nc.tensor.matmul(ps[0:r, 3 + 2 * (g % 2) + h % 2, (h // 2) * P:(h // 2) * P + r], kk, qq,
                                                start=True, stop=True)
                    last.then_inc(lev_done, 1)

                front_transposes(0)
                front_gates(0)
                for i in range(TILES):
                    r, T = rows(i), tile_of(i)
                    pe.wait_ge(qk_done, i + 1)
                    if i >= 1:
                        pe.wait_ge(kv_used, i)
                    for p in range(2):
                        last = nc.tensor.transpose(misc[0:r, p * P:(p + 1) * P], kin[:, p, 0:r], st.ident[:, :])
                    last.then_inc(kt_done, 1)
                    if i + 1 < TILES:
                        front_transposes(i + 1)
                    for l in range(lv(i)):
                        level(i, l)
                        if l == 3 and i + 1 < TILES:
                            front_gates(i + 1)
                    if i == NT:
                        pe.wait_ge(kt_act, i + 1)
                        for h in range(GLA_H):
                            for b in range(DEC_BATCH):
                                last = nc.tensor.matmul(ot_ps[h % 2][:, (h // 2) * NS + 8 * b:(h // 2) * NS + 8 * b + 8],
                                                        SS[half(h), b, h // 2, :], qin[half(h), h // 2, 8 * b:8 * b + 8],
                                                        start=True, stop=True)
                        last.then_inc(ot_done, 1)
                        pe.wait_ge(ot_act, 2)
                    pe.wait_ge(lev_used, lev0[i + 1])
                    if i >= 1:
                        pe.wait_ge(y_done, i)
                    for h in range(GLA_H):
                        nc.tensor.matmul(o_of(h, r), A_sb[0:r, h % 2, h // 2, 0:r],
                                         T[0:r, C_GV + h * DV:C_GV + (h + 1) * DV], start=True, stop=False)
                        if i < NT:
                            last = nc.tensor.matmul(o_of(h, r), qin[half(h), h // 2, 0:r],
                                                    S[half(h), h // 2, :], start=False, stop=True)
                        else:
                            last = nc.tensor.matmul(o_of(h, r), oT[:, h % 2, h // 2, :], st.ident[:, :],
                                                    start=False, stop=True)
                    last.then_inc(o_done, 1)
                    pe.wait_ge(kt_act, i + 1)
                    if i < NT:
                        pe.wait_ge(z_biased, i + 2)
                        for p in range(2):
                            last = nc.tensor.matmul(misc[:, p * 256:(p + 1) * 256], kinT[0:r, p, :],
                                                    T[0:r, C_GV + 256 * p:C_GV + 256 * p + 256], start=True, stop=True)
                        last.then_inc(kv_done, 1)
                    else:
                        for b in range(DEC_BATCH):
                            pe.wait_ge(kb_done, b + 1)
                            pe.wait_ge(kv_used, NT + b)
                            for p in range(2):
                                last = nc.tensor.matmul(misc[:, p * 256:(p + 1) * 256], kinTb[0:r, b, p, :],
                                                        T[0:r, C_GV + 256 * p:C_GV + 256 * p + 256], start=True, stop=True)
                            last.then_inc(kv_done, 1)

            @block.scalar
            def _(act):
                link = chained(act, ach)

                def front_copies(i):
                    r = rows(i)
                    act.wait_ge(t_done, i + 1)
                    if i >= 2:
                        act.wait_ge(o_done, i - 1)
                        act.wait_ge(qk_done, i - 1)
                    trv = tr.rearrange("p (a t) -> p a t", a=4)
                    nc.scalar.mul(qT[:, i % 2, :, 0:r], trv[:, 0:2, 0:r], DK ** -0.5)
                    nc.scalar.copy(kT[:, i % 2, :, 0:r], trv[:, 2:4, 0:r]).then_inc(t_act, 1)

                def front_gates(i):
                    r = rows(i)
                    act.wait_ge(z_biased, i + 1)
                    nc.scalar.activation(az[:, :, 0:r], z[:, :, 0:r], ACT.Abs).then_inc(az_done, 1)
                    act.wait_ge(az_done, i + 1)
                    link(nc.scalar.activation(az[:, :, 0:r], az[:, :, 0:r], ACT.Exp, scale=-1.0))
                    nc.scalar.activation(az[:, :, 0:r], az[:, :, 0:r], ACT.Ln, bias=1.0).then_inc(ln_done, 1)

                front_copies(0)
                front_gates(0)
                for i in range(TILES):
                    gr = tile_of(i)[0:rows(i), C_GR:C_GR + 512]
                    nc.scalar.activation(gr, gr, ACT.Silu).then_inc(silu_done, 1)
                for i in range(TILES):
                    r, T = rows(i), tile_of(i)
                    E, dec = EE[:, i % 2], decs[:, i % 2]
                    act.wait_ge(d_done, i + 1)
                    nc.scalar.activation(dec, dec, ACT.Exp, scale=1 / TAU)
                    if i < NT:
                        nc.scalar.activation(E, E, ACT.Exp, scale=1 / TAU).then_inc(e_done, 1)
                    else:
                        nc.scalar.activation(E[:, 0:4, :, 0:r], E[:, 0:4, :, 0:r], ACT.Exp, scale=1 / TAU)
                        nc.scalar.activation(E[:, NL, :, 0:r], E[:, NL, :, 0:r], ACT.Exp, scale=1 / TAU).then_inc(e_done, 1)
                    act.wait_ge(kt_done, i + 1)
                    nc.scalar.copy(kinT[0:r, :, :], misc.rearrange("p (a t) -> p a t", a=4)[0:r, 0:2, :]).then_inc(kt_act, 1)
                    if i == NT:
                        act.wait_ge(ot_done, 1)
                        for hf in range(2):
                            nc.scalar.copy(oT[:, hf, :, :], ot_ps[hf][:, 0:2 * NS].rearrange("p (h t) -> p h t", h=2)
                                           ).then_inc(ot_act, 1)
                    else:
                        front_copies(i + 1)
                        front_gates(i + 1)
                    act.wait_ge(o_done, i + 1)
                    for h in range(GLA_H):
                        ins = nc.scalar.activation(junk[0:r, :], o_of(h, r), ACT.Square, accum_out=ssq[0:r, h:h + 1])
                        if h < GLA_H - 1:
                            link(ins)
                        else:
                            ins.then_inc(sq_done, 1)
                    act.wait_ge(ms_done, i + 1)
                    link(nc.scalar.activation(rs[0:r, :], ssq[0:r, :], ACT.Ln))
                    nc.scalar.activation(rs[0:r, :], rs[0:r, :], ACT.Exp, scale=-0.5).then_inc(rs_done, 1)

            @block.gpsimd
            def _(pool):
                link = chained(pool, pch)
                pool.wait_ge(cin, 16 * 8)
                for i in range(TILES):
                    r, T = rows(i), tile_of(i)
                    pool.wait_ge(silu_done, i + 1)
                    g4 = T[0:r, C_GR:C_GR + 512].rearrange("p (h v) -> p h v", h=4)
                    nc.gpsimd.tensor_tensor(g4, g4, ng[0:r, :].unsqueeze(1).to_broadcast([r, 4, DV]), ALU.mult).then_inc(gate_done, 1)
                for i in range(TILES):
                    r, T = rows(i), tile_of(i)
                    if i == NT:
                        pool.wait_ge(kt_act, i + 1)
                        pool.wait_ge(lev_used, lev0[i + 1])
                        for b in range(DEC_BATCH):
                            nc.gpsimd.tensor_scalar(kinTb[0:r, b, :, :], kinT[0:r, :, :], bsel[0:r, b:b + 1], None,
                                                    ALU.mult).then_inc(kb_done, 1)

            @block.vector
            def _(dve):
                link = chained(dve, dch)

                def front_copy(i):
                    r = rows(i)
                    dve.wait_ge(t_done, i + 1)
                    nc.vector.tensor_copy(ggT[:, 0:r], gg_ps[0:16, 0:r]).then_inc(g_dve, 1)

                def front_bias(i):
                    r = rows(i)
                    dve.wait_ge(z_done, i + 1)
                    for p in range(2):
                        ins = nc.vector.tensor_scalar(z[:, p, 0:r], misc[:, p * P:p * P + r], gb[:, p:p + 1], None, ALU.add)
                        if p == 0:
                            link(ins)
                    ins.then_inc(z_biased, 1)
                    dve.wait_ge(az_done, i + 1)
                    link(nc.vector.tensor_scalar(z[:, :, 0:r], z[:, :, 0:r], 0.0, None, ALU.min))

                def front_differences(i):
                    r = rows(i)
                    E, dec = EE[:, i % 2], decs[:, i % 2]
                    dve.wait_ge(ln_done, i + 1)
                    link(nc.vector.tensor_tensor(z[:, :, 0:r], z[:, :, 0:r], az[:, :, 0:r], ALU.subtract))
                    o0 = 0 if i < NT else P
                    for p in range(2):
                        link(nc.vector.tensor_tensor_scan(cs[:, p, 0:r], reset[:, o0:o0 + r], z[:, p, 0:r], 0.0,
                                                          ALU.mult, ALU.add))
                    nb0 = 1 if i < NT else DEC_BATCH
                    T0 = r // nb0
                    link(nc.vector.tensor_copy(dec, cs[:, :, T0 - 1:r:T0] if i == NT else
                                               cs[:, :, r - 1:r].to_broadcast([P, 2, 8])))
                    nc.vector.tensor_tensor(
                        E[:, 0, :, 0:r].rearrange("p a (b t) -> p a b t", b=nb0),
                        dec[:, :, 0:nb0].unsqueeze(3).to_broadcast([P, 2, nb0, T0]),
                        cs[:, :, 0:r].rearrange("p a (b t) -> p a b t", b=nb0), ALU.subtract)
                    nc.vector.tensor_copy(E[:, NL, :, 0:r], cs[:, :, 0:r])
                    for l in range(1, lv(i)):
                        L = 2 ** (l - 1)
                        c3 = cs[:, :, 0:r].rearrange("p a (b f t) -> p a b f t", f=2, t=L)
                        e3 = E[:, l, :, 0:r].rearrange("p a (b f t) -> p a b f t", f=2, t=L)
                        nb = r // (2 * L)
                        anchor = c3[:, :, :, 0, L - 1:L].to_broadcast([P, 2, nb, L])
                        nc.vector.tensor_tensor(e3[:, :, :, 0, :], anchor, c3[:, :, :, 0, :], ALU.subtract)
                        ins = nc.vector.tensor_tensor(e3[:, :, :, 1, :], c3[:, :, :, 1, :], anchor, ALU.subtract)
                    ins.then_inc(d_done, 1)

                def decayed(i):
                    r, n, E = rows(i), lv(i), EE[:, i % 2]
                    dve.wait_ge(e_done, i + 1)
                    dve.wait_ge(t_act, i + 1)
                    q, k = qT[:, i % 2], kT[:, i % 2]
                    nc.vector.tensor_tensor(kin[:, :, 0:r], E[:, 0, :, 0:r], k[:, :, 0:r], ALU.mult)
                    nc.vector.tensor_tensor(qin[:, :, 0:r], E[:, NL, :, 0:r], q[:, :, 0:r], ALU.mult)
                    for p in range(2):
                        qb = q[:, p:p + 1, 0:r].to_broadcast([P, n - 1, r])
                        kb = k[:, p:p + 1, 0:r].to_broadcast([P, n - 1, r])
                        link(nc.vector.tensor_tensor(QM[:, 1:n, p, 0:r], E[:, 1:n, p, 0:r], qb, ALU.mult))
                        ins = nc.vector.tensor_tensor(E[:, 1:n, p, 0:r], E[:, 1:n, p, 0:r], kb, ALU.mult)
                    ins.then_inc(qk_done, 1)

                def take_level(i, l):
                    r, g = rows(i), lev0[i] + l
                    dve.wait_ge(lev_done, g + 1)
                    if g >= 1:
                        dve.wait_ge(lev_used, g)
                    for hf in range(2):
                        ins = nc.vector.copy_predicated(
                            A_sb[0:r, hf, :, 0:r], lev[0:r, l:l + 1, 0:r].to_broadcast([r, 2, r]),
                            ps[0:r, 3 + 2 * (g % 2) + hf, 0:2 * P].rearrange("s (h t) -> s h t", h=2)[:, :, 0:r])
                    ins.then_inc(lev_used, 1)

                def decay_state(i, state, b):
                    dec = decs[:, i % 2]
                    for h in range(GLA_H):
                        c0 = (h // 2) * 256 + (h % 2) * DV
                        ins = nc.vector.scalar_tensor_tensor(
                            out=state[half(h), h // 2, :], in0=state[half(h), h // 2, :],
                            scalar=dec[half(h), h // 2, b:b + 1], in1=misc[half(h), c0:c0 + DV],
                            op0=ALU.mult, op1=ALU.add)
                    ins.then_inc(kv_used, 1)

                def gated_output(i):
                    r, T = rows(i), tile_of(i)
                    dve.wait_ge(rs_done, i + 1)
                    dve.wait_ge(gate_done, i + 1)
                    for h in range(GLA_H):
                        gr = T[0:r, C_GR + h * DV:C_GR + (h + 1) * DV]
                        ins = nc.vector.scalar_tensor_tensor(out=gr, in0=o_of(h, r), scalar=rs[0:r, h:h + 1], in1=gr,
                                                             op0=ALU.mult, op1=ALU.mult)
                    ins.then_inc(y_done, 1)

                dve.wait_ge(cin, 16 * 8)
                link(nc.vector.tensor_copy(lev[:, :, :], lev_f[:, :, :]))
                link(nc.vector.memset(A_sb[:, :, :, :], 0.0))
                nc.vector.memset(S[:, :, :], 0.0).then_inc(cst, 1)
                dve.wait_ge(cst, 1)
                front_copy(0)
                front_bias(0)
                front_differences(0)
                for i in range(TILES):
                    r = rows(i)
                    decayed(i)
                    if i >= 1:
                        gated_output(i - 1)
                    if i < NT:
                        front_copy(i + 1)
                    else:
                        dve.wait_ge(o_done, NT)
                        dve.wait_ge(lev_used, lev0[NT])
                        link(nc.vector.memset(A_sb[0:r, :, :, 0:r], 0.0))
                    for l in range(4):
                        take_level(i, l)
                    if i < NT:
                        front_bias(i + 1)
                        for l in range(4, NL):
                            take_level(i, l)
                        front_differences(i + 1)
                        dve.wait_ge(kv_done, i + 1)
                        dve.wait_ge(o_done, i + 1)
                        decay_state(i, S, 0)
                    else:
                        for b in range(DEC_BATCH):
                            dve.wait_ge(kv_done, NT + 1 + b)
                            decay_state(i, SS[:, b], b)
                    dve.wait_ge(sq_done, i + 1)
                    nc.vector.tensor_scalar(ssq[0:r, :], ssq[0:r, :], 1.0 / DV, RMS_EPS, ALU.mult, ALU.add).then_inc(ms_done, 1)
                gated_output(NT)
                dve.wait_ge(y_done, TILES)


TOPK = 256
NEG = -1e30
TAKEN = -3e38
AS = HD ** -0.5
IWS = 512.0 ** -0.5


def dsa_prompt(nc, st, A, C, O, H, Hs, XT):
    HEADS = [(kv, g) for g in range(4) for kv in range(2)]
    NH = len(HEADS)
    chunks = lambda t: -(-(t + 1) * P // 512)
    ptg = lambda t: -(-(t + 1) // 4)
    def passes(i):
        t, out = i + 2, []
        if t < NT:
            out += [("iq", t)] if t >= 2 else []
            out += [("keys", t)]
            if t >= 2:
                out += [("dots", t, h, c) for h in range(8) for c in range(chunks(t))]
        if 0 <= i + 1 < NT:
            out.append(("q", i + 1))
        return out

    def shares(i):
        u, rounds = passes(i), range(TOPK // 8) if 2 <= i + 1 < NT else []
        per, rper = -(-len(u) // NH), -(-len(rounds) // NH)
        return [(u[n * per:(n + 1) * per], rounds[n * rper:(n + 1) * rper]) for n in range(NH)]

    pass_no, dot_no = {}, {}
    for i in range(-2, NT):
        for u in passes(i):
            pass_no[u] = len(pass_no)
            if u[0] == "dots":
                dot_no[u] = len(dot_no)
    grp_no = {}
    for i in range(NT):
        for n in range(NH):
            for c in range(ptg(i)):
                grp_no[(i, n, c)] = len(grp_no)
    with ExitStack() as ctx:
        sb = lambda n, s, d=F32: ctx.enter_context(nc.sbuf_tensor(f"dsa_{n}", s, d))
        sem = lambda n: st.sem(f"dsa_{n}")
        KT, IKT = sb("KT", [P, SEQ]), sb("IKT", [P, SEQ])
        qT, iqT = sb("qT", [P, 2, 4, P]), sb("iqT", [P, 4, P])
        rel = sb("rel", [P, 4, 512])
        iws = sb("iws", [P, 8])
        sc, wk = sb("sc", [P, SEQ]), sb("wk", [P, SEQ])
        m8 = sb("m8", [P, 8])
        bias = sb("bias", [P, 2, SEQ], BF16)
        identb = sb("identb", [P, P], BF16)
        causal = sb("causal", [P, P])
        Pb, PT = sb("P", [P, 2, SEQ]), sb("PT", [P, 2, NT, P])
        mx, nm, sm, rs = sb("mx", [P, 2]), sb("nm", [P, 2]), sb("sm", [P, NH]), sb("rs", [P, NH])
        ps = ctx.enter_context(nc.psum_tensor("dsa_ps", [P, 8, 512], F32))
        cin = sem("const_in")
        p7_done, p7_read, dots_added = sem("pass_done"), sem("pass_read"), sem("dots_added")
        b_done = sem("bias_ready")
        s_done, m_done, e_done = sem("scores"), sem("max_done"), sem("probs")
        pt_done, pt_copied = sem("probs_transposed"), sem("probsT_copied")
        o_done, y_done, yt_done, yt_act = sem("o_done"), sem("y_done"), sem("y_transposed"), sem("yT_copied")
        dch = sem("dve_step")
        half = lambda kv: slice(64 * kv, 64 * kv + 64)

        with nc.Block() as block:
            @block.sync
            def _(sp):
                sp.dma_start(causal[:, :], C["causal"]).then_inc(cin, 16)
                sp.wait_ge(cin, 16)

            @block.tensor
            def _(pe):
                def bank7(u):
                    no, T = pass_no[u], H[:, u[1], :]
                    if no >= 1:
                        pe.wait_ge(p7_read, no)
                    if u[0] == "iq":
                        for g in range(4):
                            last = nc.tensor.transpose(ps[:, 7, g * P:(g + 1) * P], T[:, C_IQ + g * P:C_IQ + (g + 1) * P], st.ident[:, :])
                    elif u[0] == "keys":
                        nc.tensor.transpose(ps[:, 7, 0:P], T[:, C_DK:C_DK + P], st.ident[:, :])
                        last = nc.tensor.transpose(ps[:, 7, P:2 * P], T[:, C_IK:C_IK + P], st.ident[:, :])
                    elif u[0] == "q":
                        for g in range(4):
                            last = nc.tensor.transpose(ps[:, 7, g * P:(g + 1) * P], T[:, C_DQ + g * P:C_DQ + (g + 1) * P], st.ident[:, :])
                    else:
                        _, t, h, c = u
                        n = min(512, (t + 1) * P - 512 * c)
                        last = nc.tensor.matmul(ps[:, 7, 0:n], iqT[half(h % 2), h // 2, :],
                                                IKT[half(h % 2), 512 * c:512 * c + n], start=True, stop=True)
                    last.then_inc(p7_done, 1)

                def scores(i, n):
                    kv, g = HEADS[n]
                    a = i * NH + n
                    if n == 0:
                        pe.wait_ge(b_done, i + 1)
                        pe.wait_ge(p7_read, pass_no[("q", i)] + 1)
                    if a >= 2:
                        pe.wait_ge(e_done, a - 1)
                    for c in range(chunks(i)):
                        w = min(512, (i + 1) * P - 512 * c)
                        nc.tensor.matmul(ps[:, 2 * kv + c, 0:w], identb[:, :], bias[:, i % 2, 512 * c:512 * c + w],
                                         start=True, stop=False)
                        last = nc.tensor.matmul(ps[:, 2 * kv + c, 0:w], qT[half(kv), i % 2, g, :],
                                                KT[half(kv), 512 * c:512 * c + w], start=False, stop=True)
                    last.then_inc(s_done, 1)

                def transpose_probs(i, n):
                    a = i * NH + n
                    pe.wait_ge(e_done, a + 1)
                    for c in range(ptg(i)):
                        gn = grp_no[(i, n, c)]
                        if gn >= 2:
                            pe.wait_ge(pt_copied, gn - 1)
                        if n == 0 and i >= 1:
                            pe.wait_ge(yt_act, 2 * i)
                        for j in range(4 * c, min(4 * c + 4, i + 1)):
                            last = nc.tensor.transpose(ps[:, 4 + gn % 2, (j % 4) * P:(j % 4 + 1) * P],
                                                       Pb[:, a % 2, j * P:(j + 1) * P], st.ident[:, :])
                        last.then_inc(pt_done, 1)

                def values(i, n):
                    kv, g = HEADS[n]
                    a, h = i * NH + n, kv * 4 + g
                    pe.wait_ge(pt_copied, grp_no[(i, n, ptg(i) - 1)] + 1)
                    if n == 0 and i >= 1:
                        pe.wait_ge(y_done, i)
                    for j in range(i + 1):
                        last = nc.tensor.matmul(ps[:, 6, h * HD:(h + 1) * HD], PT[:, a % 2, j, :],
                                                H[:, j, C_DV + kv * HD:C_DV + (kv + 1) * HD],
                                                start=(j == 0), stop=(j == i))
                    last.then_inc(o_done, 1)

                for i in (-2, -1):
                    for u in passes(i):
                        bank7(u)
                for i in range(NT):
                    T, share = H[:, i, :], shares(i)
                    scores(i, 0)
                    for n in range(NH):
                        if n + 1 < NH:
                            scores(i, n + 1)
                        transpose_probs(i, n)
                        for u in share[n][0]:
                            bank7(u)
                        values(i, n)
                    pe.wait_ge(y_done, i + 1)
                    for k in range(KD):
                        c0 = C_GR + k * P if k < 4 else C_DQ + (k - 4) * P
                        last = nc.tensor.transpose(ps[:, 4 + k // 4, (k % 4) * P:(k % 4 + 1) * P],
                                                   T[:, c0:c0 + P], st.ident[:, :])
                        if k % 4 == 3:
                            last.then_inc(yt_done, 1)

            @block.scalar
            def _(act):
                def bank7(u):
                    act.wait_ge(p7_done, pass_no[u] + 1)
                    t, full = u[1], ps[:, 7, :].rearrange("p (a t) -> p a t", a=4)
                    if u[0] == "iq":
                        nc.scalar.copy(iqT[:, :, :], full).then_inc(p7_read, 1)
                    elif u[0] == "keys":
                        nc.scalar.copy(KT[:, t * P:(t + 1) * P], ps[:, 7, 0:P])
                        nc.scalar.copy(IKT[:, t * P:(t + 1) * P], ps[:, 7, P:2 * P]).then_inc(p7_read, 1)
                    elif u[0] == "q":
                        nc.scalar.copy(qT[:, t % 2, :, :], full).then_inc(p7_read, 1)
                    else:
                        d, n = dot_no[u], min(512, (t + 1) * P - 512 * u[3])
                        if d >= 4:
                            act.wait_ge(dots_added, d - 3)
                        nc.scalar.activation(rel[:, d % 4, 0:n], ps[:, 7, 0:n], ACT.Relu).then_inc(p7_read, 1)

                def exps(i, n):
                    kv, g = HEADS[n]
                    a, L = i * NH + n, (i + 1) * P
                    act.wait_ge(m_done, a + 1)
                    if a >= 2:
                        act.wait_ge(o_done, a - 1)
                    nc.scalar.activation(Pb[:, a % 2, 0:L], ps[:, 2 * kv:2 * kv + 2, :].rearrange("p b n -> p (b n)")[:, 0:L],
                                         ACT.Exp, bias=nm[:, a % 2:a % 2 + 1], scale=AS,
                                         accum_out=sm[:, n:n + 1]).then_inc(e_done, 1)

                for i in (-2, -1):
                    for u in passes(i):
                        bank7(u)
                for i in range(NT):
                    share = shares(i)
                    if i >= 1:
                        act.wait_ge(y_done, i)
                    exps(i, 0)
                    for n in range(NH):
                        for u in share[n][0]:
                            bank7(u)
                        if n + 1 < NH:
                            exps(i, n + 1)
                    for k in range(2):
                        act.wait_ge(yt_done, 2 * i + k + 1)
                        nc.scalar.copy(XT[:, 4 * k:4 * k + 4, i * P:(i + 1) * P],
                                       ps[:, 4 + k, :].rearrange("p (a t) -> p a t", a=4)).then_inc(yt_act, 1)

            @block.vector
            def _(dve):
                link = chained(dve, dch)
                dve.wait_ge(cin, 16)
                link(nc.vector.tensor_copy(identb[:, :], st.ident[:, :]))
                link(nc.vector.memset(bias[:, 1, 0:P], 0.0))
                for t in range(2):
                    nc.vector.tensor_copy(bias[:, t, t * P:(t + 1) * P], causal[:, :]).then_inc(b_done, 1)

                def add_dots(u):
                    _, t, h, c = u
                    d, n = dot_no[u], min(512, (t + 1) * P - 512 * c)
                    if h == 0 and c == 0:
                        link(nc.vector.tensor_scalar(iws[:, :], H[:, t, C_IW:C_IW + 8], IWS, None, ALU.mult))
                    part = sc[:, 512 * c:512 * c + n]
                    dve.wait_ge(p7_read, pass_no[u] + 1)
                    if h == 0:
                        nc.vector.tensor_scalar(part, rel[:, d % 4, 0:n], iws[:, h:h + 1], None, ALU.mult).then_inc(dots_added, 1)
                    else:
                        dve.wait_ge(dots_added, d)
                        nc.vector.scalar_tensor_tensor(out=part, in0=rel[:, d % 4, 0:n], scalar=iws[:, h:h + 1], in1=part,
                                                       op0=ALU.mult, op1=ALU.add).then_inc(dots_added, 1)

                def top_round(t, k):
                    L = (t + 1) * P
                    if k == 0:
                        dve.wait_ge(dots_added, dot_no[("dots", t, 7, chunks(t) - 1)] + 1)
                        link(nc.vector.tensor_tensor(sc[:, L - P:L], sc[:, L - P:L], causal[:, :], ALU.add))
                    src = sc if k == 0 else wk
                    link(nc.vector.max(m8[:, :], src[:, 0:L]))
                    link(nc.vector.match_replace(wk[:, 0:L], m8[:, :], src[:, 0:L], TAKEN))
                    if k == TOPK // 8 - 1:
                        nc.vector.tensor_scalar(bias[:, t % 2, 0:L], wk[:, 0:L], -2e38, NEG, ALU.is_ge, ALU.mult).then_inc(b_done, 1)

                def row_max(i, n):
                    kv, g = HEADS[n]
                    a, L = i * NH + n, (i + 1) * P
                    dve.wait_ge(s_done, a + 1)
                    link(nc.vector.reduce_max(mx[:, a % 2:a % 2 + 1],
                                              ps[:, 2 * kv:2 * kv + 2, :].rearrange("p b n -> p (b n)")[:, 0:L], AX_X))
                    if a >= 2:
                        dve.wait_ge(e_done, a - 1)
                    nc.vector.tensor_scalar(nm[:, a % 2:a % 2 + 1], mx[:, a % 2:a % 2 + 1], -AS, None,
                                            ALU.mult).then_inc(m_done, 1)

                def copy_pt(i, n):
                    a = i * NH + n
                    if a >= 2:
                        dve.wait_ge(o_done, a - 1)
                    for c in range(ptg(i)):
                        gn = grp_no[(i, n, c)]
                        w = min(4, i + 1 - 4 * c)
                        dve.wait_ge(pt_done, gn + 1)
                        nc.vector.tensor_copy(PT[:, a % 2, 4 * c:4 * c + w, :],
                                              ps[:, 4 + gn % 2, 0:w * P].rearrange("p (a t) -> p a t", t=P)).then_inc(pt_copied, 1)

                for i in range(NT):
                    T, share = H[:, i, :], shares(i)
                    row_max(i, 0)
                    for n in range(NH):
                        rounds = share[n][1]
                        cut = len(rounds) // 2
                        if n + 1 < NH:
                            row_max(i, n + 1)
                        for k in rounds[:cut]:
                            top_round(i + 1, k)
                        copy_pt(i, n)
                        for k in rounds[cut:]:
                            top_round(i + 1, k)
                        for u in share[n][0]:
                            if u[0] == "dots":
                                add_dots(u)
                    dve.wait_ge(e_done, (i + 1) * NH)
                    link(nc.vector.reciprocal(rs[:, :], sm[:, :]))
                    dve.wait_ge(o_done, (i + 1) * NH)
                    for kv in range(2):
                        ins = nc.vector.tensor_tensor(
                            T[:, C_DQ + kv * 256:C_DQ + (kv + 1) * 256].rearrange("p (g d) -> p g d", g=4),
                            ps[:, 6, kv * 256:(kv + 1) * 256].rearrange("p (g d) -> p g d", g=4),
                            rs[:, kv::2].unsqueeze(2).to_broadcast([P, 4, HD]), ALU.mult)
                    ins.then_inc(y_done, 1)
                dve.wait_ge(y_done, NT)


PAGES = 16
PAST = PAGES * P
LK = PAST + DEC_SEQ
CHUNKS = [(0, 512), (512, 512), (1024, 512), (1536, 512), (2048, 8)]


def dsa_sample(nc, st, A, C, O, Hs, XT):
    NB, NP_ = DEC_BATCH, DEC_BATCH // 2
    scr_w = nc.dram_tensor("scratch_iw", (NS, 8), F32, kind="Internal").ap()
    scr_y = nc.dram_tensor("scratch_y", (NS, 512), F32, kind="Internal").ap()
    n_pool = A["cache_k"].shape[1]
    with ExitStack() as ctx:
        sb = lambda n, s, d=F32: ctx.enter_context(nc.sbuf_tensor(f"smp_{n}", s, d))
        sem = lambda n: st.sem(f"smp_{n}")
        pages = sb("pages", [1, NB * PAGES], I32)
        idxp, ikT = sb("idxp", [P, 2, PAGES, HD]), sb("ikT", [HD, 2, LK])
        iqT, ikn = sb("iqT", [HD, NB, 8, DEC_SEQ]), sb("ikn", [HD, NS])
        rel = sb("rel", [NS, 2, 512])
        iwd = sb("iwd", [NS, NB])
        gat, gw = sb("gat", [NS, NB, NS]), sb("gw", [NS, NB, NS])
        sc, wk, m8 = sb("sc", [NS, LK]), sb("wk", [NS, LK]), sb("m8", [NS, 8])
        bias = sb("bias", [NS, LK], BF16)
        c8 = sb("c8", [NS, 8])
        spf, spb = sb("spf", [NS, NP_, P]), sb("spb", [NS, NP_, P], BF16)
        qz, KnT = sb("qz", [P, NB, 2, 4, DEC_SEQ]), sb("KnT", [P, NS])
        Kp, KT = sb("Kp", [P, 2, PAGES, P]), sb("KT", [P, 2, LK])
        Vp, Vn = sb("Vp", [P, 4, PAGES, P]), sb("Vn", [DEC_SEQ, NB, P])
        Pb, PT = sb("P", [P, LK]), sb("PT", [P, PAGES + 1, P])
        mx, nm, sm, rs = sb("mx", [P, 1]), sb("nm", [P, 1]), sb("sm", [P, 1]), sb("rs", [P, 1])
        yq = sb("yq", [P, NP_, HD])
        ps = ctx.enter_context(nc.psum_tensor("smp_ps", [P, 8, 512], F32))
        flat = ps[:, 0:5, :].rearrange("p b n -> p (b n)")
        cin, pin = sem("const_in"), sem("page_table_in")
        ix_in = [sem("index_pages0"), sem("index_pages1")]
        k_in, v_in = [sem("k_pages0"), sem("k_pages1")], [sem(f"v_pages{k}") for k in range(4)]
        w_out, w_in, vn_in = sem("iw_out"), sem("iw_in"), sem("v_new_in")
        h_t, h_c = sem("heads_transposed"), sem("heads_copied")
        it_done, it_copied = sem("index_transposed"), sem("index_copied")
        dt_done, dt_relu, sum_done = sem("dots"), sem("relu"), sem("summed")
        gw_done, b_done = sem("weights_ready"), sem("bias_ready")
        kt_done, kt_copied = sem("k_transposed"), sem("k_copied")
        s_done, m_done, e_done, pt_done, pt_copied = (sem("scores"), sem("max"), sem("probs"), sem("p_transposed"),
                                                      sem("p_copied"))
        o_done, y_done, y_out, y_in, yt_done, yt_copied = (sem("o"), sem("y"), sem("y_out"), sem("y_in"),
                                                           sem("yT"), sem("yT_copied"))
        dch, ach = sem("dve_step"), sem("act_step")
        zeroed = sem("qz_zeroed")

        def load_pages(eng, b, cache, dst, slot, landed):
            with eng.Fori(0, PAGES) as j:
                page = eng.value_load(pages[0:1, bass.ds(j + b * PAGES, 1)], min_val=0, max_val=n_pool - 1)
                src = cache[bass.ds(page, 1)]
                src = src.rearrange("o p k d -> (o p) (k d)") if len(src.shape) == 4 else src.rearrange("o p d -> (o p) d")
                eng.dma_start(dst[:, slot, bass.ds(j, 1), :].rearrange("p o c -> p (o c)"), src).then_inc(landed, 16)

        with nc.Block() as block:
            @block.sync
            def _(sp):
                sp.dma_start(pages[:, :], A["page_table"].rearrange("(o a) b -> o (a b)", o=1)).then_inc(pin, 16)
                sp.dma_start(scr_w, Hs[0:NS, C_IW:C_IW + 8]).then_inc(w_out, 16)
                for dst, src in ((gat[:, :, :], C["gather"]), (c8[:, :], C["causal8"]), (spf[:, :, :], C["spread"])):
                    sp.dma_start(dst, src).then_inc(cin, 16)
                sp.wait_ge(pin, 16)
                sp.wait_ge(w_out, 16)
                for h in range(8):
                    sp.dma_start(iwd[8 * h:8 * h + 8, :], bass.AP(scr_w.tensor, h, [[8, 8], [64, 8]]),
                                 allow_slow_non_contiguous=True).then_inc(w_in, 16)
                for b in range(NB):
                    sp.dma_start(Vn[:, b, :], Hs[8 * b:8 * b + 8, C_DV:C_DV + P]).then_inc(vn_in, 16)

                for b in range(0, NB, 2):
                    if b >= 2:
                        sp.wait_ge(it_done, 4 * (b - 1))
                    load_pages(sp, b, A["cache_idx"][0], idxp, 0, ix_in[0])
                for b in range(NB):
                    if b >= 2:
                        sp.wait_ge(kt_done, 4 * (b - 1))
                    load_pages(sp, b, A["cache_k"][0], Kp, b % 2, k_in[b % 2])

            @block.gpsimd
            def _(pool):
                pool.wait_ge(pin, 16)
                for b in range(1, NB, 2):
                    if b >= 2:
                        pool.wait_ge(it_done, 4 * (b - 1))
                    load_pages(pool, b, A["cache_idx"][0], idxp, 1, ix_in[1])
                for b in range(4):
                    load_pages(pool, b, A["cache_v"][0], Vp, b % 4, v_in[b % 4])
                for p in range(NP_):
                    pool.wait_ge(y_done, p + 1)
                    for b2 in range(2):
                        pool.dma_start(bass.AP(scr_y.tensor, (2 * p + b2) * DEC_SEQ * 512, [[HD, 8], [512, DEC_SEQ], [1, HD]]),
                                       yq[64 * b2:64 * b2 + 64, p, :]).then_inc(y_out, 16)
                        if p + 2 < NP_:
                            load_pages(pool, 2 * p + 4 + b2, A["cache_v"][0], Vp, (2 * p + b2) % 4, v_in[(2 * p + b2) % 4])
                pool.wait_ge(y_out, 32 * NP_)
                pool.dma_start(Hs[0:NS, C_DQ:C_DQ + 512], scr_y).then_inc(y_in, 16)
                pool.wait_ge(y_in, 16)

            @block.tensor
            def _(pe):
                I64 = st.ident[0:NS, 0:NS]
                for h in range(8):
                    nc.tensor.transpose(ps[0:HD, 0, h * NS:(h + 1) * NS], Hs[0:NS, C_IQ + h * HD:C_IQ + (h + 1) * HD], I64)
                nc.tensor.transpose(ps[0:HD, 1, 0:NS], Hs[0:NS, C_IK:C_IK + HD], I64)
                nc.tensor.transpose(ps[:, 1, NS:2 * NS], Hs[0:NS, C_DK:C_DK + P], I64)
                for g in range(4):
                    last = nc.tensor.transpose(ps[:, 2, g * NS:(g + 1) * NS], Hs[0:NS, C_DQ + g * P:C_DQ + (g + 1) * P], I64)
                last.then_inc(h_t, 1)
                pe.wait_ge(h_c, 5)
                def index_keys_T(b, q):
                    s, g = b % 2, 4 * b + q
                    if q == 0:
                        pe.wait_ge(ix_in[s], 16 * PAGES * (b // 2 + 1))
                    if g >= 1:
                        pe.wait_ge(it_copied, g + (g - 1) // 4)
                    for j in range(4):
                        last = nc.tensor.transpose(ps[0:HD, 5, j * P:(j + 1) * P], idxp[:, s, 4 * q + j, :], st.ident[:, :])
                    last.then_inc(it_done, 1)

                def add_heads(b, c):
                    g, n = 5 * b + c, CHUNKS[c][1]
                    pe.wait_ge(dt_relu, g + 1)
                    if g == 0:
                        pe.wait_ge(gw_done, 1)
                    nc.tensor.matmul(ps[0:NS, c, 0:n], gw[:, b, :], rel[:, g % 2, 0:n],
                                     start=(b == 0), stop=(b == NB - 1)).then_inc(sum_done, 1)

                for q in range(4):
                    index_keys_T(0, q)
                for b in range(NB):
                    s = b % 2
                    pe.wait_ge(it_copied, 5 * (b + 1))
                    for c, (c0, n) in enumerate(CHUNKS):
                        g = 5 * b + c
                        if g >= 2:
                            pe.wait_ge(dt_relu, g - 1)
                        nc.tensor.matmul(ps[0:NS, 6 + g % 2, 0:n], iqT[:, b, :, :].rearrange("d h q -> d (h q)"),
                                         ikT[:, s, c0:c0 + n], start=True, stop=True).then_inc(dt_done, 1)
                        if c < 4 and b + 1 < NB:
                            index_keys_T(b + 1, c)
                        if g >= 1:
                            add_heads((g - 1) // 5, (g - 1) % 5)
                add_heads(NB - 1, 4)

                def keys_T(b):
                    s = b % 2
                    pe.wait_ge(k_in[s], 16 * PAGES * (b // 2 + 1))
                    for q in range(4):
                        g = 4 * b + q
                        if g >= 2:
                            pe.wait_ge(kt_copied, g - 1)
                        for j in range(4):
                            last = nc.tensor.transpose(ps[:, 5 + g % 2, j * P:(j + 1) * P], Kp[:, s, 4 * q + j, :], st.ident[:, :])
                        last.then_inc(kt_done, 1)

                pe.wait_ge(dt_relu, 5 * NB)
                for p in range(NP_):
                    if p >= 1:
                        pe.wait_ge(pt_copied, 5 * p)
                    keys_T(2 * p)
                    keys_T(2 * p + 1)
                    pe.wait_ge(kt_copied, 8 * (p + 1))
                    if p == 0:
                        pe.wait_ge(b_done, 1)
                    else:
                        pe.wait_ge(e_done, p)
                    for c, (c0, n) in enumerate(CHUNKS):
                        nc.tensor.matmul(ps[:, c, 0:n], spb[:, p, :], bias[:, c0:c0 + n], start=True, stop=False)
                        for b2 in range(2):
                            last = nc.tensor.matmul(ps[64 * b2:64 * b2 + 64, c, 0:n],
                                                    qz[:, 2 * p + b2, :, :, :].rearrange("d v g q -> d (v g q)"),
                                                    KT[:, b2, c0:c0 + n], start=False, stop=True)
                    last.then_inc(s_done, 1)
                    pe.wait_ge(e_done, p + 1)
                    for c in range(5):
                        g = 5 * p + c
                        if g >= 2:
                            pe.wait_ge(pt_copied, g - 1)
                        for j in range(4 * c, min(4 * c + 4, PAGES + 1)):
                            n = P if j < PAGES else DEC_SEQ
                            last = nc.tensor.transpose(ps[0:n, 5 + g % 2, (j % 4) * P:(j % 4 + 1) * P],
                                                       Pb[:, j * P:j * P + n], st.ident[:, :])
                        last.then_inc(pt_done, 1)
                    pe.wait_ge(pt_copied, 5 * (p + 1))
                    pe.wait_ge(vn_in, 16 * NB)
                    if p >= 1:
                        pe.wait_ge(y_done, p)
                    for b2 in range(2):
                        vs = (2 * p + b2) % 4
                        pe.wait_ge(v_in[vs], 16 * PAGES * (p // 2 + 1))
                        r = slice(64 * b2, 64 * b2 + 64)
                        for j in range(PAGES):
                            nc.tensor.matmul(ps[r, 7, 0:P], PT[:, j, r], Vp[:, vs, j, :], start=(j == 0), stop=False)
                        last = nc.tensor.matmul(ps[r, 7, 0:P], PT[0:DEC_SEQ, PAGES, r], Vn[:, 2 * p + b2, :], start=False, stop=True)
                    last.then_inc(o_done, 1)
                pe.wait_ge(y_in, 16)
                for k in range(KD):
                    c0 = C_GR + k * P if k < 4 else C_DQ + (k - 4) * P
                    last = nc.tensor.transpose(ps[:, 0, k * NS:(k + 1) * NS], Hs[0:NS, c0:c0 + P], I64)
                last.then_inc(yt_done, 1)

            @block.scalar
            def _(act):
                act.wait_ge(h_t, 1)
                nc.scalar.copy(iqT[:, :, :, :].rearrange("d b h q -> d h b q"),
                               ps[0:HD, 0, :].rearrange("d (h b q) -> d h b q", h=8, b=NB)).then_inc(h_c, 1)
                nc.scalar.copy(ikn[:, :], ps[0:HD, 1, 0:NS]).then_inc(h_c, 1)
                nc.scalar.copy(KnT[:, :], ps[:, 1, NS:2 * NS]).then_inc(h_c, 1)
                act.wait_ge(zeroed, 1)
                for kv in range(2):
                    hf = slice(64 * kv, 64 * kv + 64)
                    nc.scalar.copy(qz[hf, :, kv, :, :].rearrange("d b g q -> d g b q"),
                                   ps[hf, 2, 0:4 * NS].rearrange("d (g b q) -> d g b q", g=4, b=NB)).then_inc(h_c, 1)
                act.wait_ge(h_c, 5)

                for b in range(NB):
                    s = b % 2
                    if b >= 2:
                        act.wait_ge(dt_done, 5 * (b - 1))
                    for q in range(4):
                        act.wait_ge(it_done, 4 * b + q + 1)
                        nc.scalar.copy(ikT[:, s, 512 * q:512 * (q + 1)], ps[0:HD, 5, :]).then_inc(it_copied, 1)
                    nc.scalar.copy(ikT[:, s, PAST:LK], ikn[:, 8 * b:8 * b + 8]).then_inc(it_copied, 1)
                for p in range(NP_):
                    for b2 in range(2):
                        b = 2 * p + b2
                        if p >= 1 and b2 == 0:
                            act.wait_ge(s_done, p)
                        for q in range(4):
                            act.wait_ge(kt_done, 4 * b + q + 1)
                            ins = nc.scalar.copy(KT[:, b2, 512 * q:512 * (q + 1)], ps[:, 5 + (4 * b + q) % 2, :])
                            if q == 3:
                                link_kn = nc.scalar.copy(KT[:, b2, PAST:LK], KnT[:, 8 * b:8 * b + 8])
                                link_kn.then_inc(kt_copied, 1)
                            else:
                                ins.then_inc(kt_copied, 1)
                    act.wait_ge(m_done, p + 1)
                    if p >= 1:
                        act.wait_ge(pt_done, 5 * p)
                    nc.scalar.activation(Pb[:, :], flat[:, 0:LK], ACT.Exp, bias=nm[:, 0:1], scale=AS,
                                         accum_out=sm[:, 0:1]).then_inc(e_done, 1)
                act.wait_ge(yt_done, 1)
                nc.scalar.copy(XT[:, :, SEQ:NTOK], ps[:, 0, :].rearrange("p (k t) -> p k t", k=KD)).then_inc(yt_copied, 1)
                act.wait_ge(yt_copied, 1)

            @block.vector
            def _(dve):
                link = chained(dve, dch)
                nc.vector.memset(qz[:, :, :, :, :], 0.0).then_inc(zeroed, 1)
                dve.wait_ge(cin, 48)
                link(nc.vector.tensor_copy(spb[:, :, :], spf[:, :, :]))
                dve.wait_ge(w_in, 128)
                for b in range(NB):
                    link(nc.vector.tensor_scalar(gw[:, b, :], gat[:, b, :], iwd[:, b:b + 1], IWS, ALU.mult, ALU.mult))
                dve.sem_inc(gw_done, 1)
                for b in range(NB):
                    for c, (c0, n) in enumerate(CHUNKS):
                        g = 5 * b + c
                        dve.wait_ge(dt_done, g + 1)
                        if g >= 2:
                            dve.wait_ge(sum_done, g - 1)
                        nc.vector.tensor_scalar(rel[:, g % 2, 0:n], ps[0:NS, 6 + g % 2, 0:n], 0.0, None, ALU.max).then_inc(dt_relu, 1)
                dve.wait_ge(sum_done, 5 * NB)
                link(nc.vector.tensor_copy(sc[:, 0:PAST], ps[0:NS, 0:4, :].rearrange("p b n -> p (b n)")))
                link(nc.vector.tensor_tensor(sc[:, PAST:LK], ps[0:NS, 4, 0:8], c8[:, :], ALU.add))
                for k in range(TOPK // 8):
                    src = sc if k == 0 else wk
                    link(nc.vector.max(m8[:, :], src[:, :]))
                    link(nc.vector.match_replace(wk[:, :], m8[:, :], src[:, :], TAKEN))
                nc.vector.tensor_scalar(bias[:, :], wk[:, :], -2e38, NEG, ALU.is_ge, ALU.mult).then_inc(b_done, 1)
                for p in range(NP_):
                    dve.wait_ge(s_done, p + 1)
                    link(nc.vector.reduce_max(mx[:, :], flat[:, 0:LK], AX_X))
                    if p >= 1:
                        dve.wait_ge(e_done, p)
                    nc.vector.tensor_scalar(nm[:, :], mx[:, :], -AS, None, ALU.mult).then_inc(m_done, 1)
                    if p >= 1:
                        dve.wait_ge(o_done, p)
                    for c in range(5):
                        g = 5 * p + c
                        dve.wait_ge(pt_done, g + 1)
                        if c < 4:
                            nc.vector.tensor_copy(PT[:, 4 * c:4 * c + 4, :],
                                                  ps[:, 5 + g % 2, :].rearrange("p (a t) -> p a t", a=4)).then_inc(pt_copied, 1)
                        else:
                            nc.vector.tensor_copy(PT[0:DEC_SEQ, PAGES, :], ps[0:DEC_SEQ, 5 + g % 2, 0:P]).then_inc(pt_copied, 1)
                    dve.wait_ge(e_done, p + 1)
                    link(nc.vector.reciprocal(rs[:, :], sm[:, :]))
                    dve.wait_ge(o_done, p + 1)
                    for b2 in range(2):
                        for kv in range(2):
                            r = slice(64 * b2 + 32 * kv, 64 * b2 + 32 * kv + 32)
                            ins = nc.vector.tensor_scalar(yq[r, p, :], ps[r, 7, kv * HD:(kv + 1) * HD], rs[r, 0:1],
                                                          None, ALU.mult)
                    ins.then_inc(y_done, 1)


class LayerNorm:

    def __init__(self, st, ctx, tag, l, which, X, A):
        nc = st.nc
        self.nc, self.X = nc, X
        self.src = [bcast_rows(A["ln_g"][l, which], D), bcast_rows(A["ln_b"][l, which], D)]
        sb = lambda n, s: ctx.enter_context(nc.sbuf_tensor(f"{tag}_{n}", s, F32))
        self.gb, self.stats, self.mv, self.rstd = (sb("gb", [P, 2, D]), sb("stats", [P, 2, 12]), sb("mv", [P, 2, 2]),
                                                   sb("rstd", [P, 2, 1]))
        self.gb_in, self.var_ready, self.std_ready, self.scaled, self.gained, self.norm_done = (
            st.sem(f"{tag}_{n}") for n in ("gb_in", "var_ready", "std_ready", "scaled", "gained", "norm_done"))

    def load(self, eng):
        for k in range(2):
            eng.dma_start(self.gb[:, k, :], self.src[k]).then_inc(self.gb_in, 16)

    def dve_stats(self, i, link):
        r, v, s = rows(i), self.nc.vector, i % 2
        for h in range(2):
            link(v.bn_stats(self.stats[0:r, s, 6 * h:6 * h + 6], self.X[0:r, i, 512 * h:512 * h + 512]))
        link(v.bn_aggr(self.mv[0:r, s, :], self.stats[0:r, s, :]))
        v.tensor_scalar(self.mv[0:r, s, 1:2], self.mv[0:r, s, 1:2], LN_EPS, None, ALU.add).then_inc(self.var_ready, 1)

    def act(self, act, i):
        r, s = rows(i), i % 2
        act.wait_ge(self.var_ready, i + 1)
        if i >= 2:
            act.wait_ge(self.scaled, i - 1)
        self.nc.scalar.activation(self.rstd[0:r, s, :], self.mv[0:r, s, 1:2], ACT.Sqrt).then_inc(self.std_ready, 1)

    def dve_scale(self, dve, i, link):
        r, s = rows(i), i % 2
        dve.wait_ge(self.std_ready, i + 1)
        link(self.nc.vector.reciprocal(self.rstd[0:r, s, :], self.rstd[0:r, s, :]))
        self.nc.vector.tensor_scalar(self.X[0:r, i, :], self.X[0:r, i, :], self.mv[0:r, s, 0:1], self.rstd[0:r, s, :],
                                     ALU.subtract, ALU.mult).then_inc(self.scaled, 1)

    def pool(self, pool, i):
        r = rows(i)
        if i == 0:
            pool.wait_ge(self.gb_in, 32)
        pool.wait_ge(self.scaled, i + 1)
        self.nc.gpsimd.tensor_tensor(self.X[0:r, i, :], self.X[0:r, i, :], self.gb[0:r, 0, :], ALU.mult).then_inc(self.gained, 1)
        pool.wait_ge(self.gained, i + 1)
        self.nc.gpsimd.tensor_tensor(self.X[0:r, i, :], self.X[0:r, i, :], self.gb[0:r, 1, :], ALU.add).then_inc(self.norm_done, 1)


def out_projection(nc, st, A, w, l, XT, x_prompt, x_sample, h_hi, h_lo):
    tag = f"out{l}"
    with ExitStack() as ctx:
        sem = lambda n: st.sem(f"{tag}_{n}")
        X = ctx.enter_context(nc.sbuf_tensor(f"{tag}_X", [P, TILES, D], F32))
        wbuf = ctx.enter_context(nc.sbuf_tensor(f"{tag}_w", [P, 2, KD, 512], F32))
        ps = ctx.enter_context(nc.psum_tensor(f"{tag}_ps", [P, 8, 512], F32))
        ln = LayerNorm(st, ctx, f"{tag}_ln", l, 0, X, A)
        w_in, x_in, saved = [sem("w_in0"), sem("w_in1")], sem("x_in"), sem("x_saved")
        mm_done, added, t_done, hi_done, lo_done, dch = (sem("mm_done"), sem("added"), sem("transposed"), sem("hi_done"),
                                                  sem("lo_done"), sem("dve_step"))
        w_v = w.rearrange("(k p) n -> p k n", p=P)
        with nc.Block() as block:
            @block.sync
            def _(sp):
                for c in range(2):
                    sp.dma_start(wbuf[:, c, :, :], w_v[:, :, 512 * c:512 * c + 512]).then_inc(w_in[c], 16)
                ln.load(sp)
                for i in range(TILES):
                    sp.wait_ge(ln.norm_done, i + 1)
                    sp.dma_start(st.x_dram[i * P:i * P + rows(i), :], X[0:rows(i), i, :]).then_inc(saved, 16)
                sp.wait_ge(saved, 16 * TILES)

            @block.tensor
            def _(pe):
                def transposes(i):
                    pe.wait_ge(ln.norm_done, i + 1)
                    for h in range(2):
                        j, r = 2 * i + h, rows(i)
                        if j >= 4:
                            pe.wait_ge(lo_done, j - 3)
                        for k in range(4):
                            kk = 4 * h + k
                            last = nc.tensor.transpose(ps[:, 4 + j % 4, k * P:k * P + r], X[0:r, i, kk * P:(kk + 1) * P],
                                                       st.ident[0:r, 0:r])
                        last.then_inc(t_done, 1)

                LAG = 2
                for i in range(TILES):
                    r = rows(i)
                    for c in range(2):
                        s = 2 * i + c
                        if i == 0:
                            pe.wait_ge(w_in[c], 16)
                        if s >= 4:
                            pe.wait_ge(added, s - 3)
                        for k in range(KD):
                            last = nc.tensor.matmul(ps[0:r, s % 4, :], XT[:, k, i * P:i * P + r], wbuf[:, c, k, :],
                                                    start=(k == 0), stop=(k == KD - 1))
                        last.then_inc(mm_done, 1)
                    if i >= LAG:
                        transposes(i - LAG)
                for i in range(TILES - LAG, TILES):
                    transposes(i)

            @block.scalar
            def _(act):
                def split_hi(i):
                    for h in range(2):
                        j, r = 2 * i + h, rows(i)
                        act.wait_ge(t_done, j + 1)
                        nc.scalar.copy(h_hi[:, 4 * h:4 * h + 4, i * P:i * P + r],
                                       ps[:, 4 + j % 4, :].rearrange("p (k t) -> p k t", k=4)[:, :, 0:r]).then_inc(hi_done, 1)

                for i in range(TILES):
                    ln.act(act, i)
                    if i >= 1:
                        split_hi(i - 1)
                split_hi(TILES - 1)

            @block.gpsimd
            def _(pool):
                pool.dma_start(X[:, 0:NT, :], x_prompt.rearrange("(i p) c -> p i c", p=P)).then_inc(x_in, 16)
                pool.dma_start(X[0:NS, NT, :], x_sample).then_inc(x_in, 16)
                for i in range(TILES):
                    ln.pool(pool, i)

            @block.vector
            def _(dve):
                link = chained(dve, dch)

                def split_lo(i):
                    for h in range(2):
                        j, r = 2 * i + h, rows(i)
                        at = (slice(None), slice(4 * h, 4 * h + 4), slice(i * P, i * P + r))
                        dve.wait_ge(hi_done, j + 1)
                        nc.vector.tensor_tensor(h_lo[at], ps[:, 4 + j % 4, :].rearrange("p (k t) -> p k t", k=4)[:, :, 0:r],
                                                h_hi[at].bitcast(F32), ALU.subtract).then_inc(lo_done, 1)

                dve.wait_ge(x_in, 32)
                for i in range(TILES):
                    r = rows(i)
                    for c in range(2):
                        s = 2 * i + c
                        dve.wait_ge(mm_done, s + 1)
                        xs = X[0:r, i, 512 * c:512 * c + 512]
                        nc.vector.scalar_tensor_tensor(out=xs, in0=xs, scalar=ALPHA, in1=ps[0:r, s % 4, :],
                                                       op0=ALU.mult, op1=ALU.add).then_inc(added, 1)
                    dve.wait_ge(added, 2 * i + 2)
                    ln.dve_stats(i, link)
                    if i >= 1:
                        ln.dve_scale(dve, i - 1, link)
                    if i >= 3:
                        split_lo(i - 3)
                ln.dve_scale(dve, TILES - 1, link)
                for i in range(TILES - 3, TILES):
                    split_lo(i)
                dve.wait_ge(lo_done, 2 * TILES)


TOKC = [(0, 384), (384, 384), (768, 320)]
NF = 256


def ffn_up(nc, st, w, tag, h_hi, h_lo, aT):
    w_v = w.rearrange("(k p) n -> p k n", p=P)
    with ExitStack() as ctx:
        sem = lambda n: st.sem(f"{tag}_{n}")
        raw = ctx.enter_context(nc.sbuf_tensor(f"{tag}_raw", [P, 2, KD, P], F32))
        w_hi = ctx.enter_context(nc.sbuf_tensor(f"{tag}_whi", [P, 2, KD, P], F32R))
        w_lo = ctx.enter_context(nc.sbuf_tensor(f"{tag}_wlo", [P, 2, KD, P], F32R))
        sg = ctx.enter_context(nc.sbuf_tensor(f"{tag}_sg", [P, 3, 384], F32))
        ps = ctx.enter_context(nc.psum_tensor(f"{tag}_ps", [P, 3, 2, 512], F32))
        w_in, w_split_hi, w_split = ([sem(f"{n}{k}") for k in range(2)] for n in ("w_in", "w_split_hi", "w_split"))
        mm_done = [sem("gate_done"), sem("up_done")]
        silu_done, prod_done = sem("silu_done"), sem("prod_done")
        with nc.Block() as block:
            @block.sync
            def _(sp):
                def load(ff, k2):
                    sp.dma_start(raw[:, k2, :, :], w_v[:, :, bass.ds(ff * P + k2 * D_FF, P)]).then_inc(w_in[k2], 16)
                load(0, 0)
                load(0, 1)
                with sp.Fori(1, KF) as ff:
                    for k2 in range(2):
                        sp.wait_ge(w_split[k2], ff)
                        load(ff, k2)

            @block.tensor
            def _(pe):
                def body(ff, first):
                    for k2 in range(2):
                        pe.wait_ge(w_split[k2], ff + 1)
                        for t, (t0, n) in enumerate(TOKC):
                            if not first:
                                pe.wait_ge((silu_done, prod_done)[k2], ff * 3 + (t - 2))
                            for k in range(KD):
                                parts = ((w_hi, h_hi), (w_hi, h_lo), (w_lo, h_hi))
                                for j, (wp, hp) in enumerate(parts):
                                    last = nc.tensor.matmul(ps[:, t, k2, 0:n], wp[:, k2, k, :], hp[:, k, t0:t0 + n],
                                                            start=(k == 0 and j == 0), stop=(k == KD - 1 and j == 2))
                            last.then_inc(mm_done[k2], 1)
                body(0, True)
                with pe.Fori(1, KF) as ff:
                    body(ff, False)

            @block.scalar
            def _(act):
                def split_hi(ff, k2, first):
                    act.wait_ge(w_in[k2], ff * 16 + 16)
                    if not first:
                        act.wait_ge(mm_done[k2], ff * 3)
                    nc.scalar.copy(w_hi[:, k2, :, :], raw[:, k2, :, :]).then_inc(w_split_hi[k2], 1)

                def body(ff, first, last):
                    for t, (t0, n) in enumerate(TOKC):
                        act.wait_ge(mm_done[0], ff * 3 + (t + 1))
                        if not first:
                            act.wait_ge(prod_done, ff * 3 + (t - 2))
                        nc.scalar.activation(sg[:, t, 0:n], ps[:, t, 0, 0:n], ACT.Silu).then_inc(silu_done, 1)
                    if not last:
                        split_hi(ff + 1, 0, False)
                        split_hi(ff + 1, 1, False)

                split_hi(0, 0, True)
                split_hi(0, 1, True)
                body(0, True, False)
                with act.Fori(1, KF - 1) as ff:
                    body(ff, False, False)
                body(KF - 1, False, True)

            @block.vector
            def _(dve):
                def split_lo(ff, k2):
                    dve.wait_ge(w_split_hi[k2], ff + 1)
                    nc.vector.tensor_tensor(w_lo[:, k2, :, :], raw[:, k2, :, :], w_hi[:, k2, :, :].bitcast(F32),
                                            ALU.subtract).then_inc(w_split[k2], 1)

                def body(ff, last):
                    if not last:
                        split_lo(ff + 1, 0)
                    for t, (t0, n) in enumerate(TOKC):
                        dve.wait_ge(silu_done, ff * 3 + (t + 1))
                        dve.wait_ge(mm_done[1], ff * 3 + (t + 1))
                        nc.vector.tensor_tensor(aT[:, bass.ds(ff, 1), t0:t0 + n].rearrange("p o n -> p (o n)"),
                                                sg[:, t, 0:n], ps[:, t, 1, 0:n], ALU.mult).then_inc(prod_done, 1)
                    if not last:
                        split_lo(ff + 1, 1)

                split_lo(0, 0)
                split_lo(0, 1)
                with dve.Fori(0, KF - 1) as ff:
                    body(ff, False)
                body(KF - 1, True)
                dve.wait_ge(prod_done, 3 * KF)


def ffn_down(nc, st, A, l, tag, aT, XT, y_out):
    NCH, KH = D // NF, KF // 2
    w_v = A["ffn_w_down"][l].rearrange("(k p) n -> p k n", p=P)
    with ExitStack() as ctx:
        sem = lambda n: st.sem(f"{tag}_{n}")
        X = ctx.enter_context(nc.sbuf_tensor(f"{tag}_X", [P, TILES, D], F32))
        wbuf = ctx.enter_context(nc.sbuf_tensor(f"{tag}_w", [P, KF, NF], F32))
        ps = ctx.enter_context(nc.psum_tensor(f"{tag}_ps", [P, 8, 512], F32))
        ln = LayerNorm(st, ctx, f"{tag}_ln", l, 1, X, A)
        w_in, w_used = [sem("w_in0"), sem("w_in1")], [sem("w_used0"), sem("w_used1")]
        mm_done, added, t_done, t_copied, dch = sem("mm_done"), sem("added"), sem("transposed"), sem("copied"), sem("dve_step")
        stored, x_in = sem("stored"), sem("x_in")

        def acc(i):
            return ps[0:rows(i), i // 2, (i % 2) * NF:(i % 2 + 1) * NF]

        def acc_last(i):
            return ps[0:rows(i), i % 5, 0:NF]

        with nc.Block() as block:
            @block.sync
            def _(sp):
                def load(c, h):
                    sp.dma_start(wbuf[:, h * KH:(h + 1) * KH, :], w_v[:, h * KH:(h + 1) * KH, bass.ds(c * NF, NF)]).then_inc(w_in[h], 16)
                load(0, 0)
                load(0, 1)
                ln.load(sp)
                with sp.Fori(1, NCH) as c:
                    for h in range(2):
                        sp.wait_ge(w_used[h], c)
                        load(c, h)
                for i in range(TILES):
                    sp.wait_ge(ln.norm_done, i + 1)
                    sp.dma_start(y_out(i), X[0:rows(i), i, :]).then_inc(stored, 16)
                sp.wait_ge(stored, 16 * TILES)

            @block.tensor
            def _(pe):
                def product(i, k):
                    return nc.tensor.matmul(acc(i), aT[:, k, i * P:i * P + rows(i)], wbuf[:, k, :],
                                            start=(k == 0 and i % 2 == 0), stop=(k == KF - 1), skip_group_check=True)

                def side_by_side(c, first):
                    for h in range(2):
                        pe.wait_ge(w_in[h], c * 16 + 16)
                        for k in range(h * KH, (h + 1) * KH):
                            for i in range(TILES):
                                if k == 0 and i % 2 == 0 and not first:
                                    pe.wait_ge(added, c * TILES + (min(i + 2, TILES) - TILES))
                                last = product(i, k)
                                if k == KF - 1:
                                    last.then_inc(mm_done, 1)
                        if h == 0:
                            last.then_inc(w_used[0], 1)
                    pe.wait_ge(mm_done, c * TILES + TILES)
                    pe.sem_inc(w_used[1], 1)

                side_by_side(0, True)
                with pe.Fori(1, NCH - 1) as c:
                    side_by_side(c, False)

                def transposes(i):
                    pe.wait_ge(ln.norm_done, i + 1)
                    for h in range(2):
                        j, r = 2 * i + h, rows(i)
                        if j >= 2:
                            pe.wait_ge(t_copied, j - 1)
                        for k in range(4):
                            kk = 4 * h + k
                            last = nc.tensor.transpose(ps[:, 6 + j % 2, k * P:k * P + r], X[0:r, i, kk * P:(kk + 1) * P],
                                                       st.ident[0:r, 0:r])
                        last.then_inc(t_done, 1)

                LAG = 2
                c = NCH - 1
                for h in range(2):
                    pe.wait_ge(w_in[h], c * 16 + 16)
                for i in range(TILES):
                    if i < 5:
                        pe.wait_ge(added, (c - 1) * TILES + min(2 * i + 2, TILES))
                    else:
                        pe.wait_ge(added, c * TILES + i - 4)
                    for k in range(KF):
                        last = nc.tensor.matmul(acc_last(i), aT[:, k, i * P:i * P + rows(i)], wbuf[:, k, :],
                                                start=(k == 0), stop=(k == KF - 1))
                    last.then_inc(mm_done, 1)
                    if XT is not None and i >= LAG:
                        transposes(i - LAG)
                if XT is not None:
                    for i in range(TILES - LAG, TILES):
                        transposes(i)

            @block.scalar
            def _(act):
                def copy_t(i):
                    for h in range(2):
                        j, r = 2 * i + h, rows(i)
                        act.wait_ge(t_done, j + 1)
                        nc.scalar.copy(XT[:, 4 * h:4 * h + 4, i * P:i * P + r],
                                       ps[:, 6 + j % 2, :].rearrange("p (k t) -> p k t", k=4)[:, :, 0:r]).then_inc(t_copied, 1)
                for i in range(TILES):
                    ln.act(act, i)
                    if XT is not None and i >= 1:
                        copy_t(i - 1)
                if XT is not None:
                    copy_t(TILES - 1)

            @block.gpsimd
            def _(pool):
                pool.dma_start(X[:, 0:NT, :], st.x_dram[0:SEQ, :].rearrange("(i p) c -> p i c", p=P)).then_inc(x_in, 16)
                pool.dma_start(X[0:NS, NT, :], st.x_dram[SEQ:NTOK, :]).then_inc(x_in, 16)
                for i in range(TILES):
                    ln.pool(pool, i)

            @block.vector
            def _(dve):
                link = chained(dve, dch)

                def add(c, i, acc):
                    xs = X[0:rows(i), i, bass.ds(c * NF, NF)]
                    nc.vector.scalar_tensor_tensor(out=xs, in0=xs, scalar=ALPHA, in1=acc(i), op0=ALU.mult,
                                                   op1=ALU.add).then_inc(added, 1)
                dve.wait_ge(x_in, 32)
                with dve.Fori(0, NCH - 1) as c:
                    for i in range(TILES):
                        dve.wait_ge(mm_done, c * TILES + min(i // 2 * 2 + 2, TILES))
                        add(c, i, acc)
                for i in range(TILES):
                    dve.wait_ge(mm_done, (NCH - 1) * TILES + i + 1)
                    add(NCH - 1, i, acc_last)
                    dve.wait_ge(added, (NCH - 1) * TILES + i + 1)
                    ln.dve_stats(i, link)
                    if i >= 1:
                        ln.dve_scale(dve, i - 1, link)
                ln.dve_scale(dve, TILES - 1, link)
                dve.wait_ge(ln.scaled, TILES)


SQ, SK, SV = 0, 1024, 1280
SCOLS = 1536


def swa_prompt(nc, st, A, C, O, H, XT):
    units = [(m, v) for m in range(2) for v in range(2)]
    NU = len(units)
    with ExitStack() as ctx:
        sb = lambda n, s, d=F32: ctx.enter_context(nc.sbuf_tensor(f"swa_{n}", s, d))
        sem = lambda n: st.sem(f"swa_{n}")
        cs = sb("cos", [P, TILES, 32])
        sn = sb("sin", [P, TILES, 32])
        xc, xs = sb("xc", [P, 2, 20, 2, 32]), sb("xs", [P, 2, 20, 2, 32])
        KT, qT = sb("KT", [P, 2, SEQ]), sb("qT", [P, 8, P])
        band_f, band, identb = sb("bandf", [P, 2 * P]), sb("band", [P, 2 * P], BF16), sb("identb", [P, P], BF16)
        sinks = sb("sinks", [P, 16])
        mx, nm, es, sm, rs = sb("mx", [P, 16]), sb("nm", [P, 16]), sb("es", [P, 16]), sb("sm", [P, 16]), sb("rs", [P, 16])
        Pb, PT = sb("P", [P, 2, 4, 2 * P]), sb("PT", [P, 2, 8, P])
        ps = ctx.enter_context(nc.psum_tensor("swa_ps", [P, 8, 512], F32))
        cin, rot_c, rot_s, rot_done, dch = sem("const_in"), sem("cos_done"), sem("sin_done"), sem("rotated"), sem("dve_step")
        t_done, t_copied = sem("transposed"), sem("transposed_copied")
        s_done, m_done, e_done, ds_done, es_done = sem("scores"), sem("max"), sem("probs"), sem("sink_diff"), sem("sink_exp")
        pt_done, pt_dve, pt_act, o_done = sem("p_transposed"), sem("p_copied_dve"), sem("p_copied_act"), sem("o")
        y_done, yt_done, yt_copied, stored = sem("y"), sem("yT"), sem("yT_copied"), sem("stored")
        const_ready = sem("const_ready")

        with nc.Block() as block:
            @block.sync
            def _(sp):
                for dst, src in ((cs[:, :, :], C["cos"]), (sn[:, :, :], C["sin"]), (band_f[:, :], C["band"]),
                                 (sinks[:, :], bcast_rows(A["swa_sinks"], 16))):
                    sp.dma_start(dst, src).then_inc(cin, 16)
                sp.wait_ge(rot_done, NT)
                sp.dma_start(O[6][0, 0].rearrange("w k d -> w (k d)"), H[:, NT - 1, SK:SK + 256]).then_inc(stored, 16)
                sp.dma_start(O[7][0, 0].rearrange("w k d -> w (k d)"), H[:, NT - 1, SV:SV + 256]).then_inc(stored, 16)
                sp.wait_ge(stored, 32)

            @block.gpsimd
            def _(pool):
                pool.wait_ge(cin, 64)
                for i in range(TILES):
                    r = rows(i)
                    if i >= 2:
                        pool.wait_ge(rot_done, i - 1)
                    x4 = H[0:r, i, SQ:SV].rearrange("p (h f d) -> p (h f) d", f=2, d=32)
                    nc.gpsimd.tensor_tensor(xs[0:r, i % 2, :, :, :].rearrange("p h f d -> p (h f) d"), x4,
                                            sn[0:r, i:i + 1, :].to_broadcast([r, 40, 32]), ALU.mult).then_inc(rot_s, 1)
                    pool.wait_ge(rot_s, i + 1)
                    pool.wait_ge(rot_c, i + 1)
                    x3 = H[0:r, i, SQ:SV].rearrange("p (h f d) -> p h f d", f=2, d=32)
                    nc.gpsimd.tensor_tensor(x3[:, :, 0, :], xc[0:r, i % 2, :, 0, :], xs[0:r, i % 2, :, 1, :], ALU.subtract)
                    nc.gpsimd.tensor_tensor(x3[:, :, 1, :], xc[0:r, i % 2, :, 1, :], xs[0:r, i % 2, :, 0, :], ALU.add).then_inc(rot_done, 1)

            @block.tensor
            def _(pe):
                pe.wait_ge(const_ready, 1)
                for i in range(NT):
                    T = H[:, i, :]
                    w, k0 = (P, P) if i == 0 else (2 * P, 0)
                    c0 = max(i - 1, 0) * P
                    pe.wait_ge(rot_done, i + 1)
                    if i >= 1:
                        pe.wait_ge(yt_copied, 2 * i)
                    for j in range(8):
                        nc.tensor.transpose(ps[:, 4 + j // 4, (j % 4) * P:(j % 4 + 1) * P], T[:, SQ + j * P:SQ + (j + 1) * P],
                                            st.ident[:, :])
                    if i >= 1:
                        pe.wait_ge(y_done, i)
                    for m in range(2):
                        last = nc.tensor.transpose(ps[:, 6, m * P:(m + 1) * P], T[:, SK + m * P:SK + (m + 1) * P], st.ident[:, :])
                    last.then_inc(t_done, 1)
                    pe.wait_ge(t_copied, 3 * (i + 1))

                    def scores(u):
                        m, v = units[u]
                        a, hf = i * NU + u, slice(64 * v, 64 * v + 64)
                        if a >= 2:
                            pe.wait_ge(e_done, a - 1)
                        for b in range(2):
                            o2 = ps[:, 2 * v + b, 0:2 * w]
                            nc.tensor.matmul(o2.rearrange("p (a n) -> p a n", a=2), identb[:, :],
                                             band[:, k0:k0 + w].unsqueeze(1).to_broadcast([P, 2, w]), start=True, stop=False,
                                             skip_group_check=True)
                            for g2 in range(2):
                                last = nc.tensor.matmul(o2[:, g2 * w:(g2 + 1) * w], qT[hf, 4 * m + 2 * b + g2, :],
                                                        KT[hf, m, c0:c0 + w], start=False, stop=True, skip_group_check=True)
                        last.then_inc(s_done, 1)

                    def attend(u):
                        m, v = units[u]
                        a = i * NU + u
                        pe.wait_ge(e_done, a + 1)
                        if a >= 1:
                            pe.wait_ge(pt_dve, a)
                            pe.wait_ge(pt_act, a)
                        nb = w // P
                        for g in range(4):
                            for b in range(nb):
                                last = nc.tensor.transpose(ps[:, 4 + g // 2, ((g % 2) * nb + b) * P:((g % 2) * nb + b + 1) * P],
                                                           Pb[:, a % 2, g, b * P:(b + 1) * P], st.ident[:, :])
                        last.then_inc(pt_done, 1)
                        pe.wait_ge(pt_dve, a + 1)
                        pe.wait_ge(pt_act, a + 1)
                        for g in range(4):
                            h = (2 * m + v) * 4 + g
                            for b in range(nb):
                                last = nc.tensor.matmul(ps[:, 6 + m, (h % 8) * HD:(h % 8 + 1) * HD], PT[:, a % 2, g * nb + b, :],
                                                        H[:, c0 // P + b, SV + (2 * m + v) * HD:SV + (2 * m + v + 1) * HD],
                                                        start=(b == 0), stop=(b == nb - 1))
                        last.then_inc(o_done, 1)

                    scores(0)
                    for u in range(NU):
                        if u + 1 < NU:
                            scores(u + 1)
                        attend(u)
                    pe.wait_ge(y_done, i + 1)
                    for k in range(KD):
                        last = nc.tensor.transpose(ps[:, 4 + k // 4, (k % 4) * P:(k % 4 + 1) * P], T[:, k * P:(k + 1) * P],
                                                   st.ident[:, :])
                        if k % 4 == 3:
                            last.then_inc(yt_done, 1)

            @block.scalar
            def _(act):
                for i in range(NT):
                    nb = 1 if i == 0 else 2
                    act.wait_ge(t_done, i + 1)
                    for j in range(2):
                        nc.scalar.copy(qT[:, 4 * j:4 * j + 4, :], ps[:, 4 + j, :].rearrange("p (a t) -> p a t", a=4)).then_inc(t_copied, 1)
                    nc.scalar.copy(KT[:, :, i * P:(i + 1) * P], ps[:, 6, 0:2 * P].rearrange("p (a t) -> p a t", a=2)).then_inc(t_copied, 1)

                    def exps(u):
                        m, v = units[u]
                        a = i * NU + u
                        act.wait_ge(m_done, a + 1)
                        if a >= 2:
                            act.wait_ge(pt_done, a - 1)
                        for g in range(4):
                            h = 4 * (2 * m + v) + g
                            w = nb * P
                            ins = nc.scalar.activation(Pb[:, a % 2, g, 0:w], ps[:, 2 * v + g // 2, (g % 2) * w:(g % 2 + 1) * w],
                                                       ACT.Exp, bias=nm[:, h:h + 1], scale=AS, accum_out=sm[:, h:h + 1])
                        ins.then_inc(e_done, 1)

                    def copy_pt(u):
                        a = i * NU + u
                        if a >= 2:
                            act.wait_ge(o_done, a - 1)
                        act.wait_ge(pt_done, a + 1)
                        nc.scalar.copy(PT[:, a % 2, 2 * nb:4 * nb, :],
                                       ps[:, 5, 0:2 * nb * P].rearrange("p (a t) -> p a t", t=P)).then_inc(pt_act, 1)

                    exps(0)
                    for u in range(NU):
                        if u + 1 < NU:
                            exps(u + 1)
                        copy_pt(u)
                    act.wait_ge(ds_done, i + 1)
                    nc.scalar.activation(es[:, :], es[:, :], ACT.Exp).then_inc(es_done, 1)
                    for k in range(2):
                        act.wait_ge(yt_done, 2 * i + k + 1)
                        nc.scalar.copy(XT[:, 4 * k:4 * k + 4, i * P:(i + 1) * P],
                                       ps[:, 4 + k, :].rearrange("p (a t) -> p a t", a=4)).then_inc(yt_copied, 1)

            @block.vector
            def _(dve):
                link = chained(dve, dch)
                dve.wait_ge(cin, 64)
                link(nc.vector.tensor_copy(identb[:, :], st.ident[:, :]))
                link(nc.vector.tensor_copy(band[:, :], band_f[:, :]))
                dve.sem_inc(const_ready, 1)

                def rotate(i):
                    r = rows(i)
                    if i >= 2:
                        dve.wait_ge(rot_done, i - 1)
                    nc.vector.tensor_tensor(xc[0:r, i % 2, :, :, :].rearrange("p h f d -> p (h f) d"),
                                            H[0:r, i, SQ:SV].rearrange("p (h d) -> p h d", d=32),
                                            cs[0:r, i:i + 1, :].to_broadcast([r, 40, 32]), ALU.mult).then_inc(rot_c, 1)

                rotate(0)
                rotate(1)
                for i in range(NT):
                    nb = 1 if i == 0 else 2
                    w = nb * P

                    def row_max(u):
                        m, v = units[u]
                        a, h0 = i * NU + u, 4 * (2 * m + v)
                        h4 = slice(h0, h0 + 4)
                        dve.wait_ge(s_done, a + 1)
                        if nb == 2:
                            link(nc.vector.reduce_max(mx[:, h4], ps[:, 2 * v:2 * v + 2, :].rearrange("p b (g n) -> p (b g) n", g=2), AX_X))
                        else:
                            for b in range(2):
                                link(nc.vector.reduce_max(mx[:, h0 + 2 * b:h0 + 2 * b + 2],
                                                          ps[:, 2 * v + b, 0:2 * w].rearrange("p (g n) -> p g n", g=2), AX_X))
                        link(nc.vector.scalar_tensor_tensor(out=mx[:, h4], in0=mx[:, h4], scalar=AS, in1=sinks[:, h4],
                                                            op0=ALU.mult, op1=ALU.max))
                        nc.vector.tensor_scalar(nm[:, h4], mx[:, h4], -1.0, None, ALU.mult).then_inc(m_done, 1)

                    def copy_pt(u):
                        a = i * NU + u
                        if a >= 2:
                            dve.wait_ge(o_done, a - 1)
                        dve.wait_ge(pt_done, a + 1)
                        nc.vector.tensor_copy(PT[:, a % 2, 0:2 * nb, :],
                                              ps[:, 4, 0:2 * nb * P].rearrange("p (a t) -> p a t", t=P)).then_inc(pt_dve, 1)

                    if i >= 1:
                        dve.wait_ge(e_done, i * NU)
                        dve.wait_ge(y_done, i)
                    row_max(0)
                    for u in range(NU):
                        if u + 1 < NU:
                            row_max(u + 1)
                        if u == 2 and i + 2 < TILES:
                            rotate(i + 2)
                        copy_pt(u)
                    nc.vector.tensor_tensor(es[:, :], sinks[:, :], mx[:, :], ALU.subtract).then_inc(ds_done, 1)
                    dve.wait_ge(es_done, i + 1)
                    dve.wait_ge(e_done, (i + 1) * NU)
                    link(nc.vector.tensor_tensor(rs[:, :], sm[:, :], es[:, :], ALU.add))
                    link(nc.vector.reciprocal(rs[:, :], rs[:, :]))
                    dve.wait_ge(o_done, (i + 1) * NU)
                    for m in range(2):
                        ins = nc.vector.tensor_tensor(
                            H[:, i, SQ + 512 * m:SQ + 512 * m + 512].rearrange("p (h d) -> p h d", d=HD),
                            ps[:, 6 + m, :].rearrange("p (h d) -> p h d", d=HD),
                            rs[:, 8 * m:8 * m + 8].unsqueeze(2).to_broadcast([P, 8, HD]), ALU.mult)
                    ins.then_inc(y_done, 1)
                dve.wait_ge(y_done, NT)
                dve.wait_ge(rot_done, TILES)


def swa_sample(nc, st, A, C, O, H, XT):
    NB, NK = DEC_BATCH, P + DEC_SEQ
    scr = nc.dram_tensor("scratch_ys", (NS, D), F32, kind="Internal").ap()
    T = H[:, NT, :]
    with ExitStack() as ctx:
        sb = lambda n, s, d=F32: ctx.enter_context(nc.sbuf_tensor(f"sws_{n}", s, d))
        sem = lambda n: st.sem(f"sws_{n}")
        Kb, Vb, Vn = sb("Kb", [P, NB, 256]), sb("Vb", [P, NB, 256]), sb("Vn", [DEC_SEQ, NB, 256])
        KT, kn = sb("KT", [P, NB, 2, NK]), sb("kn", [P, 2, NS])
        qz = sb("qz", [P, NB, 2, 2, 4, DEC_SEQ])
        band_f, band, identb = sb("bandf", [P, NK]), sb("band", [P, NK], BF16), sb("identb", [P, P], BF16)
        sink = sb("sink", [P, 1])
        mx, nm, es, sm, rs = (sb(n, [P, NB]) for n in ("mx", "nm", "es", "sm", "rs"))
        Pb, PT = sb("P", [P, NB, NK]), sb("PT", [P, NB, P])
        PTn = sb("PTn", [DEC_SEQ, NB, P])
        yq, Y = sb("yq", [P, NB, HD]), sb("Y", [NS, D])
        ps = ctx.enter_context(nc.psum_tensor("sws_ps", [P, 8, 512], F32))
        buf_in, cin, vn_in, ready, dch = sem("buffers_in"), sem("const_in"), sem("v_new_in"), sem("ready"), sem("dve_step")
        q_done, q_copied, k_done, k_copied = sem("qT"), sem("qT_copied"), sem("kT"), sem("kT_copied")
        s_done, m_done, e_done, pt_done, pt_copied = sem("scores"), sem("max"), sem("probs"), sem("pT"), sem("pT_copied")
        o_done, y_done, y_out, y_in, yt_done, yt_copied, stored = (sem("o"), sem("y"), sem("y_out"), sem("y_in"), sem("yT"),
                                                                   sem("yT_copied"), sem("stored"))

        def score(b, n=NK):
            return ps[:, b // 3, (b % 3) * NK:(b % 3) * NK + n]

        with nc.Block() as block:
            @block.sync
            def _(sp):
                sp.dma_start(Kb[:, :, :], A["state_swa_k"][0].rearrange("b w k d -> w b (k d)")).then_inc(buf_in, 16)
                sp.dma_start(Vb[:, :, :], A["state_swa_v"][0].rearrange("b w k d -> w b (k d)")).then_inc(buf_in, 16)
                sp.dma_start(band_f[:, :], C["bands"]).then_inc(cin, 16)
                sp.dma_start(sink[:, :], bass.AP(A["swa_sinks"].tensor, 0, [[1, 16], [0, DEC_SEQ], [1, 1]]),
                             allow_slow_non_contiguous=True).then_inc(cin, 16)
                for b in range(NB):
                    sp.dma_start(Vn[:, b, :], T[8 * b:8 * b + 8, SV:SV + 256]).then_inc(vn_in, 16)
                for o, src, c in ((O[12], A["state_swa_k"], SK), (O[13], A["state_swa_v"], SV)):
                    sp.dma_start(o[0, :, 0:P - DEC_SEQ].rearrange("b w k d -> b (w k d)"),
                                 src[0, :, DEC_SEQ:P].rearrange("b w k d -> b (w k d)")).then_inc(stored, 16)
                    for b in range(NB):
                        sp.dma_start(o[0, b, P - DEC_SEQ:P].rearrange("w k d -> w (k d)"), T[8 * b:8 * b + 8, c:c + 256]).then_inc(stored, 16)
                sp.wait_ge(y_done, 1)
                for b in range(NB):
                    sp.dma_start(bass.AP(scr.tensor, b * DEC_SEQ * D, [[HD, 16], [D, DEC_SEQ], [1, HD]]), yq[:, b, :]).then_inc(y_out, 16)
                sp.wait_ge(y_out, 16 * NB)
                sp.dma_start(Y[:, :], scr).then_inc(y_in, 16)
                sp.wait_ge(stored, 32 + 32 * NB)

            @block.tensor
            def _(pe):
                I64 = st.ident[0:NS, 0:NS]
                for j in range(8):
                    nc.tensor.transpose(ps[:, 3, j * NS:(j + 1) * NS], T[0:NS, SQ + j * P:SQ + (j + 1) * P], I64)
                for m in range(2):
                    last = nc.tensor.transpose(ps[:, 4, m * NS:(m + 1) * NS], T[0:NS, SK + m * P:SK + (m + 1) * P], I64)
                last.then_inc(q_done, 1)
                pe.wait_ge(buf_in, 32)
                for b in range(0, NB, 2):
                    g = b // 2
                    if g >= 2:
                        pe.wait_ge(k_copied, g - 1)
                    for j in range(4):
                        last = nc.tensor.transpose(ps[:, 6 + g % 2, j * P:(j + 1) * P],
                                                   Kb[:, b + j // 2, (j % 2) * P:(j % 2 + 1) * P], st.ident[:, :])
                    last.then_inc(k_done, 1)
                pe.wait_ge(k_copied, NB // 2 + 1)
                pe.wait_ge(q_copied, 3)
                pe.wait_ge(ready, 1)
                for b in range(NB):
                    nc.tensor.matmul(score(b), identb[:, :], band[:, :], start=True, stop=False, skip_group_check=True)
                    for m in range(2):
                        last = nc.tensor.matmul(score(b)[64 * m:64 * m + 64, :],
                                                qz[:, b, m, :, :, :].rearrange("d v g q -> d (v g q)"), KT[:, b, m, :],
                                                start=False, stop=True, skip_group_check=True)
                last.then_inc(s_done, 1)
                pe.wait_ge(e_done, 1)
                for b in range(NB):
                    nc.tensor.transpose(ps[:, 3 + b // 4, (b % 4) * P:(b % 4 + 1) * P], Pb[:, b, 0:P], st.ident[:, :])
                for b in range(NB):
                    last = nc.tensor.transpose(ps[0:DEC_SEQ, 6 + b // 4, (b % 4) * P:(b % 4 + 1) * P], Pb[:, b, P:NK], st.ident[:, :])
                last.then_inc(pt_done, 1)
                pe.wait_ge(pt_copied, 2)
                pe.wait_ge(vn_in, 16 * NB)
                for b in range(NB):
                    for m in range(2):
                        r = slice(64 * m, 64 * m + 64)
                        o = ps[r, b // 4, (b % 4) * P:(b % 4 + 1) * P]
                        nc.tensor.matmul(o, PT[:, b, r], Vb[:, b, m * P:(m + 1) * P], start=True, stop=False)
                        last = nc.tensor.matmul(o, PTn[:, b, r], Vn[:, b, m * P:(m + 1) * P], start=False, stop=True)
                last.then_inc(o_done, 1)
                pe.wait_ge(y_in, 16)
                for k in range(KD):
                    last = nc.tensor.transpose(ps[:, 5, k * NS:(k + 1) * NS], Y[:, k * P:(k + 1) * P], I64)
                last.then_inc(yt_done, 1)

            @block.scalar
            def _(act):
                act.wait_ge(q_done, 1)
                act.wait_ge(ready, 1)
                for v in range(2):
                    hf = slice(64 * v, 64 * v + 64)
                    for m in range(2):
                        ins = nc.scalar.copy(qz[hf, :, m, v, :, :].rearrange("d b g q -> d g b q"),
                                             ps[hf, 3, 4 * m * NS:4 * (m + 1) * NS].rearrange("d (g b q) -> d g b q", g=4, b=NB))
                    ins.then_inc(q_copied, 1)
                nc.scalar.copy(kn[:, :, :], ps[:, 4, 0:2 * NS].rearrange("p (m t) -> p m t", m=2)).then_inc(q_copied, 1)
                act.wait_ge(q_copied, 3)
                for m in range(2):
                    ins = nc.scalar.copy(KT[:, :, m, P:NK], kn[:, m, :].rearrange("p (b q) -> p b q", b=NB))
                for g in range(NB // 2):
                    act.wait_ge(k_done, g + 1)
                    ins = nc.scalar.copy(KT[:, 2 * g:2 * g + 2, :, 0:P],
                                         ps[:, 6 + g % 2, :].rearrange("p (b m t) -> p b m t", b=2, m=2))
                    ins.then_inc(k_copied, 1)
                act.wait_ge(k_copied, NB // 2)
                act.sem_inc(k_copied, 1)
                act.wait_ge(m_done, 1)
                nc.scalar.activation(es[:, :], es[:, :], ACT.Exp)
                for b in range(NB):
                    ins = nc.scalar.activation(Pb[:, b, :], score(b), ACT.Exp, bias=nm[:, b:b + 1], scale=AS,
                                               accum_out=sm[:, b:b + 1])
                ins.then_inc(e_done, 1)
                act.wait_ge(pt_done, 1)
                nc.scalar.copy(PTn[:, :, :], ps[0:DEC_SEQ, 6:8, :].rearrange("p c (b t) -> p (c b) t", b=4)).then_inc(pt_copied, 1)
                act.wait_ge(yt_done, 1)
                nc.scalar.copy(XT[:, :, SEQ:NTOK], ps[:, 5, :].rearrange("p (k t) -> p k t", k=KD)).then_inc(yt_copied, 1)
                act.wait_ge(yt_copied, 1)

            @block.vector
            def _(dve):
                link = chained(dve, dch)
                link(nc.vector.memset(qz[:, :, :, :, :, :], 0.0))
                link(nc.vector.tensor_copy(identb[:, :], st.ident[:, :]))
                dve.wait_ge(cin, 32)
                nc.vector.tensor_copy(band[:, :], band_f[:, :]).then_inc(ready, 1)
                dve.wait_ge(s_done, 1)
                for c in range(3):
                    n = 3 if c < 2 else 2
                    link(nc.vector.reduce_max(mx[:, 3 * c:3 * c + n],
                                              ps[:, c, 0:n * NK].rearrange("p (b n) -> p b n", n=NK), AX_X))
                link(nc.vector.tensor_scalar(mx[:, :], mx[:, :], AS, sink[:, 0:1], ALU.mult, ALU.max))
                link(nc.vector.tensor_scalar(nm[:, :], mx[:, :], -1.0, None, ALU.mult))
                nc.vector.tensor_scalar(es[:, :], nm[:, :], sink[:, 0:1], None, ALU.add).then_inc(m_done, 1)
                dve.wait_ge(pt_done, 1)
                nc.vector.tensor_copy(PT[:, :, :], ps[:, 3:5, :].rearrange("p c (b t) -> p (c b) t", b=4)).then_inc(pt_copied, 1)
                dve.wait_ge(e_done, 1)
                link(nc.vector.tensor_tensor(rs[:, :], sm[:, :], es[:, :], ALU.add))
                link(nc.vector.reciprocal(rs[:, :], rs[:, :]))
                dve.wait_ge(o_done, 1)
                for kv in range(4):
                    r, v = slice(32 * kv, 32 * kv + 32), kv % 2
                    ins = nc.vector.tensor_tensor(
                        yq[r, :, :], ps[r, 0:2, :].rearrange("p c (b d) -> p (c b) d", b=4)[:, :, v * HD:(v + 1) * HD],
                        rs[r, :].unsqueeze(2).to_broadcast([32, NB, HD]), ALU.mult)
                ins.then_inc(y_done, 1)


def block_end(nc, st, A, l, XT, xt_place, x_prompt, x_sample, y_out):
    last = l == 1
    hs, at = ExitStack(), ExitStack()
    h_hi, h_lo = (hs.enter_context(nc.sbuf_tensor(f"h{l}_{n}", [P, KD, NTOK], F32R)) for n in ("hi", "lo"))
    out_projection(nc, st, A, A["w_out_even" if l == 0 else "w_out_odd"][0], l, XT, x_prompt, x_sample, h_hi, h_lo)
    xt_place.close()
    aT = at.enter_context(nc.sbuf_tensor(f"aT{l}", [P, KF, NTOK], F32, side="right"))
    ffn_up(nc, st, A["ffn_w_gu"][l], f"ffn{l}u", h_hi, h_lo, aT)
    hs.close()
    place, XT = ExitStack(), None
    if not last:
        XT = place.enter_context(nc.sbuf_tensor("XT_odd", [P, KD, NTOK], F32))
    ffn_down(nc, st, A, l, f"ffn{l}d", aT, XT, y_out)
    at.close()
    st.end_phase()
    return XT, place


def rest(nc, st, A, C, O, XT, xt_place):
    def y_rows(i):
        if i < NT:
            return O[0][0, i * P:(i + 1) * P, :]
        return O[1].rearrange("b s d -> (b s) d")

    XT, place = block_end(nc, st, A, 0, XT, xt_place, A["x_prompt"][0], A["x_sample"].rearrange("b s d -> (b s) d"),
                          lambda i: st.x_dram[i * P:i * P + rows(i), :])
    yt_place = ExitStack()
    YT = yt_place.enter_context(nc.sbuf_tensor("YT_odd", [P, KD, NTOK], F32, side="right"))
    with ExitStack() as mix:
        H = mix.enter_context(nc.sbuf_tensor("H1", [P, TILES, SCOLS], F32, side="right"))
        in_projection(nc, st, None, A["w_in_odd"][0], ODD_CHUNKS, XT, lambda i: H[:, i, :], [], "ino", False)
        place.close()
        swa_prompt(nc, st, A, C, O, H, YT)
        swa_sample(nc, st, A, C, O, H, YT)
        st.end_phase()
    block_end(nc, st, A, 1, YT, yt_place, st.x_dram[0:SEQ, :], st.x_dram[SEQ:NTOK, :], y_rows)
class State:

    def __init__(self, nc, ctx):
        self.nc, self.ctx = nc, ctx
        self.x_dram = nc.dram_tensor("scratch_x", (NTOK, D), F32, kind="Internal").ap()
        self.phase_sems = []

    def sem(self, name):
        s = self.nc.alloc_semaphore(name=name)
        self.phase_sems.append(s)
        return s

    def end_phase(self):
        self.nc.clear_and_free_semaphores(self.phase_sems)
        self.nc.all_engine_barrier()
        self.phase_sems = []

    def sbuf(self, name, shape, dt=F32):
        return self.ctx.enter_context(self.nc.sbuf_tensor(name, shape, dt))



def build(nc, A, C, O):
    with ExitStack() as ctx:
        st = State(nc, ctx)
        st.ident = st.sbuf("ident", [P, P])
        s_c = st.sem("const_in")
        with nc.Block() as block:
            @block.sync
            def _(sp):
                sp.dma_start(st.ident[:, :], C["ident"]).then_inc(s_c, 16)
                sp.wait_ge(s_c, 16)
        xt_place = ExitStack()
        XT = xt_place.enter_context(nc.sbuf_tensor("XT", [P, KD, NTOK], F32, side="right"))

        def x_rows(i):
            if i < NT:
                return A["x_prompt"][0, i * P:(i + 1) * P, :]
            return A["x_sample"].rearrange("b s d -> (b s) d")

        with ExitStack() as mix:
            Hs = mix.enter_context(nc.sbuf_tensor("Hs", [P, C_END], F32))
            with ExitStack() as mixp:
                H = mixp.enter_context(nc.sbuf_tensor("H", [P, NT, C_END], F32))
                stores = []
                for out_p, out_s, a, b in ((O[2], O[8], C_DK, C_DV), (O[3], O[9], C_DV, C_IK), (O[4], O[10], C_IK, C_IK + HD)):
                    fl = "o b t k d -> (o b t) (k d)" if len(out_p.shape) == 5 else "o b t d -> (o b t) d"
                    stores.append((out_p.rearrange(fl).rearrange("(i p) c -> p i c", p=P), H[:, :, a:b]))
                    stores.append((out_s.rearrange(fl), Hs[0:NS, a:b]))
                in_projection(nc, st, x_rows, A["w_in_even"][0], EVEN_CHUNKS, XT,
                              lambda i: H[:, i, :] if i < NT else Hs[:, :], stores, "ine", True)
                st.end_phase()
                gla(nc, st, A, C, O, H, Hs)
                st.end_phase()
                dsa_prompt(nc, st, A, C, O, H, Hs, XT)
            st.end_phase()
            dsa_sample(nc, st, A, C, O, Hs, XT)
            st.end_phase()
        rest(nc, st, A, C, O, XT, xt_place)


_INS = ["x_prompt", "x_sample", "cache_k", "cache_v", "cache_idx", "state_gla", "state_swa_k", "state_swa_v",
        "page_table", "w_in_even", "gla_gate_w2", "gla_gate_b", "gla_norm_g", "w_out_even", "w_in_odd", "swa_sinks",
        "w_out_odd", "ffn_w_gu", "ffn_w_down", "ln_g", "ln_b"]
_OUTS = [(1, 1024, 1024), (8, 8, 1024), (1, 1, 1024, 2, 64), (1, 1, 1024, 2, 64), (1, 1, 1024, 64), (1, 1, 4, 64, 128),
         (1, 1, 128, 4, 64), (1, 1, 128, 4, 64), (1, 8, 8, 2, 64), (1, 8, 8, 2, 64), (1, 8, 8, 64), (1, 8, 4, 64, 128),
         (1, 8, 128, 4, 64), (1, 8, 128, 4, 64)]


def shape_constants():
    import numpy as np
    c = {"ident": np.eye(128, dtype=np.float32)}
    s, t = np.arange(128)[:, None], np.arange(128)[None, :]
    lev = [(s == t)]
    for n in range(7):
        L = 2 ** n
        lev.append((s // (2 * L) == t // (2 * L)) & (s // L % 2 == 0) & (t // L % 2 == 1))
    c["levels"] = np.stack(lev, 1).astype(np.float32)
    reset = np.ones((128, 192), np.float32)
    reset[:, 128:192:8] = 0.0
    c["reset"] = reset
    c["batchsel"] = (np.arange(64)[:, None] // 8 == np.arange(8)[None, :]).astype(np.float32)
    c["causal"] = np.where(t <= s, 0.0, -1e30).astype(np.float32)
    qi, ki = np.arange(64)[:, None], np.arange(8)[None, :]
    c["causal8"] = np.where(ki <= qi % 8, 0.0, -1e30).astype(np.float32)
    sp = np.zeros((64, 4, 128), np.float32)
    for pair in range(4):
        for r in range(128):
            sp[(2 * pair + r // 64) * 8 + r % 8, pair, r] = 1.0
    c["spread"] = sp
    gat = np.zeros((64, 8, 64), np.float32)
    for b in range(8):
        for r in range(64):
            gat[r, b, b * 8 + r % 8] = 1.0
    c["gather"] = gat
    a, k2 = np.arange(128)[:, None], np.arange(256)[None, :]
    c["band"] = np.where((k2 > a) & (k2 <= a + 128), 0.0, -1e30).astype(np.float32)
    q8, k136 = (np.arange(128) % 8)[:, None], np.arange(136)[None, :]
    c["bands"] = np.where((k136 > q8) & (k136 <= q8 + 128), 0.0, -1e30).astype(np.float32)
    pos = np.concatenate([np.arange(1024), 2048 + np.arange(64) % 8, np.zeros(64)]).astype(np.float32)
    inv = (np.float32(150000.0) ** (-np.arange(32, dtype=np.float32) / np.float32(32))).astype(np.float32)
    ang = pos[:, None] * inv[None, :]
    c["cos"] = np.cos(ang).astype(np.float32).reshape(9, 128, 32).transpose(1, 0, 2)
    c["sin"] = np.sin(ang).astype(np.float32).reshape(9, 128, 32).transpose(1, 0, 2)
    return c


def kernel(**inputs):
    import numpy as _np
    import concourse.bacc as _bacc
    from concourse import mybir as _mybir
    from concourse.bass_utils import run_bass_kernel_spmd as _run

    nc = _bacc.Bacc("TRN2", target_bir_lowering=False, num_devices=1)
    arrays, A, C, O = {}, {}, {}, []
    for name in _INS:
        a = _np.ascontiguousarray(inputs[name])
        arrays[f"in_{name}_dram"] = a
        A[name] = nc.dram_tensor(f"in_{name}_dram", a.shape, _mybir.dt.from_np(a.dtype), kind="ExternalInput").ap()
    for name, a in shape_constants().items():
        a = _np.ascontiguousarray(a)
        arrays[f"const_{name}"] = a
        C[name] = nc.dram_tensor(f"const_{name}", a.shape, _mybir.dt.from_np(a.dtype), kind="ExternalInput").ap()
    for i, shape in enumerate(_OUTS):
        O.append(nc.dram_tensor(f"out_{i}_dram", shape, F32, kind="ExternalOutput").ap())
    build(nc, A, C, O)
    r = _run(nc, [arrays], core_ids=[0])
    return tuple(r.results[0][f"out_{i}_dram"] for i in range(len(_OUTS)))
```

```python
from contextlib import ExitStack
import math

import concourse.bass as bass
from concourse import mybir

ALU = mybir.AluOpType
ACT = mybir.ActivationFunctionType
AX_X = mybir.AxisListType.X
F32 = mybir.dt.float32
F32R = mybir.dt.float32r
BF16 = mybir.dt.bfloat16
I32 = mybir.dt.int32
U8 = mybir.dt.uint8

P = 128
D = 1024
KD = D // P
SEQ, DEC_BATCH, DEC_SEQ = 1024, 8, 8
NS = DEC_BATCH * DEC_SEQ
NT = SEQ // P
NTOK = SEQ + NS
TILES = NT + 1
ALPHA = 4.0 ** 0.25
LN_EPS, RMS_EPS = 1e-5, 1e-6
GLA_H, DK, DV, TAU = 4, 64, 128, 16.0
HD = 64
W_GQ, W_GK, W_GV, W_GR, W_GG, W_DQ, W_DK, W_DV, W_IQ, W_IK, W_IW, W_END = (
    0, 256, 512, 1024, 1536, 1552, 2064, 2192, 2320, 2832, 2896, 2904)
C_GQ, C_GK, C_GV, C_GR, C_DQ, C_IQ, C_GG, C_DK, C_DV, C_IK, C_IW, C_END = (
    0, 256, 512, 1024, 1536, 2048, 2560, 2576, 2704, 2832, 2960, 2968)
D_FF = 2816
KF = D_FF // P

def rows(i):
    return P if i < NT else NS

def bcast_rows(ap1d, n, parts=P):
    return bass.AP(ap1d.tensor, ap1d.offset, [[0, parts], [1, n]])

def by_group(start):
    return [((g * 2 + kv) * HD, start + (kv * 4 + g) * HD, HD) for g in range(4) for kv in range(2)]

EVEN_CHUNKS = [[(0, W_GQ, 512)], [(0, W_GV, 512)], [(0, W_GR, 512)], by_group(W_DQ), [(0, W_IQ, 512)],
               [(0, W_GG, 16), (C_DK - C_GG, W_DK, 256), (C_IK - C_GG, W_IK, 64), (C_IK + 64 - C_GG, W_IK, 72)]]
ODD_CHUNKS = [by_group(0), by_group(512), [(0, 1024, 512)]]

NP = 256
RING = 4


def halved(chunks):
    cut = []
    for pieces in chunks:
        for h0 in range(0, 512, NP):
            part = [(max(a, h0) - h0, b + max(a, h0) - a, min(a + n, h0 + NP) - max(a, h0)) for a, b, n in pieces
                    if max(a, h0) < min(a + n, h0 + NP)]
            if part:
                cut.append(part)
    return cut


def in_projection(nc, st, x_tile, w, chunks, XT, dest, stores, tag):
    chunks = halved(chunks)
    NCH, NB = len(chunks), (TILES + 1) // 2
    width = [max(a + n for a, _, n in pieces) for pieces in chunks]
    landed = [16 * sum(len(chunks[d]) for d in range(c + 1)) for c in range(NCH)]
    w_v = w.rearrange("(k p) n -> p k n", p=P)
    with ExitStack() as ctx:
        sb = lambda n, s, d=F32, **kw: ctx.enter_context(nc.sbuf_tensor(f"{tag}_{n}", s, d, **kw))
        sem = lambda n: st.sem(f"{tag}_{n}")
        raw = sb("w", [P, KD, NP])
        w_hi, w_lo = sb("w_hi", [P, RING, NP], F32R), sb("w_lo", [P, RING, NP], F32R)
        x_hi, x_lo = sb("x_hi", [P, KD, NTOK], F32R), sb("x_lo", [P, KD, NTOK], F32R)
        ps = ctx.enter_context(nc.psum_tensor(f"{tag}_ps", [P, 8, 512], F32))
        w_in, w_split_hi, w_split, block_done = sem("w_in"), sem("w_split_hi"), sem("w_split"), sem("block_done")
        x_split_hi, x_split = sem("x_split_hi"), sem("x_split")
        bank_done, act_evac, dve_evac = sem("bank_done"), sem("act_evac"), sem("dve_evac")
        stored = sem("stored")
        if XT is None:
            xbuf = sb("x", [P, 2, D])
            x_in = [sem(f"x_in{k}") for k in range(2)]
            t_done = sem("t_done")

        def wait_block(eng, g):
            if g % KD == KD - 1:
                eng.wait_ge(bank_done, NB * (g // KD + 1))
            else:
                eng.wait_ge(block_done, (KD - 1) * (g // KD) + g % KD + 1)

        with nc.Block() as block:
            @block.sync
            def _(sp):
                def load_w(c):
                    if c >= 1:
                        sp.wait_ge(w_split, KD * c)
                    for a, b, n in chunks[c]:
                        sp.dma_start(raw[:, :, a:a + n], w_v[:, :, b:b + n]).then_inc(w_in, 16)
                if XT is None:
                    for i in range(TILES):
                        if i >= 2:
                            sp.wait_ge(t_done, 2 * (i - 1))
                        sp.dma_start(xbuf[0:rows(i), i % 2, :], x_tile(i)).then_inc(x_in[i % 2], 16)
                        if i == 0:
                            load_w(0)
                else:
                    load_w(0)
                for c in range(1, NCH):
                    load_w(c)

            @block.tensor
            def _(pe):
                if XT is None:
                    for i in range(TILES):
                        r = rows(i)
                        pe.wait_ge(x_in[i % 2], 16 * (i // 2 + 1))
                        for h in range(2):
                            j = 2 * i + h
                            if j >= 8:
                                pe.wait_ge(x_split, j - 7)
                            for k in range(4):
                                kk = 4 * h + k
                                last = nc.tensor.transpose(ps[:, j % 8, k * P:k * P + r],
                                                           xbuf[0:r, i % 2, kk * P:(kk + 1) * P], st.ident[0:r, 0:r])
                            last.then_inc(t_done, 1)
                    pe.wait_ge(x_split, 2 * TILES)
                for c in range(NCH):
                    n = width[c]
                    for k in range(KD):
                        g = KD * c + k
                        pe.wait_ge(w_split, g + 1)
                        if XT is not None and c == 0:
                            pe.wait_ge(x_split, k + 1)
                        for i in range(TILES):
                            u, r = NB * c + i // 2, rows(i)
                            if k == 0 and i % 2 == 0 and u >= 8:
                                pe.wait_ge(act_evac if u % 2 == 0 else dve_evac, (u - 8) // 2 + 1)
                            o = ps[0:r, u % 8, (i % 2) * NP:(i % 2) * NP + n]
                            for j, (xp, wp) in enumerate(((x_hi, w_hi), (x_lo, w_hi), (x_hi, w_lo))):
                                last = nc.tensor.matmul(o, xp[:, k, i * P:i * P + r], wp[:, g % RING, 0:n],
                                                        start=(k == 0 and j == 0 and i % 2 == 0),
                                                        stop=(k == KD - 1 and j == 2), skip_group_check=True)
                            if k == KD - 1 and (i % 2 == 1 or i == TILES - 1):
                                last.then_inc(bank_done, 1)
                        if k < KD - 1:
                            last.then_inc(block_done, 1)

            def copy_out(eng, op, parity, done, c):
                for b in range(NB):
                    u = NB * c + b
                    if u % 2 == parity:
                        eng.wait_ge(bank_done, u + 1)
                        for i in range(2 * b, min(2 * b + 2, TILES)):
                            ins = op(dest(i)[0:rows(i), NP * c:NP * c + width[c]],
                                     ps[0:rows(i), u % 8, (i % 2) * NP:(i % 2) * NP + width[c]])
                        ins.then_inc(done, 1)

            def run(eng, op, parity, done, split_x, split_w):
                for c in range(NCH):
                    for k in range(KD):
                        if c == 0 and XT is not None:
                            split_x(k)
                        split_w(c, k)
                        if k == RING - 1 and c >= 1:
                            copy_out(eng, op, parity, done, c - 1)
                copy_out(eng, op, parity, done, NCH - 1)

            def x_part(t, j):
                i, h = j // 2, j % 2
                return t[:, 4 * h:4 * h + 4, i * P:i * P + rows(i)]

            def t_part(j):
                return ps[:, j % 8, :].rearrange("p (k t) -> p k t", k=4)[:, :, 0:rows(j // 2)]

            @block.scalar
            def _(act):
                if XT is None:
                    for j in range(2 * TILES):
                        act.wait_ge(t_done, j + 1)
                        nc.scalar.copy(x_part(x_hi, j), t_part(j)).then_inc(x_split_hi, 1)

                def split_x(k):
                    nc.scalar.copy(x_hi[:, k, :], XT[:, k, :]).then_inc(x_split_hi, 1)

                def split_w(c, k):
                    g = KD * c + k
                    if k == 0:
                        act.wait_ge(w_in, landed[c])
                    if g >= RING:
                        wait_block(act, g - RING)
                    nc.scalar.copy(w_hi[:, g % RING, 0:width[c]], raw[:, k, 0:width[c]]).then_inc(w_split_hi, 1)

                run(act, nc.scalar.copy, 0, act_evac, split_x, split_w)

            @block.vector
            def _(dve):
                if XT is None:
                    for j in range(2 * TILES):
                        dve.wait_ge(x_split_hi, j + 1)
                        nc.vector.tensor_tensor(x_part(x_lo, j), t_part(j), x_part(x_hi, j).bitcast(F32),
                                                ALU.subtract).then_inc(x_split, 1)

                def split_x(k):
                    dve.wait_ge(x_split_hi, k + 1)
                    nc.vector.tensor_tensor(x_lo[:, k, :], XT[:, k, :], x_hi[:, k, :].bitcast(F32), ALU.subtract).then_inc(x_split, 1)

                def split_w(c, k):
                    g, n = KD * c + k, width[c]
                    dve.wait_ge(w_split_hi, g + 1)
                    nc.vector.tensor_tensor(w_lo[:, g % RING, 0:n], raw[:, k, 0:n], w_hi[:, g % RING, 0:n].bitcast(F32),
                                            ALU.subtract).then_inc(w_split, 1)

                run(dve, nc.vector.tensor_copy, 1, dve_evac, split_x, split_w)

            @block.gpsimd
            def _(pool):
                total = NB * NCH
                pool.wait_ge(act_evac, (total + 1) // 2)
                pool.wait_ge(dve_evac, total // 2)
                n = 0
                for out_ap, src in stores:
                    pool.dma_start(out_ap, src).then_inc(stored, 16)
                    n += 1
                if n:
                    pool.wait_ge(stored, 16 * n)


def chained(eng, sem):
    count = [0]

    def link(ins):
        count[0] += 1
        ins.then_inc(sem, 1)
        eng.wait_ge(sem, count[0])
    return link


def gla(nc, st, A, C, O, H, Hs):
    NL = 8
    with ExitStack() as ctx:
        sb = lambda n, s, d=F32: ctx.enter_context(nc.sbuf_tensor(f"gla_{n}", s, d))
        sem = lambda n: st.sem(f"gla_{n}")
        w2, gb, ng = sb("w2", [16, 256]), sb("gb", [P, 2]), sb("ng", [P, DV])
        lev_f, lev = sb("levf", [P, NL, P]), sb("lev", [P, NL, P], U8)
        reset, bsel = sb("reset", [P, 192]), sb("bsel", [NS, 8])
        S = sb("S", [P, 2, DV])
        SS = sb("SS", [P, DEC_BATCH, 2, DV])
        qT, kT = sb("qT", [P, 2, 2, P]), sb("kT", [P, 2, 2, P])
        ggT = sb("ggT", [16, P])
        z, az, cs = sb("z", [P, 2, P]), sb("az", [P, 2, P]), sb("cs", [P, 2, P])
        EE = sb("E", [P, 2, NL + 1, 2, P])
        QM = sb("QM", [P, NL, 2, P])
        decs = sb("dec", [P, 2, 2, 8])
        A_sb = sb("A", [P, 2, 2, P])
        qin, kin, kinT = sb("qin", [P, 2, P]), sb("kin", [P, 2, P]), sb("kinT", [P, 2, P])
        oT = sb("oT", [P, 2, 2, NS])
        ssq, rs = sb("ssq", [P, 4]), sb("rs", [P, 4])
        junk = sb("junk", [P, DV])
        ps = ctx.enter_context(nc.psum_tensor("gla_ps", [P, 8, 512], F32))
        tr, misc, gg_ps = ps[:, 0, :], ps[:, 1, :], ps[:, 7, :]
        o_ps = [ps[:, 7, :], ps[:, 2, :]]
        ot_ps = [ps[:, 0, :], ps[:, 1, :]]

        def o_of(h, r):
            return o_ps[h % 2][0:r, (h // 2) * DV:(h // 2 + 1) * DV]

        cin, cst = sem("const_in"), sem("const_ready")
        t_done, t_act, g_dve = sem("qk_transposed"), sem("qk_copied"), sem("gg_copied")
        z_biased = sem("z_biased")
        z_done, az_done, ln_done = sem("z_done"), sem("az_done"), sem("ln_done")
        d_done, e_done, qk_done = sem("diff_done"), sem("exp_done"), sem("scaled_done")
        lev_done, lev_used = sem("level_done"), sem("level_used")
        kt_done, kt_act = sem("kin_transposed"), sem("kin_copied")
        o_done, ot_done, ot_act = sem("o_done"), sem("oT_done"), sem("oT_copied")
        kv_done, kv_used = sem("kv_done"), sem("kv_used")
        sq_done, ms_done, rs_done, y_done = sem("sq_done"), sem("ms_done"), sem("rs_done"), sem("y_done")
        silu_done, gate_done = sem("silu_done"), sem("gate_done")
        dch, ach, pch, kb_done = sem("dve_step"), sem("act_step"), sem("pool_step"), sem("kin_masked")
        s_out = sem("state_out")
        kinTb = QM

        def tile_of(i):
            return H[:, i, :] if i < NT else Hs[:, :]

        def lv(i):
            return NL if i < NT else 4

        lev0 = [0]
        for i in range(TILES):
            lev0.append(lev0[-1] + lv(i))
        half = lambda h: slice(64 * (h % 2), 64 * (h % 2) + 64)

        with nc.Block() as block:
            @block.sync
            def _(sp):
                for dst, src in ((w2[:, :], A["gla_gate_w2"][0]),
                                 (ng[:, :], bcast_rows(A["gla_norm_g"], DV)), (lev_f[:, :, :], C["levels"]),
                                 (reset[:, :], C["reset"]), (bsel[:, :], C["batchsel"])):
                    sp.dma_start(dst, src).then_inc(cin, 16)
                sp.dma_start(gb[:, :], A["gla_gate_b"].rearrange("o (c p) -> p (o c)", p=P),
                             allow_slow_non_contiguous=True).then_inc(cin, 16)
                for hf in range(2):
                    sp.dma_start(SS[64 * hf:64 * hf + 64, :, :, :],
                                 A["state_gla"][0].rearrange("b (r f) d v -> f d b r v", f=2)[hf]).then_inc(cin, 16)
                sp.wait_ge(kv_used, NT)
                for hf in range(2):
                    sp.dma_start(O[5][0, 0].rearrange("(r f) d v -> f d r v", f=2)[hf],
                                 S[64 * hf:64 * hf + 64, :, :]).then_inc(s_out, 16)
                sp.wait_ge(kv_used, NT + DEC_BATCH)
                for hf in range(2):
                    sp.dma_start(O[11][0].rearrange("b (r f) d v -> f d b r v", f=2)[hf],
                                 SS[64 * hf:64 * hf + 64, :, :, :]).then_inc(s_out, 16)
                sp.wait_ge(s_out, 64)

            @block.tensor
            def _(pe):
                def front_transposes(i):
                    r, T = rows(i), tile_of(i)
                    if i >= 1:
                        pe.wait_ge(t_act, i)
                    if i >= 2:
                        pe.wait_ge(y_done, i - 1)
                    for p in range(2):
                        nc.tensor.transpose(tr[:, p * P:p * P + r], T[0:r, C_GQ + p * P:C_GQ + (p + 1) * P], st.ident[0:r, 0:r])
                        nc.tensor.transpose(tr[:, (2 + p) * P:(2 + p) * P + r], T[0:r, C_GK + p * P:C_GK + (p + 1) * P], st.ident[0:r, 0:r])
                    nc.tensor.transpose(gg_ps[0:16, 0:r], T[0:r, C_GG:C_GG + 16], st.ident[0:r, 0:r]).then_inc(t_done, 1)

                def front_gates(i):
                    r = rows(i)
                    pe.wait_ge(g_dve, i + 1)
                    if i == 0:
                        pe.wait_ge(cin, 16 * 8)
                    else:
                        pe.wait_ge(kt_act, i)
                    for p in range(2):
                        last = nc.tensor.matmul(misc[:, p * P:p * P + r], w2[:, p * P:(p + 1) * P], ggT[:, 0:r],
                                                start=True, stop=True)
                    last.then_inc(z_done, 1)

                def level(i, l):
                    r, s, g = rows(i), i % 2, lev0[i] + l
                    if g >= 2:
                        pe.wait_ge(lev_used, g - 1)
                    for h in range(GLA_H):
                        kk = kT[half(h), s, h // 2, 0:r] if l == 0 else EE[half(h), s, l, h // 2, 0:r]
                        qq = qT[half(h), s, h // 2, 0:r] if l == 0 else QM[half(h), l, h // 2, 0:r]
                        last = nc.tensor.matmul(ps[0:r, 3 + 2 * (g % 2) + h % 2, (h // 2) * P:(h // 2) * P + r], kk, qq,
                                                start=True, stop=True)
                    last.then_inc(lev_done, 1)

                front_transposes(0)
                front_gates(0)
                for i in range(TILES):
                    r, T = rows(i), tile_of(i)
                    pe.wait_ge(qk_done, i + 1)
                    if i >= 1:
                        pe.wait_ge(kv_used, i)
                    for p in range(2):
                        last = nc.tensor.transpose(misc[0:r, p * P:(p + 1) * P], kin[:, p, 0:r], st.ident[:, :])
                    last.then_inc(kt_done, 1)
                    if i + 1 < TILES:
                        front_transposes(i + 1)
                    for l in range(lv(i)):
                        level(i, l)
                        if l == 3 and i + 1 < TILES:
                            front_gates(i + 1)
                    if i == NT:
                        pe.wait_ge(kt_act, i + 1)
                        for h in range(GLA_H):
                            for b in range(DEC_BATCH):
                                last = nc.tensor.matmul(ot_ps[h % 2][:, (h // 2) * NS + 8 * b:(h // 2) * NS + 8 * b + 8],
                                                        SS[half(h), b, h // 2, :], qin[half(h), h // 2, 8 * b:8 * b + 8],
                                                        start=True, stop=True)
                        last.then_inc(ot_done, 1)
                        pe.wait_ge(ot_act, 2)
                    pe.wait_ge(lev_used, lev0[i + 1])
                    if i >= 1:
                        pe.wait_ge(y_done, i)
                    for h in range(GLA_H):
                        nc.tensor.matmul(o_of(h, r), A_sb[0:r, h % 2, h // 2, 0:r],
                                         T[0:r, C_GV + h * DV:C_GV + (h + 1) * DV], start=True, stop=False)
                        if i < NT:
                            last = nc.tensor.matmul(o_of(h, r), qin[half(h), h // 2, 0:r],
                                                    S[half(h), h // 2, :], start=False, stop=True)
                        else:
                            last = nc.tensor.matmul(o_of(h, r), oT[:, h % 2, h // 2, :], st.ident[:, :],
                                                    start=False, stop=True)
                    last.then_inc(o_done, 1)
                    pe.wait_ge(kt_act, i + 1)
                    if i < NT:
                        pe.wait_ge(z_biased, i + 2)
                        for p in range(2):
                            last = nc.tensor.matmul(misc[:, p * 256:(p + 1) * 256], kinT[0:r, p, :],
                                                    T[0:r, C_GV + 256 * p:C_GV + 256 * p + 256], start=True, stop=True)
                        last.then_inc(kv_done, 1)
                    else:
                        for b in range(DEC_BATCH):
                            pe.wait_ge(kb_done, b + 1)
                            pe.wait_ge(kv_used, NT + b)
                            for p in range(2):
                                last = nc.tensor.matmul(misc[:, p * 256:(p + 1) * 256], kinTb[0:r, b, p, :],
                                                        T[0:r, C_GV + 256 * p:C_GV + 256 * p + 256], start=True, stop=True)
                            last.then_inc(kv_done, 1)

            @block.scalar
            def _(act):
                link = chained(act, ach)

                def front_copies(i):
                    r = rows(i)
                    act.wait_ge(t_done, i + 1)
                    if i >= 2:
                        act.wait_ge(o_done, i - 1)
                        act.wait_ge(qk_done, i - 1)
                    trv = tr.rearrange("p (a t) -> p a t", a=4)
                    nc.scalar.mul(qT[:, i % 2, :, 0:r], trv[:, 0:2, 0:r], DK ** -0.5)
                    nc.scalar.copy(kT[:, i % 2, :, 0:r], trv[:, 2:4, 0:r]).then_inc(t_act, 1)

                def front_gates(i):
                    r = rows(i)
                    act.wait_ge(z_biased, i + 1)
                    nc.scalar.activation(az[:, :, 0:r], z[:, :, 0:r], ACT.Abs).then_inc(az_done, 1)
                    act.wait_ge(az_done, i + 1)
                    link(nc.scalar.activation(az[:, :, 0:r], az[:, :, 0:r], ACT.Exp, scale=-1.0))
                    nc.scalar.activation(az[:, :, 0:r], az[:, :, 0:r], ACT.Ln, bias=1.0).then_inc(ln_done, 1)

                front_copies(0)
                front_gates(0)
                for i in range(TILES):
                    gr = tile_of(i)[0:rows(i), C_GR:C_GR + 512]
                    nc.scalar.activation(gr, gr, ACT.Silu).then_inc(silu_done, 1)
                for i in range(TILES):
                    r, T = rows(i), tile_of(i)
                    E, dec = EE[:, i % 2], decs[:, i % 2]
                    act.wait_ge(d_done, i + 1)
                    nc.scalar.activation(dec, dec, ACT.Exp, scale=1 / TAU)
                    if i < NT:
                        nc.scalar.activation(E, E, ACT.Exp, scale=1 / TAU).then_inc(e_done, 1)
                    else:
                        nc.scalar.activation(E[:, 0:4, :, 0:r], E[:, 0:4, :, 0:r], ACT.Exp, scale=1 / TAU)
                        nc.scalar.activation(E[:, NL, :, 0:r], E[:, NL, :, 0:r], ACT.Exp, scale=1 / TAU).then_inc(e_done, 1)
                    act.wait_ge(kt_done, i + 1)
                    nc.scalar.copy(kinT[0:r, :, :], misc.rearrange("p (a t) -> p a t", a=4)[0:r, 0:2, :]).then_inc(kt_act, 1)
                    if i == NT:
                        act.wait_ge(ot_done, 1)
                        for hf in range(2):
                            nc.scalar.copy(oT[:, hf, :, :], ot_ps[hf][:, 0:2 * NS].rearrange("p (h t) -> p h t", h=2)
                                           ).then_inc(ot_act, 1)
                    else:
                        front_copies(i + 1)
                        front_gates(i + 1)
                    act.wait_ge(o_done, i + 1)
                    for h in range(GLA_H):
                        ins = nc.scalar.activation(junk[0:r, :], o_of(h, r), ACT.Square, accum_out=ssq[0:r, h:h + 1])
                        if h < GLA_H - 1:
                            link(ins)
                        else:
                            ins.then_inc(sq_done, 1)
                    act.wait_ge(ms_done, i + 1)
                    link(nc.scalar.activation(rs[0:r, :], ssq[0:r, :], ACT.Ln))
                    nc.scalar.activation(rs[0:r, :], rs[0:r, :], ACT.Exp, scale=-0.5).then_inc(rs_done, 1)

            @block.gpsimd
            def _(pool):
                link = chained(pool, pch)
                pool.wait_ge(cin, 16 * 8)
                for i in range(TILES):
                    r, T = rows(i), tile_of(i)
                    pool.wait_ge(silu_done, i + 1)
                    g4 = T[0:r, C_GR:C_GR + 512].rearrange("p (h v) -> p h v", h=4)
                    nc.gpsimd.tensor_tensor(g4, g4, ng[0:r, :].unsqueeze(1).to_broadcast([r, 4, DV]), ALU.mult).then_inc(gate_done, 1)
                for i in range(TILES):
                    r, T = rows(i), tile_of(i)
                    if i == NT:
                        pool.wait_ge(kt_act, i + 1)
                        pool.wait_ge(lev_used, lev0[i + 1])
                        for b in range(DEC_BATCH):
                            nc.gpsimd.tensor_scalar(kinTb[0:r, b, :, :], kinT[0:r, :, :], bsel[0:r, b:b + 1], None,
                                                    ALU.mult).then_inc(kb_done, 1)

            @block.vector
            def _(dve):
                link = chained(dve, dch)

                def front_copy(i):
                    r = rows(i)
                    dve.wait_ge(t_done, i + 1)
                    nc.vector.tensor_copy(ggT[:, 0:r], gg_ps[0:16, 0:r]).then_inc(g_dve, 1)

                def front_bias(i):
                    r = rows(i)
                    dve.wait_ge(z_done, i + 1)
                    for p in range(2):
                        ins = nc.vector.tensor_scalar(z[:, p, 0:r], misc[:, p * P:p * P + r], gb[:, p:p + 1], None, ALU.add)
                        if p == 0:
                            link(ins)
                    ins.then_inc(z_biased, 1)
                    dve.wait_ge(az_done, i + 1)
                    link(nc.vector.tensor_scalar(z[:, :, 0:r], z[:, :, 0:r], 0.0, None, ALU.min))

                def front_differences(i):
                    r = rows(i)
                    E, dec = EE[:, i % 2], decs[:, i % 2]
                    dve.wait_ge(ln_done, i + 1)
                    link(nc.vector.tensor_tensor(z[:, :, 0:r], z[:, :, 0:r], az[:, :, 0:r], ALU.subtract))
                    o0 = 0 if i < NT else P
                    for p in range(2):
                        link(nc.vector.tensor_tensor_scan(cs[:, p, 0:r], reset[:, o0:o0 + r], z[:, p, 0:r], 0.0,
                                                          ALU.mult, ALU.add))
                    nb0 = 1 if i < NT else DEC_BATCH
                    T0 = r // nb0
                    link(nc.vector.tensor_copy(dec, cs[:, :, T0 - 1:r:T0] if i == NT else
                                               cs[:, :, r - 1:r].to_broadcast([P, 2, 8])))
                    nc.vector.tensor_tensor(
                        E[:, 0, :, 0:r].rearrange("p a (b t) -> p a b t", b=nb0),
                        dec[:, :, 0:nb0].unsqueeze(3).to_broadcast([P, 2, nb0, T0]),
                        cs[:, :, 0:r].rearrange("p a (b t) -> p a b t", b=nb0), ALU.subtract)
                    nc.vector.tensor_copy(E[:, NL, :, 0:r], cs[:, :, 0:r])
                    for l in range(1, lv(i)):
                        L = 2 ** (l - 1)
                        c3 = cs[:, :, 0:r].rearrange("p a (b f t) -> p a b f t", f=2, t=L)
                        e3 = E[:, l, :, 0:r].rearrange("p a (b f t) -> p a b f t", f=2, t=L)
                        nb = r // (2 * L)
                        anchor = c3[:, :, :, 0, L - 1:L].to_broadcast([P, 2, nb, L])
                        nc.vector.tensor_tensor(e3[:, :, :, 0, :], anchor, c3[:, :, :, 0, :], ALU.subtract)
                        ins = nc.vector.tensor_tensor(e3[:, :, :, 1, :], c3[:, :, :, 1, :], anchor, ALU.subtract)
                    ins.then_inc(d_done, 1)

                def decayed(i):
                    r, n, E = rows(i), lv(i), EE[:, i % 2]
                    dve.wait_ge(e_done, i + 1)
                    dve.wait_ge(t_act, i + 1)
                    q, k = qT[:, i % 2], kT[:, i % 2]
                    nc.vector.tensor_tensor(kin[:, :, 0:r], E[:, 0, :, 0:r], k[:, :, 0:r], ALU.mult)
                    nc.vector.tensor_tensor(qin[:, :, 0:r], E[:, NL, :, 0:r], q[:, :, 0:r], ALU.mult)
                    for p in range(2):
                        qb = q[:, p:p + 1, 0:r].to_broadcast([P, n - 1, r])
                        kb = k[:, p:p + 1, 0:r].to_broadcast([P, n - 1, r])
                        link(nc.vector.tensor_tensor(QM[:, 1:n, p, 0:r], E[:, 1:n, p, 0:r], qb, ALU.mult))
                        ins = nc.vector.tensor_tensor(E[:, 1:n, p, 0:r], E[:, 1:n, p, 0:r], kb, ALU.mult)
                    ins.then_inc(qk_done, 1)

                def take_level(i, l):
                    r, g = rows(i), lev0[i] + l
                    dve.wait_ge(lev_done, g + 1)
                    if g >= 1:
                        dve.wait_ge(lev_used, g)
                    for hf in range(2):
                        ins = nc.vector.copy_predicated(
                            A_sb[0:r, hf, :, 0:r], lev[0:r, l:l + 1, 0:r].to_broadcast([r, 2, r]),
                            ps[0:r, 3 + 2 * (g % 2) + hf, 0:2 * P].rearrange("s (h t) -> s h t", h=2)[:, :, 0:r])
                    ins.then_inc(lev_used, 1)

                def decay_state(i, state, b):
                    dec = decs[:, i % 2]
                    for h in range(GLA_H):
                        c0 = (h // 2) * 256 + (h % 2) * DV
                        ins = nc.vector.scalar_tensor_tensor(
                            out=state[half(h), h // 2, :], in0=state[half(h), h // 2, :],
                            scalar=dec[half(h), h // 2, b:b + 1], in1=misc[half(h), c0:c0 + DV],
                            op0=ALU.mult, op1=ALU.add)
                    ins.then_inc(kv_used, 1)

                def gated_output(i):
                    r, T = rows(i), tile_of(i)
                    dve.wait_ge(rs_done, i + 1)
                    dve.wait_ge(gate_done, i + 1)
                    for h in range(GLA_H):
                        gr = T[0:r, C_GR + h * DV:C_GR + (h + 1) * DV]
                        ins = nc.vector.scalar_tensor_tensor(out=gr, in0=o_of(h, r), scalar=rs[0:r, h:h + 1], in1=gr,
                                                             op0=ALU.mult, op1=ALU.mult)
                    ins.then_inc(y_done, 1)

                dve.wait_ge(cin, 16 * 8)
                link(nc.vector.tensor_copy(lev[:, :, :], lev_f[:, :, :]))
                link(nc.vector.memset(A_sb[:, :, :, :], 0.0))
                nc.vector.memset(S[:, :, :], 0.0).then_inc(cst, 1)
                dve.wait_ge(cst, 1)
                front_copy(0)
                front_bias(0)
                front_differences(0)
                for i in range(TILES):
                    r = rows(i)
                    decayed(i)
                    if i >= 1:
                        gated_output(i - 1)
                    if i < NT:
                        front_copy(i + 1)
                    else:
                        dve.wait_ge(o_done, NT)
                        dve.wait_ge(lev_used, lev0[NT])
                        link(nc.vector.memset(A_sb[0:r, :, :, 0:r], 0.0))
                    for l in range(4):
                        take_level(i, l)
                    if i < NT:
                        front_bias(i + 1)
                        for l in range(4, NL):
                            take_level(i, l)
                        front_differences(i + 1)
                        dve.wait_ge(kv_done, i + 1)
                        dve.wait_ge(o_done, i + 1)
                        decay_state(i, S, 0)
                    else:
                        for b in range(DEC_BATCH):
                            dve.wait_ge(kv_done, NT + 1 + b)
                            decay_state(i, SS[:, b], b)
                    dve.wait_ge(sq_done, i + 1)
                    nc.vector.tensor_scalar(ssq[0:r, :], ssq[0:r, :], 1.0 / DV, RMS_EPS, ALU.mult, ALU.add).then_inc(ms_done, 1)
                gated_output(NT)
                dve.wait_ge(y_done, TILES)


TOPK = 256
NEG = -1e30
TAKEN = -3e38
AS = HD ** -0.5
IWS = 512.0 ** -0.5


def dsa_prompt(nc, st, A, C, O, H, Hs, XT):
    HEADS = [(kv, g) for g in range(4) for kv in range(2)]
    NH = len(HEADS)
    chunks = lambda t: -(-(t + 1) * P // 512)
    ptg = lambda t: -(-(t + 1) // 4)
    def passes(i):
        t, out = i + 2, []
        if t < NT:
            out += [("iq", t)] if t >= 2 else []
            out += [("keys", t)]
            if t >= 2:
                out += [("dots", t, h, c) for h in range(8) for c in range(chunks(t))]
        if 0 <= i + 1 < NT:
            out.append(("q", i + 1))
        return out

    def shares(i):
        u, rounds = passes(i), range(TOPK // 8) if 2 <= i + 1 < NT else []
        per, rper = -(-len(u) // NH), -(-len(rounds) // NH)
        return [(u[n * per:(n + 1) * per], rounds[n * rper:(n + 1) * rper]) for n in range(NH)]

    pass_no, dot_no = {}, {}
    for i in range(-2, NT):
        for u in passes(i):
            pass_no[u] = len(pass_no)
            if u[0] == "dots":
                dot_no[u] = len(dot_no)
    grp_no = {}
    for i in range(NT):
        for n in range(NH):
            for c in range(ptg(i)):
                grp_no[(i, n, c)] = len(grp_no)
    with ExitStack() as ctx:
        sb = lambda n, s, d=F32: ctx.enter_context(nc.sbuf_tensor(f"dsa_{n}", s, d))
        sem = lambda n: st.sem(f"dsa_{n}")
        KT, IKT = sb("KT", [P, SEQ]), sb("IKT", [P, SEQ])
        qT, iqT = sb("qT", [P, 2, 4, P]), sb("iqT", [P, 4, P])
        rel = sb("rel", [P, 4, 512])
        iws = sb("iws", [P, 8])
        sc, wk = sb("sc", [P, SEQ]), sb("wk", [P, SEQ])
        m8 = sb("m8", [P, 8])
        bias = sb("bias", [P, 2, SEQ], BF16)
        identb = sb("identb", [P, P], BF16)
        causal = sb("causal", [P, P])
        Pb, PT = sb("P", [P, 2, SEQ]), sb("PT", [P, 2, NT, P])
        mx, nm, sm, rs = sb("mx", [P, 2]), sb("nm", [P, 2]), sb("sm", [P, NH]), sb("rs", [P, NH])
        ps = ctx.enter_context(nc.psum_tensor("dsa_ps", [P, 8, 512], F32))
        cin = sem("const_in")
        p7_done, p7_read, dots_added = sem("pass_done"), sem("pass_read"), sem("dots_added")
        b_done = sem("bias_ready")
        s_done, m_done, e_done = sem("scores"), sem("max_done"), sem("probs")
        pt_done, pt_copied = sem("probs_transposed"), sem("probsT_copied")
        o_done, y_done, yt_done, yt_act = sem("o_done"), sem("y_done"), sem("y_transposed"), sem("yT_copied")
        dch = sem("dve_step")
        half = lambda kv: slice(64 * kv, 64 * kv + 64)

        with nc.Block() as block:
            @block.sync
            def _(sp):
                sp.dma_start(causal[:, :], C["causal"]).then_inc(cin, 16)
                sp.wait_ge(cin, 16)

            @block.tensor
            def _(pe):
                def bank7(u):
                    no, T = pass_no[u], H[:, u[1], :]
                    if no >= 1:
                        pe.wait_ge(p7_read, no)
                    if u[0] == "iq":
                        for g in range(4):
                            last = nc.tensor.transpose(ps[:, 7, g * P:(g + 1) * P], T[:, C_IQ + g * P:C_IQ + (g + 1) * P], st.ident[:, :])
                    elif u[0] == "keys":
                        nc.tensor.transpose(ps[:, 7, 0:P], T[:, C_DK:C_DK + P], st.ident[:, :])
                        last = nc.tensor.transpose(ps[:, 7, P:2 * P], T[:, C_IK:C_IK + P], st.ident[:, :])
                    elif u[0] == "q":
                        for g in range(4):
                            last = nc.tensor.transpose(ps[:, 7, g * P:(g + 1) * P], T[:, C_DQ + g * P:C_DQ + (g + 1) * P], st.ident[:, :])
                    else:
                        _, t, h, c = u
                        n = min(512, (t + 1) * P - 512 * c)
                        last = nc.tensor.matmul(ps[:, 7, 0:n], iqT[half(h % 2), h // 2, :],
                                                IKT[half(h % 2), 512 * c:512 * c + n], start=True, stop=True)
                    last.then_inc(p7_done, 1)

                def scores(i, n):
                    kv, g = HEADS[n]
                    a = i * NH + n
                    if n == 0:
                        pe.wait_ge(b_done, i + 1)
                        pe.wait_ge(p7_read, pass_no[("q", i)] + 1)
                    if a >= 2:
                        pe.wait_ge(e_done, a - 1)
                    for c in range(chunks(i)):
                        w = min(512, (i + 1) * P - 512 * c)
                        nc.tensor.matmul(ps[:, 2 * kv + c, 0:w], identb[:, :], bias[:, i % 2, 512 * c:512 * c + w],
                                         start=True, stop=False)
                        last = nc.tensor.matmul(ps[:, 2 * kv + c, 0:w], qT[half(kv), i % 2, g, :],
                                                KT[half(kv), 512 * c:512 * c + w], start=False, stop=True)
                    last.then_inc(s_done, 1)

                def transpose_probs(i, n):
                    a = i * NH + n
                    pe.wait_ge(e_done, a + 1)
                    for c in range(ptg(i)):
                        gn = grp_no[(i, n, c)]
                        if gn >= 2:
                            pe.wait_ge(pt_copied, gn - 1)
                        if n == 0 and i >= 1:
                            pe.wait_ge(yt_act, 2 * i)
                        for j in range(4 * c, min(4 * c + 4, i + 1)):
                            last = nc.tensor.transpose(ps[:, 4 + gn % 2, (j % 4) * P:(j % 4 + 1) * P],
                                                       Pb[:, a % 2, j * P:(j + 1) * P], st.ident[:, :])
                        last.then_inc(pt_done, 1)

                def values(i, n):
                    kv, g = HEADS[n]
                    a, h = i * NH + n, kv * 4 + g
                    pe.wait_ge(pt_copied, grp_no[(i, n, ptg(i) - 1)] + 1)
                    if n == 0 and i >= 1:
                        pe.wait_ge(y_done, i)
                    for j in range(i + 1):
                        last = nc.tensor.matmul(ps[:, 6, h * HD:(h + 1) * HD], PT[:, a % 2, j, :],
                                                H[:, j, C_DV + kv * HD:C_DV + (kv + 1) * HD],
                                                start=(j == 0), stop=(j == i))
                    last.then_inc(o_done, 1)

                for i in (-2, -1):
                    for u in passes(i):
                        bank7(u)
                for i in range(NT):
                    T, share = H[:, i, :], shares(i)
                    scores(i, 0)
                    for n in range(NH):
                        if n + 1 < NH:
                            scores(i, n + 1)
                        transpose_probs(i, n)
                        for u in share[n][0]:
                            bank7(u)
                        values(i, n)
                    pe.wait_ge(y_done, i + 1)
                    for k in range(KD):
                        c0 = C_GR + k * P if k < 4 else C_DQ + (k - 4) * P
                        last = nc.tensor.transpose(ps[:, 4 + k // 4, (k % 4) * P:(k % 4 + 1) * P],
                                                   T[:, c0:c0 + P], st.ident[:, :])
                        if k % 4 == 3:
                            last.then_inc(yt_done, 1)

            @block.scalar
            def _(act):
                def bank7(u):
                    act.wait_ge(p7_done, pass_no[u] + 1)
                    t, full = u[1], ps[:, 7, :].rearrange("p (a t) -> p a t", a=4)
                    if u[0] == "iq":
                        nc.scalar.copy(iqT[:, :, :], full).then_inc(p7_read, 1)
                    elif u[0] == "keys":
                        nc.scalar.copy(KT[:, t * P:(t + 1) * P], ps[:, 7, 0:P])
                        nc.scalar.copy(IKT[:, t * P:(t + 1) * P], ps[:, 7, P:2 * P]).then_inc(p7_read, 1)
                    elif u[0] == "q":
                        nc.scalar.copy(qT[:, t % 2, :, :], full).then_inc(p7_read, 1)
                    else:
                        d, n = dot_no[u], min(512, (t + 1) * P - 512 * u[3])
                        if d >= 4:
                            act.wait_ge(dots_added, d - 3)
                        nc.scalar.activation(rel[:, d % 4, 0:n], ps[:, 7, 0:n], ACT.Relu).then_inc(p7_read, 1)

                def exps(i, n):
                    kv, g = HEADS[n]
                    a, L = i * NH + n, (i + 1) * P
                    act.wait_ge(m_done, a + 1)
                    if a >= 2:
                        act.wait_ge(o_done, a - 1)
                    nc.scalar.activation(Pb[:, a % 2, 0:L], ps[:, 2 * kv:2 * kv + 2, :].rearrange("p b n -> p (b n)")[:, 0:L],
                                         ACT.Exp, bias=nm[:, a % 2:a % 2 + 1], scale=AS,
                                         accum_out=sm[:, n:n + 1]).then_inc(e_done, 1)

                for i in (-2, -1):
                    for u in passes(i):
                        bank7(u)
                for i in range(NT):
                    share = shares(i)
                    if i >= 1:
                        act.wait_ge(y_done, i)
                    exps(i, 0)
                    for n in range(NH):
                        for u in share[n][0]:
                            bank7(u)
                        if n + 1 < NH:
                            exps(i, n + 1)
                    for k in range(2):
                        act.wait_ge(yt_done, 2 * i + k + 1)
                        nc.scalar.copy(XT[:, 4 * k:4 * k + 4, i * P:(i + 1) * P],
                                       ps[:, 4 + k, :].rearrange("p (a t) -> p a t", a=4)).then_inc(yt_act, 1)

            @block.vector
            def _(dve):
                link = chained(dve, dch)
                dve.wait_ge(cin, 16)
                link(nc.vector.tensor_copy(identb[:, :], st.ident[:, :]))
                link(nc.vector.memset(bias[:, 1, 0:P], 0.0))
                for t in range(2):
                    nc.vector.tensor_copy(bias[:, t, t * P:(t + 1) * P], causal[:, :]).then_inc(b_done, 1)

                def add_dots(u):
                    _, t, h, c = u
                    d, n = dot_no[u], min(512, (t + 1) * P - 512 * c)
                    if h == 0 and c == 0:
                        link(nc.vector.tensor_scalar(iws[:, :], H[:, t, C_IW:C_IW + 8], IWS, None, ALU.mult))
                    part = sc[:, 512 * c:512 * c + n]
                    dve.wait_ge(p7_read, pass_no[u] + 1)
                    if h == 0:
                        nc.vector.tensor_scalar(part, rel[:, d % 4, 0:n], iws[:, h:h + 1], None, ALU.mult).then_inc(dots_added, 1)
                    else:
                        dve.wait_ge(dots_added, d)
                        nc.vector.scalar_tensor_tensor(out=part, in0=rel[:, d % 4, 0:n], scalar=iws[:, h:h + 1], in1=part,
                                                       op0=ALU.mult, op1=ALU.add).then_inc(dots_added, 1)

                def top_round(t, k):
                    L = (t + 1) * P
                    if k == 0:
                        dve.wait_ge(dots_added, dot_no[("dots", t, 7, chunks(t) - 1)] + 1)
                        link(nc.vector.tensor_tensor(sc[:, L - P:L], sc[:, L - P:L], causal[:, :], ALU.add))
                    src = sc if k == 0 else wk
                    link(nc.vector.max(m8[:, :], src[:, 0:L]))
                    link(nc.vector.match_replace(wk[:, 0:L], m8[:, :], src[:, 0:L], TAKEN))
                    if k == TOPK // 8 - 1:
                        nc.vector.tensor_scalar(bias[:, t % 2, 0:L], wk[:, 0:L], -2e38, NEG, ALU.is_ge, ALU.mult).then_inc(b_done, 1)

                def row_max(i, n):
                    kv, g = HEADS[n]
                    a, L = i * NH + n, (i + 1) * P
                    dve.wait_ge(s_done, a + 1)
                    link(nc.vector.reduce_max(mx[:, a % 2:a % 2 + 1],
                                              ps[:, 2 * kv:2 * kv + 2, :].rearrange("p b n -> p (b n)")[:, 0:L], AX_X))
                    if a >= 2:
                        dve.wait_ge(e_done, a - 1)
                    nc.vector.tensor_scalar(nm[:, a % 2:a % 2 + 1], mx[:, a % 2:a % 2 + 1], -AS, None,
                                            ALU.mult).then_inc(m_done, 1)

                def copy_pt(i, n):
                    a = i * NH + n
                    if a >= 2:
                        dve.wait_ge(o_done, a - 1)
                    for c in range(ptg(i)):
                        gn = grp_no[(i, n, c)]
                        w = min(4, i + 1 - 4 * c)
                        dve.wait_ge(pt_done, gn + 1)
                        nc.vector.tensor_copy(PT[:, a % 2, 4 * c:4 * c + w, :],
                                              ps[:, 4 + gn % 2, 0:w * P].rearrange("p (a t) -> p a t", t=P)).then_inc(pt_copied, 1)

                for i in range(NT):
                    T, share = H[:, i, :], shares(i)
                    row_max(i, 0)
                    for n in range(NH):
                        rounds = share[n][1]
                        cut = len(rounds) // 2
                        if n + 1 < NH:
                            row_max(i, n + 1)
                        for k in rounds[:cut]:
                            top_round(i + 1, k)
                        copy_pt(i, n)
                        for k in rounds[cut:]:
                            top_round(i + 1, k)
                        for u in share[n][0]:
                            if u[0] == "dots":
                                add_dots(u)
                    dve.wait_ge(e_done, (i + 1) * NH)
                    link(nc.vector.reciprocal(rs[:, :], sm[:, :]))
                    dve.wait_ge(o_done, (i + 1) * NH)
                    for kv in range(2):
                        ins = nc.vector.tensor_tensor(
                            T[:, C_DQ + kv * 256:C_DQ + (kv + 1) * 256].rearrange("p (g d) -> p g d", g=4),
                            ps[:, 6, kv * 256:(kv + 1) * 256].rearrange("p (g d) -> p g d", g=4),
                            rs[:, kv::2].unsqueeze(2).to_broadcast([P, 4, HD]), ALU.mult)
                    ins.then_inc(y_done, 1)
                dve.wait_ge(y_done, NT)


PAGES = 16
PAST = PAGES * P
LK = PAST + DEC_SEQ
CHUNKS = [(0, 512), (512, 512), (1024, 512), (1536, 512), (2048, 8)]


def dsa_sample(nc, st, A, C, O, Hs, XT):
    NB, NP_ = DEC_BATCH, DEC_BATCH // 2
    scr_w = nc.dram_tensor("scratch_iw", (NS, 8), F32, kind="Internal").ap()
    scr_y = nc.dram_tensor("scratch_y", (NS, 512), F32, kind="Internal").ap()
    n_pool = A["cache_k"].shape[1]
    with ExitStack() as ctx:
        sb = lambda n, s, d=F32: ctx.enter_context(nc.sbuf_tensor(f"smp_{n}", s, d))
        sem = lambda n: st.sem(f"smp_{n}")
        pages = sb("pages", [1, NB * PAGES], I32)
        ikT = sb("ikT", [HD, 2, LK])
        iqT, ikn = sb("iqT", [HD, NB, 8, DEC_SEQ]), sb("ikn", [HD, NS])
        rel = sb("rel", [NS, 2, 512])
        iwd = sb("iwd", [NS, NB])
        gat, gw = sb("gat", [NS, NB, NS]), sb("gw", [NS, NB, NS])
        sc, wk, m8 = sb("sc", [NS, LK]), sb("wk", [NS, LK]), sb("m8", [NS, 8])
        bias = sb("bias", [NS, LK], BF16)
        c8 = sb("c8", [NS, 8])
        spb = sb("spb", [NS, NP_, P], BF16)
        qz, KnT = sb("qz", [P, NB, 2, 4, DEC_SEQ]), sb("KnT", [P, NS])
        Kp, KT = sb("Kp", [P, 4, PAGES, P]), sb("KT", [P, 2, LK])
        idxp = Kp[:, 2:4, :, :].rearrange("p s j c -> p (s j c)").rearrange("p (s j d) -> p s j d", s=4, d=HD)
        Vp, Vn = sb("Vp", [P, 4, PAGES, P]), sb("Vn", [DEC_SEQ, NB, P])
        Pb, PT = sb("P", [P, LK]), sb("PT", [P, PAGES + 1, P])
        spf = PT[0:NS, 0:NP_, :]
        mx, nm, sm, rs = sb("mx", [P, 1]), sb("nm", [P, 1]), sb("sm", [P, 1]), sb("rs", [P, 1])
        yq = sb("yq", [P, NP_, HD])
        ps = ctx.enter_context(nc.psum_tensor("smp_ps", [P, 8, 512], F32))
        flat = ps[:, 0:5, :].rearrange("p b n -> p (b n)")
        cin, pin = sem("const_in"), sem("page_table_in")
        ix_in = [sem(f"index_pages{k}") for k in range(4)]
        k_in, v_in = [sem(f"k_pages{k}") for k in range(4)], [sem(f"v_pages{k}") for k in range(4)]
        v_last_in = [sem("v_last_pages0"), sem("v_last_pages1")]
        w_out, w_in, vn_in = sem("iw_out"), sem("iw_in"), sem("v_new_in")
        h_t, h_c = sem("heads_transposed"), sem("heads_copied")
        it_done, it_copied = sem("index_transposed"), sem("index_copied")
        dt_done, dt_relu, sum_done = sem("dots"), sem("relu"), sem("summed")
        gw_done, b_done = sem("weights_ready"), sem("bias_ready")
        kt_done, kt_act, kt_dve, kn_copied = sem("k_transposed"), sem("k_copied_act"), sem("k_copied_dve"), sem("k_new_copied")
        s_done, m_done, e_done, pt_done, pt_copied = (sem("scores"), sem("max"), sem("probs"), sem("p_transposed"),
                                                      sem("p_copied"))
        o_done, y_done, y_out, y_in, yt_done, yt_copied = (sem("o"), sem("y"), sem("y_out"), sem("y_in"),
                                                           sem("yT"), sem("yT_copied"))
        dch, ach = sem("dve_step"), sem("act_step")
        zeroed = sem("qz_zeroed")

        def key_copy(g):
            if g < 8:
                return kt_act, g + 1
            return (kt_act, 8 + (g - 8) // 2 + 1) if g % 2 == 0 else (kt_dve, (g - 8) // 2 + 1)

        def copy_keys(eng, op, g):
            eng.wait_ge(kt_done, g + 1)
            op(KT[:, g // 4 % 2, 512 * (g % 4):512 * (g % 4 + 1)], ps[:, 5 + g % 2, :]).then_inc(key_copy(g)[0], 1)

        def load_pages(eng, b, cache, dst, slot, landed):
            with eng.Fori(0, PAGES) as j:
                page = eng.value_load(pages[0:1, bass.ds(j + b * PAGES, 1)], min_val=0, max_val=n_pool - 1)
                src = cache[bass.ds(page, 1)]
                src = src.rearrange("o p k d -> (o p) (k d)") if len(src.shape) == 4 else src.rearrange("o p d -> (o p) d")
                eng.dma_start(dst[:, slot, bass.ds(j, 1), :].rearrange("p o c -> p (o c)"), src).then_inc(landed, 16)

        with nc.Block() as block:
            @block.sync
            def _(sp):
                sp.dma_start(pages[:, :], A["page_table"].rearrange("(o a) b -> o (a b)", o=1)).then_inc(pin, 16)
                sp.dma_start(scr_w, Hs[0:NS, C_IW:C_IW + 8]).then_inc(w_out, 16)
                for dst, src in ((gat[:, :, :], C["gather"]), (c8[:, :], C["causal8"]), (spf, C["spread"])):
                    sp.dma_start(dst, src).then_inc(cin, 16)
                sp.wait_ge(pin, 16)
                sp.wait_ge(w_out, 16)
                for h in range(8):
                    sp.dma_start(iwd[8 * h:8 * h + 8, :], bass.AP(scr_w.tensor, h, [[8, 8], [64, 8]]),
                                 allow_slow_non_contiguous=True).then_inc(w_in, 16)
                for b in range(NB):
                    sp.dma_start(Vn[:, b, :], Hs[8 * b:8 * b + 8, C_DV:C_DV + P]).then_inc(vn_in, 16)

                for b in range(0, NB, 2):
                    if b >= 4:
                        sp.wait_ge(it_done, 4 * (b - 3))
                    load_pages(sp, b, A["cache_idx"][0], idxp, b % 4, ix_in[b % 4])
                for b in range(NB):
                    if b == 2:
                        sp.wait_ge(it_done, 4 * NB)
                    if b >= 4:
                        sp.wait_ge(kt_done, 4 * (b - 3))
                    load_pages(sp, b, A["cache_k"][0], Kp, b % 4, k_in[b % 4])
                sp.wait_ge(y_done, NP_ - 2)
                for b in range(NB - 2, NB):
                    load_pages(sp, b, A["cache_v"][0], Vp, b % 4, v_last_in[b % 2])

            @block.gpsimd
            def _(pool):
                pool.wait_ge(pin, 16)
                for b in range(1, NB, 2):
                    if b >= 4:
                        pool.wait_ge(it_done, 4 * (b - 3))
                    load_pages(pool, b, A["cache_idx"][0], idxp, b % 4, ix_in[b % 4])
                for b in range(4):
                    load_pages(pool, b, A["cache_v"][0], Vp, b % 4, v_in[b % 4])
                for p in range(NP_):
                    pool.wait_ge(y_done, p + 1)
                    for b2 in range(2):
                        pool.dma_start(bass.AP(scr_y.tensor, (2 * p + b2) * DEC_SEQ * 512, [[HD, 8], [512, DEC_SEQ], [1, HD]]),
                                       yq[64 * b2:64 * b2 + 64, p, :]).then_inc(y_out, 16)
                        if p + 3 < NP_:
                            load_pages(pool, 2 * p + 4 + b2, A["cache_v"][0], Vp, (2 * p + b2) % 4, v_in[(2 * p + b2) % 4])
                pool.wait_ge(y_out, 32 * NP_)
                pool.dma_start(Hs[0:NS, C_DQ:C_DQ + 512], scr_y).then_inc(y_in, 16)
                pool.wait_ge(y_in, 16)

            @block.tensor
            def _(pe):
                I64 = st.ident[0:NS, 0:NS]
                for h in range(8):
                    nc.tensor.transpose(ps[0:HD, 0, h * NS:(h + 1) * NS], Hs[0:NS, C_IQ + h * HD:C_IQ + (h + 1) * HD], I64)
                nc.tensor.transpose(ps[0:HD, 1, 0:NS], Hs[0:NS, C_IK:C_IK + HD], I64)
                nc.tensor.transpose(ps[:, 1, NS:2 * NS], Hs[0:NS, C_DK:C_DK + P], I64)
                for g in range(4):
                    last = nc.tensor.transpose(ps[:, 2, g * NS:(g + 1) * NS], Hs[0:NS, C_DQ + g * P:C_DQ + (g + 1) * P], I64)
                last.then_inc(h_t, 1)
                pe.wait_ge(h_c, 5)
                def index_keys_T(b, q):
                    g = 4 * b + q
                    if q == 0:
                        pe.wait_ge(ix_in[b % 4], 16 * PAGES * (b // 4 + 1))
                    if g >= 1:
                        pe.wait_ge(it_copied, g + (g - 1) // 4)
                    for j in range(4):
                        last = nc.tensor.transpose(ps[0:HD, 5, j * P:(j + 1) * P], idxp[:, b % 4, 4 * q + j, :], st.ident[:, :])
                    last.then_inc(it_done, 1)

                def add_heads(b, c):
                    g, n = 5 * b + c, CHUNKS[c][1]
                    pe.wait_ge(dt_relu, g + 1)
                    if g == 0:
                        pe.wait_ge(gw_done, 1)
                    nc.tensor.matmul(ps[0:NS, c, 0:n], gw[:, b, :], rel[:, g % 2, 0:n],
                                     start=(b == 0), stop=(b == NB - 1)).then_inc(sum_done, 1)

                for q in range(4):
                    index_keys_T(0, q)
                for b in range(NB):
                    s = b % 2
                    pe.wait_ge(it_copied, 5 * (b + 1))
                    for c, (c0, n) in enumerate(CHUNKS):
                        g = 5 * b + c
                        if g >= 2:
                            pe.wait_ge(dt_relu, g - 1)
                        nc.tensor.matmul(ps[0:NS, 6 + g % 2, 0:n], iqT[:, b, :, :].rearrange("d h q -> d (h q)"),
                                         ikT[:, s, c0:c0 + n], start=True, stop=True).then_inc(dt_done, 1)
                        if c < 4 and b + 1 < NB:
                            index_keys_T(b + 1, c)
                        if g >= 1:
                            add_heads((g - 1) // 5, (g - 1) % 5)
                add_heads(NB - 1, 4)

                def keys_T(p):
                    for b in (2 * p, 2 * p + 1):
                        pe.wait_ge(k_in[b % 4], 16 * PAGES * (b // 4 + 1))
                        for q in range(4):
                            g = 4 * b + q
                            if g >= 2:
                                pe.wait_ge(*key_copy(g - 2))
                            for j in range(4):
                                last = nc.tensor.transpose(ps[:, 5 + g % 2, j * P:(j + 1) * P], Kp[:, b % 4, 4 * q + j, :],
                                                           st.ident[:, :])
                            last.then_inc(kt_done, 1)

                def keys_copied(p):
                    pe.wait_ge(*key_copy(8 * p + 6))
                    pe.wait_ge(*key_copy(8 * p + 7))

                pe.wait_ge(dt_relu, 5 * NB)
                keys_T(0)
                for p in range(NP_):
                    keys_copied(p)
                    pe.wait_ge(kn_copied, 2 * (p + 1))
                    if p == 0:
                        pe.wait_ge(b_done, 1)
                    else:
                        pe.wait_ge(e_done, p)
                    for c, (c0, n) in enumerate(CHUNKS):
                        nc.tensor.matmul(ps[:, c, 0:n], spb[:, p, :], bias[:, c0:c0 + n], start=True, stop=False)
                        for b2 in range(2):
                            last = nc.tensor.matmul(ps[64 * b2:64 * b2 + 64, c, 0:n],
                                                    qz[:, 2 * p + b2, :, :, :].rearrange("d v g q -> d (v g q)"),
                                                    KT[:, b2, c0:c0 + n], start=False, stop=True)
                    last.then_inc(s_done, 1)
                    if p + 1 < NP_:
                        keys_T(p + 1)
                        keys_copied(p + 1)
                    pe.wait_ge(e_done, p + 1)
                    for c in range(5):
                        g = 5 * p + c
                        if g >= 2:
                            pe.wait_ge(pt_copied, g - 1)
                        for j in range(4 * c, min(4 * c + 4, PAGES + 1)):
                            n = P if j < PAGES else DEC_SEQ
                            last = nc.tensor.transpose(ps[0:n, 5 + g % 2, (j % 4) * P:(j % 4 + 1) * P],
                                                       Pb[:, j * P:j * P + n], st.ident[:, :])
                        last.then_inc(pt_done, 1)
                    pe.wait_ge(pt_copied, 5 * (p + 1))
                    pe.wait_ge(vn_in, 16 * NB)
                    if p >= 1:
                        pe.wait_ge(y_done, p)
                    for b2 in range(2):
                        vs = (2 * p + b2) % 4
                        if p < NP_ - 1:
                            pe.wait_ge(v_in[vs], 16 * PAGES * (p // 2 + 1))
                        else:
                            pe.wait_ge(v_last_in[b2], 16 * PAGES)
                        r = slice(64 * b2, 64 * b2 + 64)
                        for j in range(PAGES):
                            nc.tensor.matmul(ps[r, 7, 0:P], PT[:, j, r], Vp[:, vs, j, :], start=(j == 0), stop=False)
                        last = nc.tensor.matmul(ps[r, 7, 0:P], PT[0:DEC_SEQ, PAGES, r], Vn[:, 2 * p + b2, :], start=False, stop=True)
                    last.then_inc(o_done, 1)
                pe.wait_ge(y_in, 16)
                for k in range(KD):
                    c0 = C_GR + k * P if k < 4 else C_DQ + (k - 4) * P
                    last = nc.tensor.transpose(ps[:, 0, k * NS:(k + 1) * NS], Hs[0:NS, c0:c0 + P], I64)
                last.then_inc(yt_done, 1)

            @block.scalar
            def _(act):
                act.wait_ge(h_t, 1)
                nc.scalar.copy(iqT[:, :, :, :].rearrange("d b h q -> d h b q"),
                               ps[0:HD, 0, :].rearrange("d (h b q) -> d h b q", h=8, b=NB)).then_inc(h_c, 1)
                nc.scalar.copy(ikn[:, :], ps[0:HD, 1, 0:NS]).then_inc(h_c, 1)
                nc.scalar.copy(KnT[:, :], ps[:, 1, NS:2 * NS]).then_inc(h_c, 1)
                act.wait_ge(zeroed, 1)
                for kv in range(2):
                    hf = slice(64 * kv, 64 * kv + 64)
                    nc.scalar.copy(qz[hf, :, kv, :, :].rearrange("d b g q -> d g b q"),
                                   ps[hf, 2, 0:4 * NS].rearrange("d (g b q) -> d g b q", g=4, b=NB)).then_inc(h_c, 1)
                act.wait_ge(h_c, 5)

                for b in range(NB):
                    s = b % 2
                    if b >= 2:
                        act.wait_ge(dt_done, 5 * (b - 1))
                    for q in range(4):
                        act.wait_ge(it_done, 4 * b + q + 1)
                        nc.scalar.copy(ikT[:, s, 512 * q:512 * (q + 1)], ps[0:HD, 5, :]).then_inc(it_copied, 1)
                    nc.scalar.copy(ikT[:, s, PAST:LK], ikn[:, 8 * b:8 * b + 8]).then_inc(it_copied, 1)
                def new_keys(p):
                    for b2 in range(2):
                        b = 2 * p + b2
                        nc.scalar.copy(KT[:, b2, PAST:LK], KnT[:, 8 * b:8 * b + 8]).then_inc(kn_copied, 1)

                new_keys(0)
                for g in range(8):
                    copy_keys(act, nc.scalar.copy, g)
                for p in range(NP_):
                    act.wait_ge(m_done, p + 1)
                    if p >= 1:
                        act.wait_ge(pt_done, 5 * p)
                    nc.scalar.activation(Pb[:, :], flat[:, 0:LK], ACT.Exp, bias=nm[:, 0:1], scale=AS,
                                         accum_out=sm[:, 0:1]).then_inc(e_done, 1)
                    if p + 1 < NP_:
                        act.wait_ge(s_done, p + 1)
                        new_keys(p + 1)
                        for g in range(8 * p + 8, 8 * p + 16, 2):
                            copy_keys(act, nc.scalar.copy, g)
                act.wait_ge(yt_done, 1)
                nc.scalar.copy(XT[:, :, SEQ:NTOK], ps[:, 0, :].rearrange("p (k t) -> p k t", k=KD)).then_inc(yt_copied, 1)
                act.wait_ge(yt_copied, 1)

            @block.vector
            def _(dve):
                link = chained(dve, dch)
                nc.vector.memset(qz[:, :, :, :, :], 0.0).then_inc(zeroed, 1)
                dve.wait_ge(cin, 48)
                link(nc.vector.tensor_copy(spb[:, :, :], spf))
                dve.wait_ge(w_in, 128)
                for b in range(NB):
                    link(nc.vector.tensor_scalar(gw[:, b, :], gat[:, b, :], iwd[:, b:b + 1], IWS, ALU.mult, ALU.mult))
                dve.sem_inc(gw_done, 1)
                for b in range(NB):
                    for c, (c0, n) in enumerate(CHUNKS):
                        g = 5 * b + c
                        dve.wait_ge(dt_done, g + 1)
                        if g >= 2:
                            dve.wait_ge(sum_done, g - 1)
                        nc.vector.tensor_scalar(rel[:, g % 2, 0:n], ps[0:NS, 6 + g % 2, 0:n], 0.0, None, ALU.max).then_inc(dt_relu, 1)
                dve.wait_ge(sum_done, 5 * NB)
                link(nc.vector.tensor_copy(sc[:, 0:PAST], ps[0:NS, 0:4, :].rearrange("p b n -> p (b n)")))
                link(nc.vector.tensor_tensor(sc[:, PAST:LK], ps[0:NS, 4, 0:8], c8[:, :], ALU.add))
                for k in range(TOPK // 8):
                    src = sc if k == 0 else wk
                    link(nc.vector.max(m8[:, :], src[:, :]))
                    link(nc.vector.match_replace(wk[:, :], m8[:, :], src[:, :], TAKEN))
                nc.vector.tensor_scalar(bias[:, :], wk[:, :], -2e38, NEG, ALU.is_ge, ALU.mult).then_inc(b_done, 1)
                for p in range(NP_):
                    dve.wait_ge(s_done, p + 1)
                    link(nc.vector.reduce_max(mx[:, :], flat[:, 0:LK], AX_X))
                    if p >= 1:
                        dve.wait_ge(e_done, p)
                    nc.vector.tensor_scalar(nm[:, :], mx[:, :], -AS, None, ALU.mult).then_inc(m_done, 1)
                    if p + 1 < NP_:
                        for g in range(8 * p + 9, 8 * p + 16, 2):
                            copy_keys(dve, nc.vector.tensor_copy, g)
                    if p >= 1:
                        dve.wait_ge(o_done, p)
                    for c in range(5):
                        g = 5 * p + c
                        dve.wait_ge(pt_done, g + 1)
                        if c < 4:
                            nc.vector.tensor_copy(PT[:, 4 * c:4 * c + 4, :],
                                                  ps[:, 5 + g % 2, :].rearrange("p (a t) -> p a t", a=4)).then_inc(pt_copied, 1)
                        else:
                            nc.vector.tensor_copy(PT[0:DEC_SEQ, PAGES, :], ps[0:DEC_SEQ, 5 + g % 2, 0:P]).then_inc(pt_copied, 1)
                    dve.wait_ge(e_done, p + 1)
                    link(nc.vector.reciprocal(rs[:, :], sm[:, :]))
                    dve.wait_ge(o_done, p + 1)
                    for b2 in range(2):
                        for kv in range(2):
                            r = slice(64 * b2 + 32 * kv, 64 * b2 + 32 * kv + 32)
                            ins = nc.vector.tensor_scalar(yq[r, p, :], ps[r, 7, kv * HD:(kv + 1) * HD], rs[r, 0:1],
                                                          None, ALU.mult)
                    ins.then_inc(y_done, 1)


class LayerNorm:

    def __init__(self, st, ctx, tag, l, which, X, A):
        nc = st.nc
        self.nc, self.X = nc, X
        self.src = [bcast_rows(A["ln_g"][l, which], D), bcast_rows(A["ln_b"][l, which], D)]
        sb = lambda n, s: ctx.enter_context(nc.sbuf_tensor(f"{tag}_{n}", s, F32))
        self.gb, self.stats, self.mv, self.rstd = (sb("gb", [P, 2, D]), sb("stats", [P, TILES, 12]), sb("mv", [P, TILES, 2]),
                                                   sb("rstd", [P, TILES, 1]))
        self.gb_in, self.var_ready, self.std_ready, self.rstd_ready, self.gained, self.scaled, self.norm_done = (
            st.sem(f"{tag}_{n}") for n in ("gb_in", "var_ready", "std_ready", "rstd_ready", "gained", "scaled", "norm_done"))

    def load(self, eng):
        for k in range(2):
            eng.dma_start(self.gb[:, k, :], self.src[k]).then_inc(self.gb_in, 16)

    def dve_half_stats(self, i, h, link):
        link(self.nc.vector.bn_stats(self.stats[0:rows(i), i, 6 * h:6 * h + 6], self.X[0:rows(i), i, 512 * h:512 * h + 512]))

    def dve_center(self, dve, i, link):
        r, v, x = rows(i), self.nc.vector, self.X[0:rows(i), i, :]
        link(v.bn_aggr(self.mv[0:r, i, :], self.stats[0:r, i, :]))
        v.tensor_scalar(self.mv[0:r, i, 1:2], self.mv[0:r, i, 1:2], LN_EPS, None, ALU.add).then_inc(self.var_ready, 1)
        if i == 0:
            dve.wait_ge(self.gb_in, 32)
        v.scalar_tensor_tensor(out=x, in0=x, scalar=self.mv[0:r, i, 0:1], in1=self.gb[0:r, 0, :],
                               op0=ALU.subtract, op1=ALU.mult).then_inc(self.gained, 1)

    def act(self, act, i):
        r = rows(i)
        act.wait_ge(self.var_ready, i + 1)
        self.nc.scalar.activation(self.rstd[0:r, i, :], self.mv[0:r, i, 1:2], ACT.Sqrt).then_inc(self.std_ready, 1)

    def act_scale(self, act, i):
        x = self.X[0:rows(i), i, :]
        act.wait_ge(self.gained, i + 1)
        act.wait_ge(self.rstd_ready, i + 1)
        self.nc.scalar.activation(x, x, ACT.Identity, scale=self.rstd[0:rows(i), i, :]).then_inc(self.scaled, 1)

    def dve_rstd(self, dve, i):
        r = rows(i)
        dve.wait_ge(self.std_ready, i + 1)
        self.nc.vector.reciprocal(self.rstd[0:r, i, :], self.rstd[0:r, i, :]).then_inc(self.rstd_ready, 1)

    def pool(self, pool, i):
        r, x = rows(i), self.X[0:rows(i), i, :]
        pool.wait_ge(self.scaled, i + 1)
        self.nc.gpsimd.tensor_tensor(x, x, self.gb[0:r, 1, :], ALU.add).then_inc(self.norm_done, 1)


def out_projection(nc, st, A, w, l, XT, x_prompt, x_sample, h_hi, h_lo):
    tag = f"out{l}"
    with ExitStack() as ctx:
        sem = lambda n: st.sem(f"{tag}_{n}")
        X = ctx.enter_context(nc.sbuf_tensor(f"{tag}_X", [P, TILES, D], F32))
        wbuf = ctx.enter_context(nc.sbuf_tensor(f"{tag}_w", [P, 2, KD, 512], F32))
        ps = ctx.enter_context(nc.psum_tensor(f"{tag}_ps", [P, 8, 512], F32))
        ln = LayerNorm(st, ctx, f"{tag}_ln", l, 0, X, A)
        w_in, x_in, saved = [sem("w_in0"), sem("w_in1")], sem("x_in"), sem("x_saved")
        mm_done, added, t_done, hi_done, lo_done, dch = (sem("mm_done"), sem("added"), sem("transposed"), sem("hi_done"),
                                                  sem("lo_done"), sem("dve_step"))
        w_v = w.rearrange("(k p) n -> p k n", p=P)
        with nc.Block() as block:
            @block.sync
            def _(sp):
                for c in range(2):
                    sp.dma_start(wbuf[:, c, :, :], w_v[:, :, 512 * c:512 * c + 512]).then_inc(w_in[c], 16)
                ln.load(sp)
                for i in range(TILES):
                    sp.wait_ge(ln.norm_done, i + 1)
                    sp.dma_start(st.x_dram[i * P:i * P + rows(i), :], X[0:rows(i), i, :]).then_inc(saved, 16)
                sp.wait_ge(saved, 16 * TILES)

            @block.tensor
            def _(pe):
                def transposes(i):
                    pe.wait_ge(ln.norm_done, i + 1)
                    for h in range(2):
                        j, r = 2 * i + h, rows(i)
                        if j >= 4:
                            pe.wait_ge(lo_done, j - 3)
                        for k in range(4):
                            kk = 4 * h + k
                            last = nc.tensor.transpose(ps[:, 4 + j % 4, k * P:k * P + r], X[0:r, i, kk * P:(kk + 1) * P],
                                                       st.ident[0:r, 0:r])
                        last.then_inc(t_done, 1)

                LAG = 2
                for i in range(TILES):
                    r = rows(i)
                    for c in range(2):
                        s = 2 * i + c
                        if i == 0:
                            pe.wait_ge(w_in[c], 16)
                        if s >= 4:
                            pe.wait_ge(added, s - 3)
                        for k in range(KD):
                            last = nc.tensor.matmul(ps[0:r, s % 4, :], XT[:, k, i * P:i * P + r], wbuf[:, c, k, :],
                                                    start=(k == 0), stop=(k == KD - 1))
                        last.then_inc(mm_done, 1)
                    if i >= LAG:
                        transposes(i - LAG)
                for i in range(TILES - LAG, TILES):
                    transposes(i)

            @block.scalar
            def _(act):
                def split_hi(i):
                    for h in range(2):
                        j, r = 2 * i + h, rows(i)
                        act.wait_ge(t_done, j + 1)
                        nc.scalar.copy(h_hi[:, 4 * h:4 * h + 4, i * P:i * P + r],
                                       ps[:, 4 + j % 4, :].rearrange("p (k t) -> p k t", k=4)[:, :, 0:r]).then_inc(hi_done, 1)

                for i in range(TILES):
                    ln.act(act, i)
                    if i >= 1:
                        ln.act_scale(act, i - 1)
                    if i >= 2:
                        split_hi(i - 2)
                ln.act_scale(act, TILES - 1)
                split_hi(TILES - 2)
                split_hi(TILES - 1)

            @block.gpsimd
            def _(pool):
                pool.dma_start(X[:, 0:NT, :], x_prompt.rearrange("(i p) c -> p i c", p=P)).then_inc(x_in, 16)
                pool.dma_start(X[0:NS, NT, :], x_sample).then_inc(x_in, 16)
                for i in range(TILES):
                    ln.pool(pool, i)

            @block.vector
            def _(dve):
                link = chained(dve, dch)

                def split_lo(i):
                    for h in range(2):
                        j, r = 2 * i + h, rows(i)
                        at = (slice(None), slice(4 * h, 4 * h + 4), slice(i * P, i * P + r))
                        dve.wait_ge(hi_done, j + 1)
                        nc.vector.tensor_tensor(h_lo[at], ps[:, 4 + j % 4, :].rearrange("p (k t) -> p k t", k=4)[:, :, 0:r],
                                                h_hi[at].bitcast(F32), ALU.subtract).then_inc(lo_done, 1)

                dve.wait_ge(x_in, 32)
                for i in range(TILES):
                    r = rows(i)
                    for c in range(2):
                        s = 2 * i + c
                        dve.wait_ge(mm_done, s + 1)
                        xs = X[0:r, i, 512 * c:512 * c + 512]
                        nc.vector.scalar_tensor_tensor(out=xs, in0=xs, scalar=ALPHA, in1=ps[0:r, s % 4, :],
                                                       op0=ALU.mult, op1=ALU.add).then_inc(added, 1)
                    dve.wait_ge(added, 2 * i + 2)
                    for h in range(2):
                        ln.dve_half_stats(i, h, link)
                    ln.dve_center(dve, i, link)
                    if i >= 1:
                        ln.dve_rstd(dve, i - 1)
                    if i >= 3:
                        split_lo(i - 3)
                ln.dve_rstd(dve, TILES - 1)
                for i in range(TILES - 3, TILES):
                    split_lo(i)
                dve.wait_ge(lo_done, 2 * TILES)


TOKC = [(0, 384), (384, 384), (768, 320)]
NF = 256


def ffn_up(nc, st, w, tag, h_hi, h_lo, aT):
    w_v = w.rearrange("(k p) n -> p k n", p=P)
    with ExitStack() as ctx:
        sem = lambda n: st.sem(f"{tag}_{n}")
        raw = ctx.enter_context(nc.sbuf_tensor(f"{tag}_raw", [P, 2, KD, P], F32))
        w_hi = ctx.enter_context(nc.sbuf_tensor(f"{tag}_whi", [P, 2, KD, P], F32R))
        w_lo = ctx.enter_context(nc.sbuf_tensor(f"{tag}_wlo", [P, 2, KD, P], F32R))
        sg = ctx.enter_context(nc.sbuf_tensor(f"{tag}_sg", [P, 3, 384], F32))
        ps = ctx.enter_context(nc.psum_tensor(f"{tag}_ps", [P, 3, 2, 512], F32))
        w_in, w_split_hi, w_split = ([sem(f"{n}{k}") for k in range(2)] for n in ("w_in", "w_split_hi", "w_split"))
        mm_done = [sem("gate_done"), sem("up_done")]
        silu_done, prod_done = sem("silu_done"), sem("prod_done")
        with nc.Block() as block:
            @block.sync
            def _(sp):
                def load(ff, k2):
                    sp.dma_start(raw[:, k2, :, :], w_v[:, :, bass.ds(ff * P + k2 * D_FF, P)]).then_inc(w_in[k2], 16)
                load(0, 0)
                load(0, 1)
                with sp.Fori(1, KF) as ff:
                    for k2 in range(2):
                        sp.wait_ge(w_split[k2], ff)
                        load(ff, k2)

            @block.tensor
            def _(pe):
                def body(ff, first):
                    for k2 in range(2):
                        pe.wait_ge(w_split[k2], ff + 1)
                        for t, (t0, n) in enumerate(TOKC):
                            if not first:
                                pe.wait_ge((silu_done, prod_done)[k2], ff * 3 + (t - 2))
                            for k in range(KD):
                                parts = ((w_hi, h_hi), (w_hi, h_lo), (w_lo, h_hi))
                                for j, (wp, hp) in enumerate(parts):
                                    last = nc.tensor.matmul(ps[:, t, k2, 0:n], wp[:, k2, k, :], hp[:, k, t0:t0 + n],
                                                            start=(k == 0 and j == 0), stop=(k == KD - 1 and j == 2))
                            last.then_inc(mm_done[k2], 1)
                body(0, True)
                with pe.Fori(1, KF) as ff:
                    body(ff, False)

            @block.scalar
            def _(act):
                def split_hi(ff, k2, first):
                    act.wait_ge(w_in[k2], ff * 16 + 16)
                    if not first:
                        act.wait_ge(mm_done[k2], ff * 3)
                    nc.scalar.copy(w_hi[:, k2, :, :], raw[:, k2, :, :]).then_inc(w_split_hi[k2], 1)

                def body(ff, first, last):
                    for t, (t0, n) in enumerate(TOKC):
                        act.wait_ge(mm_done[0], ff * 3 + (t + 1))
                        if not first:
                            act.wait_ge(prod_done, ff * 3 + (t - 2))
                        nc.scalar.activation(sg[:, t, 0:n], ps[:, t, 0, 0:n], ACT.Silu).then_inc(silu_done, 1)
                    if not last:
                        split_hi(ff + 1, 0, False)
                        split_hi(ff + 1, 1, False)

                split_hi(0, 0, True)
                split_hi(0, 1, True)
                body(0, True, False)
                with act.Fori(1, KF - 1) as ff:
                    body(ff, False, False)
                body(KF - 1, False, True)

            @block.vector
            def _(dve):
                def split_lo(ff, k2):
                    dve.wait_ge(w_split_hi[k2], ff + 1)
                    nc.vector.tensor_tensor(w_lo[:, k2, :, :], raw[:, k2, :, :], w_hi[:, k2, :, :].bitcast(F32),
                                            ALU.subtract).then_inc(w_split[k2], 1)

                def body(ff, last):
                    if not last:
                        split_lo(ff + 1, 0)
                    for t, (t0, n) in enumerate(TOKC):
                        dve.wait_ge(silu_done, ff * 3 + (t + 1))
                        dve.wait_ge(mm_done[1], ff * 3 + (t + 1))
                        nc.vector.tensor_tensor(aT[:, bass.ds(ff, 1), t0:t0 + n].rearrange("p o n -> p (o n)"),
                                                sg[:, t, 0:n], ps[:, t, 1, 0:n], ALU.mult).then_inc(prod_done, 1)
                    if not last:
                        split_lo(ff + 1, 1)

                split_lo(0, 0)
                split_lo(0, 1)
                with dve.Fori(0, KF - 1) as ff:
                    body(ff, False)
                body(KF - 1, True)
                dve.wait_ge(prod_done, 3 * KF)


def ffn_down(nc, st, A, l, tag, aT, XT, y_out):
    NCH, KH, NB = D // NF, KF // 2, (TILES + 1) // 2
    GROUPS = [(0, 6), (6, KH)]
    w_v = A["ffn_w_down"][l].rearrange("(k p) n -> p k n", p=P)
    with ExitStack() as ctx:
        sem = lambda n: st.sem(f"{tag}_{n}")
        X = ctx.enter_context(nc.sbuf_tensor(f"{tag}_X", [P, TILES, D], F32))
        raw = ctx.enter_context(nc.sbuf_tensor(f"{tag}_w", [P, KH, NF], F32))
        w_hi, w_lo = (ctx.enter_context(nc.sbuf_tensor(f"{tag}_w_{n}", [P, 2, NF], F32R)) for n in ("hi", "lo"))
        a_hi, a_lo = (ctx.enter_context(nc.sbuf_tensor(f"{tag}_a_{n}", [P, 2, NTOK], F32R)) for n in ("hi", "lo"))
        ps = ctx.enter_context(nc.psum_tensor(f"{tag}_ps", [P, 8, 512], F32))
        ln = LayerNorm(st, ctx, f"{tag}_ln", l, 1, X, A)
        w_in, split_hi, split = [sem("w_in0"), sem("w_in1")], sem("split_hi"), sem("split")
        block_done, bank_done = sem("block_done"), sem("bank_done")
        added, t_done, t_copied, dch = sem("added"), sem("transposed"), sem("copied"), sem("dve_step")
        stored, x_in = sem("stored"), sem("x_in")

        def acc(i):
            return ps[0:rows(i), i // 2, (i % 2) * NF:(i % 2 + 1) * NF]

        with nc.Block() as block:
            @block.sync
            def _(sp):
                def load(c, first):
                    for h in range(2):
                        for q, (k0, k1) in enumerate(GROUPS):
                            if not (first and h == 0):
                                sp.wait_ge(split, c * KF + (KH * (h - 1) + k1))
                            sp.dma_start(raw[:, k0:k1, :], w_v[:, KH * h + k0:KH * h + k1, bass.ds(c * NF, NF)]).then_inc(w_in[q], 16)
                load(0, True)
                ln.load(sp)
                with sp.Fori(1, NCH) as c:
                    load(c, False)
                for i in range(TILES):
                    sp.wait_ge(ln.norm_done, i + 1)
                    sp.dma_start(y_out(i), X[0:rows(i), i, :]).then_inc(stored, 16)
                sp.wait_ge(stored, 16 * TILES)

            @block.tensor
            def _(pe):
                def products(c, first):
                    for k in range(KF):
                        pe.wait_ge(split, c * KF + (k + 1))
                        for i in range(TILES):
                            if k == 0 and i % 2 == 0 and not first:
                                pe.wait_ge(added, c * TILES + (min(i + 2, TILES) - TILES))
                            for j, (ap, wp) in enumerate(((a_hi, w_hi), (a_lo, w_hi), (a_hi, w_lo))):
                                last = nc.tensor.matmul(acc(i), ap[:, k % 2, i * P:i * P + rows(i)], wp[:, k % 2, :],
                                                        start=(k == 0 and j == 0 and i % 2 == 0),
                                                        stop=(k == KF - 1 and j == 2), skip_group_check=True)
                            if k == KF - 1 and (i % 2 == 1 or i == TILES - 1):
                                last.then_inc(bank_done, 1)
                        if k < KF - 1:
                            last.then_inc(block_done, 1)

                products(0, True)
                with pe.Fori(1, NCH) as c:
                    products(c, False)

                def transposes(i):
                    pe.wait_ge(ln.norm_done, i + 1)
                    for h in range(2):
                        j, r = 2 * i + h, rows(i)
                        if j >= 2:
                            pe.wait_ge(t_copied, j - 1)
                        for k in range(4):
                            kk = 4 * h + k
                            last = nc.tensor.transpose(ps[:, 6 + j % 2, k * P:k * P + r], X[0:r, i, kk * P:(kk + 1) * P],
                                                       st.ident[0:r, 0:r])
                        last.then_inc(t_done, 1)

                if XT is not None:
                    for i in range(TILES):
                        transposes(i)

            @block.scalar
            def _(act):
                def splits(c, first):
                    for k in range(KF):
                        h, s = k // KH, k % KH
                        for q, (k0, _) in enumerate(GROUPS):
                            if s == k0:
                                act.wait_ge(w_in[q], c * 32 + 16 * (h + 1))
                        if k >= 2:
                            act.wait_ge(block_done, c * (KF - 1) + (k - 1))
                        elif k == 0 and not first:
                            act.wait_ge(block_done, c * (KF - 1))
                        elif k == 1 and not first:
                            act.wait_ge(bank_done, c * NB)
                        nc.scalar.copy(a_hi[:, k % 2, :], aT[:, k, :])
                        nc.scalar.copy(w_hi[:, k % 2, :], raw[:, s, :]).then_inc(split_hi, 1)

                splits(0, True)
                with act.Fori(1, NCH) as c:
                    splits(c, False)

                def copy_t(i):
                    for h in range(2):
                        j, r = 2 * i + h, rows(i)
                        act.wait_ge(t_done, j + 1)
                        nc.scalar.copy(XT[:, 4 * h:4 * h + 4, i * P:i * P + r],
                                       ps[:, 6 + j % 2, :].rearrange("p (k t) -> p k t", k=4)[:, :, 0:r]).then_inc(t_copied, 1)
                for i in range(TILES):
                    ln.act(act, i)
                    if i >= 1:
                        ln.act_scale(act, i - 1)
                    if XT is not None and i >= 3:
                        copy_t(i - 3)
                ln.act_scale(act, TILES - 1)
                if XT is not None:
                    for i in range(TILES - 3, TILES):
                        copy_t(i)

            @block.gpsimd
            def _(pool):
                pool.dma_start(X[:, 0:NT, :], st.x_dram[0:SEQ, :].rearrange("(i p) c -> p i c", p=P)).then_inc(x_in, 16)
                pool.dma_start(X[0:NS, NT, :], st.x_dram[SEQ:NTOK, :]).then_inc(x_in, 16)
                for i in range(TILES):
                    ln.pool(pool, i)

            @block.vector
            def _(dve):
                link = chained(dve, dch)

                def add(c, i):
                    xs = X[0:rows(i), i, bass.ds(c * NF, NF)]
                    nc.vector.scalar_tensor_tensor(out=xs, in0=xs, scalar=ALPHA, in1=acc(i), op0=ALU.mult,
                                                   op1=ALU.add).then_inc(added, 1)

                def splits(c, first):
                    for k in range(KF):
                        dve.wait_ge(split_hi, c * KF + (k + 1))
                        nc.vector.tensor_tensor(a_lo[:, k % 2, :], aT[:, k, :], a_hi[:, k % 2, :].bitcast(F32), ALU.subtract)
                        nc.vector.tensor_tensor(w_lo[:, k % 2, :], raw[:, k % KH, :], w_hi[:, k % 2, :].bitcast(F32),
                                                ALU.subtract).then_inc(split, 1)
                        if k == 1 and not first:
                            for i in range(TILES):
                                dve.wait_ge(bank_done, c * NB + (i // 2 + 1 - NB))
                                add(c - 1, i)

                splits(0, True)
                dve.wait_ge(x_in, 32)
                with dve.Fori(1, NCH) as c:
                    splits(c, False)
                dve.wait_ge(added, (NCH - 1) * TILES)
                for i in range(TILES):
                    ln.dve_half_stats(i, 0, link)
                for i in range(TILES):
                    dve.wait_ge(bank_done, (NCH - 1) * NB + i // 2 + 1)
                    add(NCH - 1, i)
                    dve.wait_ge(added, (NCH - 1) * TILES + i + 1)
                    ln.dve_half_stats(i, 1, link)
                    ln.dve_center(dve, i, link)
                    if i >= 1:
                        ln.dve_rstd(dve, i - 1)
                ln.dve_rstd(dve, TILES - 1)
                dve.wait_ge(ln.rstd_ready, TILES)


SQ, SK, SV = 0, 1024, 1280
SCOLS = 1536


def swa_prompt(nc, st, A, C, O, H, XT):
    units = [(m, v) for m in range(2) for v in range(2)]
    NU = len(units)
    with ExitStack() as ctx:
        sb = lambda n, s, d=F32: ctx.enter_context(nc.sbuf_tensor(f"swa_{n}", s, d))
        sem = lambda n: st.sem(f"swa_{n}")
        cs = sb("cos", [P, TILES, 32])
        sn = sb("sin", [P, TILES, 32])
        xc, xs = sb("xc", [P, 2, 20, 2, 32]), sb("xs", [P, 2, 20, 2, 32])
        KT, qT = sb("KT", [P, 2, SEQ]), sb("qT", [P, 8, P])
        band_f, band, identb = sb("bandf", [P, 2 * P]), sb("band", [P, 2 * P], BF16), sb("identb", [P, P], BF16)
        sinks = sb("sinks", [P, 16])
        mx, nm, es, sm, rs = sb("mx", [P, 16]), sb("nm", [P, 16]), sb("es", [P, 16]), sb("sm", [P, 16]), sb("rs", [P, 16])
        Pb, PT = sb("P", [P, 2, 4, 2 * P]), sb("PT", [P, 2, 8, P])
        ps = ctx.enter_context(nc.psum_tensor("swa_ps", [P, 8, 512], F32))
        cin, rot_c, rot_s, rot_done, dch = sem("const_in"), sem("cos_done"), sem("sin_done"), sem("rotated"), sem("dve_step")
        t_done, t_copied = sem("transposed"), sem("transposed_copied")
        s_done, m_done, e_done, ds_done, es_done = sem("scores"), sem("max"), sem("probs"), sem("sink_diff"), sem("sink_exp")
        pt_done, pt_dve, pt_act, o_done = sem("p_transposed"), sem("p_copied_dve"), sem("p_copied_act"), sem("o")
        y_done, yt_done, yt_copied, stored = sem("y"), sem("yT"), sem("yT_copied"), sem("stored")
        const_ready = sem("const_ready")

        with nc.Block() as block:
            @block.sync
            def _(sp):
                for dst, src in ((cs[:, :, :], C["cos"]), (sn[:, :, :], C["sin"]), (band_f[:, :], C["band"]),
                                 (sinks[:, :], bcast_rows(A["swa_sinks"], 16))):
                    sp.dma_start(dst, src).then_inc(cin, 16)
                sp.wait_ge(rot_done, NT)
                sp.dma_start(O[6][0, 0].rearrange("w k d -> w (k d)"), H[:, NT - 1, SK:SK + 256]).then_inc(stored, 16)
                sp.dma_start(O[7][0, 0].rearrange("w k d -> w (k d)"), H[:, NT - 1, SV:SV + 256]).then_inc(stored, 16)
                sp.wait_ge(stored, 32)

            @block.gpsimd
            def _(pool):
                pool.wait_ge(cin, 64)
                for i in range(TILES):
                    r = rows(i)
                    if i >= 2:
                        pool.wait_ge(rot_done, i - 1)
                    x4 = H[0:r, i, SQ:SV].rearrange("p (h f d) -> p (h f) d", f=2, d=32)
                    nc.gpsimd.tensor_tensor(xs[0:r, i % 2, :, :, :].rearrange("p h f d -> p (h f) d"), x4,
                                            sn[0:r, i:i + 1, :].to_broadcast([r, 40, 32]), ALU.mult).then_inc(rot_s, 1)
                    pool.wait_ge(rot_s, i + 1)
                    pool.wait_ge(rot_c, i + 1)
                    x3 = H[0:r, i, SQ:SV].rearrange("p (h f d) -> p h f d", f=2, d=32)
                    nc.gpsimd.tensor_tensor(x3[:, :, 0, :], xc[0:r, i % 2, :, 0, :], xs[0:r, i % 2, :, 1, :], ALU.subtract)
                    nc.gpsimd.tensor_tensor(x3[:, :, 1, :], xc[0:r, i % 2, :, 1, :], xs[0:r, i % 2, :, 0, :], ALU.add).then_inc(rot_done, 1)

            @block.tensor
            def _(pe):
                pe.wait_ge(const_ready, 1)
                for i in range(NT):
                    T = H[:, i, :]
                    w, k0 = (P, P) if i == 0 else (2 * P, 0)
                    c0 = max(i - 1, 0) * P
                    pe.wait_ge(rot_done, i + 1)
                    if i >= 1:
                        pe.wait_ge(yt_copied, 2 * i)
                    for j in range(8):
                        nc.tensor.transpose(ps[:, 4 + j // 4, (j % 4) * P:(j % 4 + 1) * P], T[:, SQ + j * P:SQ + (j + 1) * P],
                                            st.ident[:, :])
                    if i >= 1:
                        pe.wait_ge(y_done, i)
                    for m in range(2):
                        last = nc.tensor.transpose(ps[:, 6, m * P:(m + 1) * P], T[:, SK + m * P:SK + (m + 1) * P], st.ident[:, :])
                    last.then_inc(t_done, 1)
                    pe.wait_ge(t_copied, 3 * (i + 1))

                    def scores(u):
                        m, v = units[u]
                        a, hf = i * NU + u, slice(64 * v, 64 * v + 64)
                        if a >= 2:
                            pe.wait_ge(e_done, a - 1)
                        for b in range(2):
                            o2 = ps[:, 2 * v + b, 0:2 * w]
                            nc.tensor.matmul(o2.rearrange("p (a n) -> p a n", a=2), identb[:, :],
                                             band[:, k0:k0 + w].unsqueeze(1).to_broadcast([P, 2, w]), start=True, stop=False,
                                             skip_group_check=True)
                            for g2 in range(2):
                                last = nc.tensor.matmul(o2[:, g2 * w:(g2 + 1) * w], qT[hf, 4 * m + 2 * b + g2, :],
                                                        KT[hf, m, c0:c0 + w], start=False, stop=True, skip_group_check=True)
                        last.then_inc(s_done, 1)

                    def attend(u):
                        m, v = units[u]
                        a = i * NU + u
                        pe.wait_ge(e_done, a + 1)
                        if a >= 1:
                            pe.wait_ge(pt_dve, a)
                            pe.wait_ge(pt_act, a)
                        nb = w // P
                        for g in range(4):
                            for b in range(nb):
                                last = nc.tensor.transpose(ps[:, 4 + g // 2, ((g % 2) * nb + b) * P:((g % 2) * nb + b + 1) * P],
                                                           Pb[:, a % 2, g, b * P:(b + 1) * P], st.ident[:, :])
                        last.then_inc(pt_done, 1)
                        pe.wait_ge(pt_dve, a + 1)
                        pe.wait_ge(pt_act, a + 1)
                        for g in range(4):
                            h = (2 * m + v) * 4 + g
                            for b in range(nb):
                                last = nc.tensor.matmul(ps[:, 6 + m, (h % 8) * HD:(h % 8 + 1) * HD], PT[:, a % 2, g * nb + b, :],
                                                        H[:, c0 // P + b, SV + (2 * m + v) * HD:SV + (2 * m + v + 1) * HD],
                                                        start=(b == 0), stop=(b == nb - 1))
                        last.then_inc(o_done, 1)

                    scores(0)
                    for u in range(NU):
                        if u + 1 < NU:
                            scores(u + 1)
                        attend(u)
                    pe.wait_ge(y_done, i + 1)
                    for k in range(KD):
                        last = nc.tensor.transpose(ps[:, 4 + k // 4, (k % 4) * P:(k % 4 + 1) * P], T[:, k * P:(k + 1) * P],
                                                   st.ident[:, :])
                        if k % 4 == 3:
                            last.then_inc(yt_done, 1)

            @block.scalar
            def _(act):
                for i in range(NT):
                    nb = 1 if i == 0 else 2
                    act.wait_ge(t_done, i + 1)
                    for j in range(2):
                        nc.scalar.copy(qT[:, 4 * j:4 * j + 4, :], ps[:, 4 + j, :].rearrange("p (a t) -> p a t", a=4)).then_inc(t_copied, 1)
                    nc.scalar.copy(KT[:, :, i * P:(i + 1) * P], ps[:, 6, 0:2 * P].rearrange("p (a t) -> p a t", a=2)).then_inc(t_copied, 1)

                    def exps(u):
                        m, v = units[u]
                        a = i * NU + u
                        act.wait_ge(m_done, a + 1)
                        if a >= 2:
                            act.wait_ge(pt_done, a - 1)
                        for g in range(4):
                            h = 4 * (2 * m + v) + g
                            w = nb * P
                            ins = nc.scalar.activation(Pb[:, a % 2, g, 0:w], ps[:, 2 * v + g // 2, (g % 2) * w:(g % 2 + 1) * w],
                                                       ACT.Exp, bias=nm[:, h:h + 1], scale=AS, accum_out=sm[:, h:h + 1])
                        ins.then_inc(e_done, 1)

                    def copy_pt(u):
                        a = i * NU + u
                        if a >= 2:
                            act.wait_ge(o_done, a - 1)
                        act.wait_ge(pt_done, a + 1)
                        nc.scalar.copy(PT[:, a % 2, 2 * nb:4 * nb, :],
                                       ps[:, 5, 0:2 * nb * P].rearrange("p (a t) -> p a t", t=P)).then_inc(pt_act, 1)

                    exps(0)
                    for u in range(NU):
                        if u + 1 < NU:
                            exps(u + 1)
                        copy_pt(u)
                    act.wait_ge(ds_done, i + 1)
                    nc.scalar.activation(es[:, :], es[:, :], ACT.Exp).then_inc(es_done, 1)
                    for k in range(2):
                        act.wait_ge(yt_done, 2 * i + k + 1)
                        nc.scalar.copy(XT[:, 4 * k:4 * k + 4, i * P:(i + 1) * P],
                                       ps[:, 4 + k, :].rearrange("p (a t) -> p a t", a=4)).then_inc(yt_copied, 1)

            @block.vector
            def _(dve):
                link = chained(dve, dch)
                dve.wait_ge(cin, 64)
                link(nc.vector.tensor_copy(identb[:, :], st.ident[:, :]))
                link(nc.vector.tensor_copy(band[:, :], band_f[:, :]))
                dve.sem_inc(const_ready, 1)

                def rotate(i):
                    r = rows(i)
                    if i >= 2:
                        dve.wait_ge(rot_done, i - 1)
                    nc.vector.tensor_tensor(xc[0:r, i % 2, :, :, :].rearrange("p h f d -> p (h f) d"),
                                            H[0:r, i, SQ:SV].rearrange("p (h d) -> p h d", d=32),
                                            cs[0:r, i:i + 1, :].to_broadcast([r, 40, 32]), ALU.mult).then_inc(rot_c, 1)

                rotate(0)
                rotate(1)
                for i in range(NT):
                    nb = 1 if i == 0 else 2
                    w = nb * P

                    def row_max(u):
                        m, v = units[u]
                        a, h0 = i * NU + u, 4 * (2 * m + v)
                        h4 = slice(h0, h0 + 4)
                        dve.wait_ge(s_done, a + 1)
                        if nb == 2:
                            link(nc.vector.reduce_max(mx[:, h4], ps[:, 2 * v:2 * v + 2, :].rearrange("p b (g n) -> p (b g) n", g=2), AX_X))
                        else:
                            for b in range(2):
                                link(nc.vector.reduce_max(mx[:, h0 + 2 * b:h0 + 2 * b + 2],
                                                          ps[:, 2 * v + b, 0:2 * w].rearrange("p (g n) -> p g n", g=2), AX_X))
                        link(nc.vector.scalar_tensor_tensor(out=mx[:, h4], in0=mx[:, h4], scalar=AS, in1=sinks[:, h4],
                                                            op0=ALU.mult, op1=ALU.max))
                        nc.vector.tensor_scalar(nm[:, h4], mx[:, h4], -1.0, None, ALU.mult).then_inc(m_done, 1)

                    def copy_pt(u):
                        a = i * NU + u
                        if a >= 2:
                            dve.wait_ge(o_done, a - 1)
                        dve.wait_ge(pt_done, a + 1)
                        nc.vector.tensor_copy(PT[:, a % 2, 0:2 * nb, :],
                                              ps[:, 4, 0:2 * nb * P].rearrange("p (a t) -> p a t", t=P)).then_inc(pt_dve, 1)

                    if i >= 1:
                        dve.wait_ge(e_done, i * NU)
                        dve.wait_ge(y_done, i)
                    row_max(0)
                    for u in range(NU):
                        if u + 1 < NU:
                            row_max(u + 1)
                        if u == 2 and i + 2 < TILES:
                            rotate(i + 2)
                        copy_pt(u)
                    nc.vector.tensor_tensor(es[:, :], sinks[:, :], mx[:, :], ALU.subtract).then_inc(ds_done, 1)
                    dve.wait_ge(es_done, i + 1)
                    dve.wait_ge(e_done, (i + 1) * NU)
                    link(nc.vector.tensor_tensor(rs[:, :], sm[:, :], es[:, :], ALU.add))
                    link(nc.vector.reciprocal(rs[:, :], rs[:, :]))
                    dve.wait_ge(o_done, (i + 1) * NU)
                    for m in range(2):
                        ins = nc.vector.tensor_tensor(
                            H[:, i, SQ + 512 * m:SQ + 512 * m + 512].rearrange("p (h d) -> p h d", d=HD),
                            ps[:, 6 + m, :].rearrange("p (h d) -> p h d", d=HD),
                            rs[:, 8 * m:8 * m + 8].unsqueeze(2).to_broadcast([P, 8, HD]), ALU.mult)
                    ins.then_inc(y_done, 1)
                dve.wait_ge(y_done, NT)
                dve.wait_ge(rot_done, TILES)


def swa_sample(nc, st, A, C, O, H, XT):
    NB, NK = DEC_BATCH, P + DEC_SEQ
    scr = nc.dram_tensor("scratch_ys", (NS, D), F32, kind="Internal").ap()
    T = H[:, NT, :]
    with ExitStack() as ctx:
        sb = lambda n, s, d=F32: ctx.enter_context(nc.sbuf_tensor(f"sws_{n}", s, d))
        sem = lambda n: st.sem(f"sws_{n}")
        Kb, Vb, Vn = sb("Kb", [P, NB, 256]), sb("Vb", [P, NB, 256]), sb("Vn", [DEC_SEQ, NB, 256])
        KT, kn = sb("KT", [P, NB, 2, NK]), sb("kn", [P, 2, NS])
        qz = sb("qz", [P, NB, 2, 2, 4, DEC_SEQ])
        band_f, band, identb = sb("bandf", [P, NK]), sb("band", [P, NK], BF16), sb("identb", [P, P], BF16)
        sink = sb("sink", [P, 1])
        mx, nm, es, sm, rs = (sb(n, [P, NB]) for n in ("mx", "nm", "es", "sm", "rs"))
        Pb, PT = sb("P", [P, NB, NK]), sb("PT", [P, NB, P])
        PTn = sb("PTn", [DEC_SEQ, NB, P])
        yq, Y = sb("yq", [P, NB, HD]), sb("Y", [NS, D])
        ps = ctx.enter_context(nc.psum_tensor("sws_ps", [P, 8, 512], F32))
        buf_in, cin, vn_in, ready, dch = sem("buffers_in"), sem("const_in"), sem("v_new_in"), sem("ready"), sem("dve_step")
        q_done, q_copied, k_done, k_copied = sem("qT"), sem("qT_copied"), sem("kT"), sem("kT_copied")
        s_done, m_done, e_done, pt_done, pt_copied = sem("scores"), sem("max"), sem("probs"), sem("pT"), sem("pT_copied")
        o_done, y_done, y_out, y_in, yt_done, yt_copied, stored = (sem("o"), sem("y"), sem("y_out"), sem("y_in"), sem("yT"),
                                                                   sem("yT_copied"), sem("stored"))

        def score(b, n=NK):
            return ps[:, b // 3, (b % 3) * NK:(b % 3) * NK + n]

        with nc.Block() as block:
            @block.sync
            def _(sp):
                sp.dma_start(Kb[:, :, :], A["state_swa_k"][0].rearrange("b w k d -> w b (k d)")).then_inc(buf_in, 16)
                sp.dma_start(Vb[:, :, :], A["state_swa_v"][0].rearrange("b w k d -> w b (k d)")).then_inc(buf_in, 16)
                sp.dma_start(band_f[:, :], C["bands"]).then_inc(cin, 16)
                sp.dma_start(sink[:, :], bass.AP(A["swa_sinks"].tensor, 0, [[1, 16], [0, DEC_SEQ], [1, 1]]),
                             allow_slow_non_contiguous=True).then_inc(cin, 16)
                for b in range(NB):
                    sp.dma_start(Vn[:, b, :], T[8 * b:8 * b + 8, SV:SV + 256]).then_inc(vn_in, 16)
                for o, src, c in ((O[12], A["state_swa_k"], SK), (O[13], A["state_swa_v"], SV)):
                    sp.dma_start(o[0, :, 0:P - DEC_SEQ].rearrange("b w k d -> b (w k d)"),
                                 src[0, :, DEC_SEQ:P].rearrange("b w k d -> b (w k d)")).then_inc(stored, 16)
                    for b in range(NB):
                        sp.dma_start(o[0, b, P - DEC_SEQ:P].rearrange("w k d -> w (k d)"), T[8 * b:8 * b + 8, c:c + 256]).then_inc(stored, 16)
                sp.wait_ge(y_done, 1)
                for b in range(NB):
                    sp.dma_start(bass.AP(scr.tensor, b * DEC_SEQ * D, [[HD, 16], [D, DEC_SEQ], [1, HD]]), yq[:, b, :]).then_inc(y_out, 16)
                sp.wait_ge(y_out, 16 * NB)
                sp.dma_start(Y[:, :], scr).then_inc(y_in, 16)
                sp.wait_ge(stored, 32 + 32 * NB)

            @block.tensor
            def _(pe):
                I64 = st.ident[0:NS, 0:NS]
                for j in range(8):
                    nc.tensor.transpose(ps[:, 3, j * NS:(j + 1) * NS], T[0:NS, SQ + j * P:SQ + (j + 1) * P], I64)
                for m in range(2):
                    last = nc.tensor.transpose(ps[:, 4, m * NS:(m + 1) * NS], T[0:NS, SK + m * P:SK + (m + 1) * P], I64)
                last.then_inc(q_done, 1)
                pe.wait_ge(buf_in, 32)
                for b in range(0, NB, 2):
                    g = b // 2
                    if g >= 2:
                        pe.wait_ge(k_copied, g - 1)
                    for j in range(4):
                        last = nc.tensor.transpose(ps[:, 6 + g % 2, j * P:(j + 1) * P],
                                                   Kb[:, b + j // 2, (j % 2) * P:(j % 2 + 1) * P], st.ident[:, :])
                    last.then_inc(k_done, 1)
                pe.wait_ge(k_copied, NB // 2 + 1)
                pe.wait_ge(q_copied, 3)
                pe.wait_ge(ready, 1)
                for b in range(NB):
                    nc.tensor.matmul(score(b), identb[:, :], band[:, :], start=True, stop=False, skip_group_check=True)
                    for m in range(2):
                        last = nc.tensor.matmul(score(b)[64 * m:64 * m + 64, :],
                                                qz[:, b, m, :, :, :].rearrange("d v g q -> d (v g q)"), KT[:, b, m, :],
                                                start=False, stop=True, skip_group_check=True)
                last.then_inc(s_done, 1)
                pe.wait_ge(e_done, 1)
                for b in range(NB):
                    nc.tensor.transpose(ps[:, 3 + b // 4, (b % 4) * P:(b % 4 + 1) * P], Pb[:, b, 0:P], st.ident[:, :])
                for b in range(NB):
                    last = nc.tensor.transpose(ps[0:DEC_SEQ, 6 + b // 4, (b % 4) * P:(b % 4 + 1) * P], Pb[:, b, P:NK], st.ident[:, :])
                last.then_inc(pt_done, 1)
                pe.wait_ge(pt_copied, 2)
                pe.wait_ge(vn_in, 16 * NB)
                for b in range(NB):
                    for m in range(2):
                        r = slice(64 * m, 64 * m + 64)
                        o = ps[r, b // 4, (b % 4) * P:(b % 4 + 1) * P]
                        nc.tensor.matmul(o, PT[:, b, r], Vb[:, b, m * P:(m + 1) * P], start=True, stop=False)
                        last = nc.tensor.matmul(o, PTn[:, b, r], Vn[:, b, m * P:(m + 1) * P], start=False, stop=True)
                last.then_inc(o_done, 1)
                pe.wait_ge(y_in, 16)
                for k in range(KD):
                    last = nc.tensor.transpose(ps[:, 5, k * NS:(k + 1) * NS], Y[:, k * P:(k + 1) * P], I64)
                last.then_inc(yt_done, 1)

            @block.scalar
            def _(act):
                act.wait_ge(q_done, 1)
                act.wait_ge(ready, 1)
                for v in range(2):
                    hf = slice(64 * v, 64 * v + 64)
                    for m in range(2):
                        ins = nc.scalar.copy(qz[hf, :, m, v, :, :].rearrange("d b g q -> d g b q"),
                                             ps[hf, 3, 4 * m * NS:4 * (m + 1) * NS].rearrange("d (g b q) -> d g b q", g=4, b=NB))
                    ins.then_inc(q_copied, 1)
                nc.scalar.copy(kn[:, :, :], ps[:, 4, 0:2 * NS].rearrange("p (m t) -> p m t", m=2)).then_inc(q_copied, 1)
                act.wait_ge(q_copied, 3)
                for m in range(2):
                    ins = nc.scalar.copy(KT[:, :, m, P:NK], kn[:, m, :].rearrange("p (b q) -> p b q", b=NB))
                for g in range(NB // 2):
                    act.wait_ge(k_done, g + 1)
                    ins = nc.scalar.copy(KT[:, 2 * g:2 * g + 2, :, 0:P],
                                         ps[:, 6 + g % 2, :].rearrange("p (b m t) -> p b m t", b=2, m=2))
                    ins.then_inc(k_copied, 1)
                act.wait_ge(k_copied, NB // 2)
                act.sem_inc(k_copied, 1)
                act.wait_ge(m_done, 1)
                nc.scalar.activation(es[:, :], es[:, :], ACT.Exp)
                for b in range(NB):
                    ins = nc.scalar.activation(Pb[:, b, :], score(b), ACT.Exp, bias=nm[:, b:b + 1], scale=AS,
                                               accum_out=sm[:, b:b + 1])
                ins.then_inc(e_done, 1)
                act.wait_ge(pt_done, 1)
                nc.scalar.copy(PTn[:, :, :], ps[0:DEC_SEQ, 6:8, :].rearrange("p c (b t) -> p (c b) t", b=4)).then_inc(pt_copied, 1)
                act.wait_ge(yt_done, 1)
                nc.scalar.copy(XT[:, :, SEQ:NTOK], ps[:, 5, :].rearrange("p (k t) -> p k t", k=KD)).then_inc(yt_copied, 1)
                act.wait_ge(yt_copied, 1)

            @block.vector
            def _(dve):
                link = chained(dve, dch)
                link(nc.vector.memset(qz[:, :, :, :, :, :], 0.0))
                link(nc.vector.tensor_copy(identb[:, :], st.ident[:, :]))
                dve.wait_ge(cin, 32)
                nc.vector.tensor_copy(band[:, :], band_f[:, :]).then_inc(ready, 1)
                dve.wait_ge(s_done, 1)
                for c in range(3):
                    n = 3 if c < 2 else 2
                    link(nc.vector.reduce_max(mx[:, 3 * c:3 * c + n],
                                              ps[:, c, 0:n * NK].rearrange("p (b n) -> p b n", n=NK), AX_X))
                link(nc.vector.tensor_scalar(mx[:, :], mx[:, :], AS, sink[:, 0:1], ALU.mult, ALU.max))
                link(nc.vector.tensor_scalar(nm[:, :], mx[:, :], -1.0, None, ALU.mult))
                nc.vector.tensor_scalar(es[:, :], nm[:, :], sink[:, 0:1], None, ALU.add).then_inc(m_done, 1)
                dve.wait_ge(pt_done, 1)
                nc.vector.tensor_copy(PT[:, :, :], ps[:, 3:5, :].rearrange("p c (b t) -> p (c b) t", b=4)).then_inc(pt_copied, 1)
                dve.wait_ge(e_done, 1)
                link(nc.vector.tensor_tensor(rs[:, :], sm[:, :], es[:, :], ALU.add))
                link(nc.vector.reciprocal(rs[:, :], rs[:, :]))
                dve.wait_ge(o_done, 1)
                for kv in range(4):
                    r, v = slice(32 * kv, 32 * kv + 32), kv % 2
                    ins = nc.vector.tensor_tensor(
                        yq[r, :, :], ps[r, 0:2, :].rearrange("p c (b d) -> p (c b) d", b=4)[:, :, v * HD:(v + 1) * HD],
                        rs[r, :].unsqueeze(2).to_broadcast([32, NB, HD]), ALU.mult)
                ins.then_inc(y_done, 1)


def block_end(nc, st, A, l, XT, xt_place, x_prompt, x_sample, y_out):
    last = l == 1
    h_side, a_side = ("left", "right") if l == 0 else ("right", "left")
    hs, at = ExitStack(), ExitStack()
    h_hi, h_lo = (hs.enter_context(nc.sbuf_tensor(f"h{l}_{n}", [P, KD, NTOK], F32R, side=h_side)) for n in ("hi", "lo"))
    out_projection(nc, st, A, A["w_out_even" if l == 0 else "w_out_odd"][0], l, XT, x_prompt, x_sample, h_hi, h_lo)
    xt_place.close()
    aT = at.enter_context(nc.sbuf_tensor(f"aT{l}", [P, KF, NTOK], F32, side=a_side))
    ffn_up(nc, st, A["ffn_w_gu"][l], f"ffn{l}u", h_hi, h_lo, aT)
    hs.close()
    place, XT = ExitStack(), None
    if not last:
        XT = place.enter_context(nc.sbuf_tensor("XT_odd", [P, KD, NTOK], F32))
    ffn_down(nc, st, A, l, f"ffn{l}d", aT, XT, y_out)
    at.close()
    st.end_phase()
    return XT, place


def rest(nc, st, A, C, O, XT, xt_place):
    def y_rows(i):
        if i < NT:
            return O[0][0, i * P:(i + 1) * P, :]
        return O[1].rearrange("b s d -> (b s) d")

    XT, place = block_end(nc, st, A, 0, XT, xt_place, A["x_prompt"][0], A["x_sample"].rearrange("b s d -> (b s) d"),
                          lambda i: st.x_dram[i * P:i * P + rows(i), :])
    yt_place = ExitStack()
    with ExitStack() as mix:
        H = mix.enter_context(nc.sbuf_tensor("H1", [P, TILES, SCOLS], F32, side="right"))
        in_projection(nc, st, None, A["w_in_odd"][0], ODD_CHUNKS, XT, lambda i: H[:, i, :], [], "ino")
        place.close()
        YT = yt_place.enter_context(nc.sbuf_tensor("YT_odd", [P, KD, NTOK], F32))
        swa_prompt(nc, st, A, C, O, H, YT)
        swa_sample(nc, st, A, C, O, H, YT)
        st.end_phase()
    block_end(nc, st, A, 1, YT, yt_place, st.x_dram[0:SEQ, :], st.x_dram[SEQ:NTOK, :], y_rows)
class State:

    def __init__(self, nc, ctx):
        self.nc, self.ctx = nc, ctx
        self.x_dram = nc.dram_tensor("scratch_x", (NTOK, D), F32, kind="Internal").ap()
        self.phase_sems = []

    def sem(self, name):
        s = self.nc.alloc_semaphore(name=name)
        self.phase_sems.append(s)
        return s

    def end_phase(self):
        self.nc.clear_and_free_semaphores(self.phase_sems)
        self.nc.all_engine_barrier()
        self.phase_sems = []

    def sbuf(self, name, shape, dt=F32):
        return self.ctx.enter_context(self.nc.sbuf_tensor(name, shape, dt))



def build(nc, A, C, O):
    with ExitStack() as ctx:
        st = State(nc, ctx)
        st.ident = st.sbuf("ident", [P, P])
        s_c = st.sem("const_in")
        with nc.Block() as block:
            @block.sync
            def _(sp):
                sp.dma_start(st.ident[:, :], C["ident"]).then_inc(s_c, 16)
                sp.wait_ge(s_c, 16)
        xt_place = ExitStack()

        def x_rows(i):
            if i < NT:
                return A["x_prompt"][0, i * P:(i + 1) * P, :]
            return A["x_sample"].rearrange("b s d -> (b s) d")

        with ExitStack() as mix:
            Hs = mix.enter_context(nc.sbuf_tensor("Hs", [P, C_END], F32))
            with ExitStack() as mixp:
                H = mixp.enter_context(nc.sbuf_tensor("H", [P, NT, C_END], F32))
                stores = []
                for out_p, out_s, a, b in ((O[2], O[8], C_DK, C_DV), (O[3], O[9], C_DV, C_IK), (O[4], O[10], C_IK, C_IK + HD)):
                    fl = "o b t k d -> (o b t) (k d)" if len(out_p.shape) == 5 else "o b t d -> (o b t) d"
                    stores.append((out_p.rearrange(fl).rearrange("(i p) c -> p i c", p=P), H[:, :, a:b]))
                    stores.append((out_s.rearrange(fl), Hs[0:NS, a:b]))
                in_projection(nc, st, x_rows, A["w_in_even"][0], EVEN_CHUNKS, None,
                              lambda i: H[:, i, :] if i < NT else Hs[:, :], stores, "ine")
                st.end_phase()
                XT = xt_place.enter_context(nc.sbuf_tensor("XT", [P, KD, NTOK], F32, side="right"))
                gla(nc, st, A, C, O, H, Hs)
                st.end_phase()
                dsa_prompt(nc, st, A, C, O, H, Hs, XT)
            st.end_phase()
            dsa_sample(nc, st, A, C, O, Hs, XT)
            st.end_phase()
        rest(nc, st, A, C, O, XT, xt_place)


_INS = ["x_prompt", "x_sample", "cache_k", "cache_v", "cache_idx", "state_gla", "state_swa_k", "state_swa_v",
        "page_table", "w_in_even", "gla_gate_w2", "gla_gate_b", "gla_norm_g", "w_out_even", "w_in_odd", "swa_sinks",
        "w_out_odd", "ffn_w_gu", "ffn_w_down", "ln_g", "ln_b"]
_OUTS = [(1, 1024, 1024), (8, 8, 1024), (1, 1, 1024, 2, 64), (1, 1, 1024, 2, 64), (1, 1, 1024, 64), (1, 1, 4, 64, 128),
         (1, 1, 128, 4, 64), (1, 1, 128, 4, 64), (1, 8, 8, 2, 64), (1, 8, 8, 2, 64), (1, 8, 8, 64), (1, 8, 4, 64, 128),
         (1, 8, 128, 4, 64), (1, 8, 128, 4, 64)]


def shape_constants():
    import numpy as np
    c = {"ident": np.eye(128, dtype=np.float32)}
    s, t = np.arange(128)[:, None], np.arange(128)[None, :]
    lev = [(s == t)]
    for n in range(7):
        L = 2 ** n
        lev.append((s // (2 * L) == t // (2 * L)) & (s // L % 2 == 0) & (t // L % 2 == 1))
    c["levels"] = np.stack(lev, 1).astype(np.float32)
    reset = np.ones((128, 192), np.float32)
    reset[:, 128:192:8] = 0.0
    c["reset"] = reset
    c["batchsel"] = (np.arange(64)[:, None] // 8 == np.arange(8)[None, :]).astype(np.float32)
    c["causal"] = np.where(t <= s, 0.0, -1e30).astype(np.float32)
    qi, ki = np.arange(64)[:, None], np.arange(8)[None, :]
    c["causal8"] = np.where(ki <= qi % 8, 0.0, -1e30).astype(np.float32)
    sp = np.zeros((64, 4, 128), np.float32)
    for pair in range(4):
        for r in range(128):
            sp[(2 * pair + r // 64) * 8 + r % 8, pair, r] = 1.0
    c["spread"] = sp
    gat = np.zeros((64, 8, 64), np.float32)
    for b in range(8):
        for r in range(64):
            gat[r, b, b * 8 + r % 8] = 1.0
    c["gather"] = gat
    a, k2 = np.arange(128)[:, None], np.arange(256)[None, :]
    c["band"] = np.where((k2 > a) & (k2 <= a + 128), 0.0, -1e30).astype(np.float32)
    q8, k136 = (np.arange(128) % 8)[:, None], np.arange(136)[None, :]
    c["bands"] = np.where((k136 > q8) & (k136 <= q8 + 128), 0.0, -1e30).astype(np.float32)
    pos = np.concatenate([np.arange(1024), 2048 + np.arange(64) % 8, np.zeros(64)]).astype(np.float32)
    inv = (np.float32(150000.0) ** (-np.arange(32, dtype=np.float32) / np.float32(32))).astype(np.float32)
    ang = pos[:, None] * inv[None, :]
    c["cos"] = np.cos(ang).astype(np.float32).reshape(9, 128, 32).transpose(1, 0, 2)
    c["sin"] = np.sin(ang).astype(np.float32).reshape(9, 128, 32).transpose(1, 0, 2)
    return c


def kernel(**inputs):
    import numpy as _np
    import concourse.bacc as _bacc
    from concourse import mybir as _mybir
    from concourse.bass_utils import run_bass_kernel_spmd as _run

    nc = _bacc.Bacc("TRN2", target_bir_lowering=False, num_devices=1)
    arrays, A, C, O = {}, {}, {}, []
    for name in _INS:
        a = _np.ascontiguousarray(inputs[name])
        arrays[f"in_{name}_dram"] = a
        A[name] = nc.dram_tensor(f"in_{name}_dram", a.shape, _mybir.dt.from_np(a.dtype), kind="ExternalInput").ap()
    for name, a in shape_constants().items():
        a = _np.ascontiguousarray(a)
        arrays[f"const_{name}"] = a
        C[name] = nc.dram_tensor(f"const_{name}", a.shape, _mybir.dt.from_np(a.dtype), kind="ExternalInput").ap()
    for i, shape in enumerate(_OUTS):
        O.append(nc.dram_tensor(f"out_{i}_dram", shape, F32, kind="ExternalOutput").ap())
    build(nc, A, C, O)
    r = _run(nc, [arrays], core_ids=[0])
    return tuple(r.results[0][f"out_{i}_dram"] for i in range(len(_OUTS)))
```
